# Optimizing a Trainium2 kernel written in Bass

```python
import jax, jax.numpy as jnp
from jax import lax
import numpy as np

D_MODEL = 1024
BATCH = 1
SEQ = 2048
DEPTH = 1

CHUNK = 64
N_META = 16
MIX_WIDTH = D_MODEL
ATTN_WIDTH = MIX_WIDTH // 2
POOL_WIDTH = MIX_WIDTH - ATTN_WIDTH
HEAD_DIM = 64
N_HEADS = ATTN_WIDTH // HEAD_DIM
POOL_WINDOWS = (2, 4, 8, 16)
N_POOL_GROUPS = len(POOL_WINDOWS)
POOL_GROUP_DIM = POOL_WIDTH // N_POOL_GROUPS
IN_WIDTH = 3 * ATTN_WIDTH + N_HEADS + POOL_WIDTH
D_FF = 128 * int(round(8 * D_MODEL / 3 / 128))
CONV_WIDTH = 3
Q_BLOCK = 128
EPS = 1e-6
NEG_BIG = -1e30

kernel_name = "hybrid_fox_pool_convffn_block"

def rmsnorm(x, g):
    xf = x.astype(jnp.float32)
    y = xf * lax.rsqrt(jnp.mean(xf * xf, axis=-1, keepdims=True) + EPS)
    return (y * g.astype(jnp.float32)).astype(x.dtype)

def forgetting_attention(q, k, v, f_logit):
    B, L = q.shape[0], q.shape[1]
    F = jnp.cumsum(jax.nn.log_sigmoid(f_logit.astype(jnp.float32)), axis=1)
    n_blocks = -(-L // Q_BLOCK)
    pad = n_blocks * Q_BLOCK - L
    padw = ((0, 0), (0, pad), (0, 0), (0, 0))
    qf = jnp.pad(q.astype(jnp.float32), padw) * (HEAD_DIM ** -0.5)
    kf = jnp.pad(k.astype(jnp.float32), padw)
    vf = jnp.pad(v.astype(jnp.float32), padw)
    Fh = jnp.pad(F, ((0, 0), (0, pad), (0, 0))).transpose(0, 2, 1)
    outs = []
    for i in range(n_blocks):
        q0, q1 = i * Q_BLOCK, (i + 1) * Q_BLOCK
        s = jnp.einsum('bqhd,bkhd->bhqk', qf[:, q0:q1], kf[:, :q1])
        decay = Fh[:, :, q0:q1, None] - Fh[:, :, None, :q1]
        causal = jnp.arange(q0, q1)[:, None] >= jnp.arange(q1)[None, :]
        p = jax.nn.softmax(jnp.where(causal, s + decay, NEG_BIG), axis=-1)
        outs.append(jnp.einsum('bhqk,bkhd->bqhd', p, vf[:, :q1]))
    o = jnp.concatenate(outs, axis=1)[:, :L]
    return o.astype(v.dtype)

def multiscale_pool(u, w_pool, pool_scale):
    B, L, _ = u.shape
    uf = u.astype(jnp.float32)
    t = jnp.arange(L)
    diffs = []
    for g, w in enumerate(POOL_WINDOWS):
        ug = uf[..., g * POOL_GROUP_DIM:(g + 1) * POOL_GROUP_DIM]
        c = jnp.cumsum(ug, axis=1)
        c_prev = jnp.pad(c, ((0, 0), (w, 0), (0, 0)))[:, :L]
        cnt = jnp.minimum(t + 1, w).astype(jnp.float32)[None, :, None]
        diffs.append((c - c_prev) / cnt - ug)
    d = jnp.stack(diffs, axis=2)
    y = jnp.einsum('blgc,gcd->blgd', d, w_pool.astype(jnp.float32)).reshape(B, L, POOL_WIDTH)
    return (y * pool_scale.astype(jnp.float32)).astype(u.dtype)

def causal_dwconv(h, w, b):
    L = h.shape[1]
    hp = jnp.pad(h, ((0, 0), (CONV_WIDTH - 1, 0), (0, 0)))
    y = b
    for j in range(CONV_WIDTH):
        y = y + w[j] * hp[:, j:j + L]
    return y

def setup_inputs(seed: int = 0) -> dict:
    key = jax.random.key(seed)
    ks = jax.random.split(key, 16)
    f32 = jnp.float32
    n = lambda k, shape, s: (jax.random.normal(k, shape, f32) * s)
    return {
        "x": n(ks[0], (BATCH, SEQ, D_MODEL), 1.0),
        "meta_tokens": n(ks[1], (N_META, D_MODEL), 1.0),
        "norm1_g": 1.0 + n(ks[2], (DEPTH, D_MODEL), 0.02),
        "w_in": n(ks[3], (DEPTH, D_MODEL, IN_WIDTH), D_MODEL ** -0.5),
        "b_f": 3.0 + n(ks[4], (DEPTH, N_HEADS), 0.5),
        "w_pool": n(ks[5], (DEPTH, N_POOL_GROUPS, POOL_GROUP_DIM, POOL_GROUP_DIM), POOL_GROUP_DIM ** -0.5),
        "pool_scale": 1.0 + n(ks[6], (DEPTH, POOL_WIDTH), 0.1),
        "w_out": n(ks[7], (DEPTH, MIX_WIDTH, D_MODEL), MIX_WIDTH ** -0.5),
        "norm2_g": 1.0 + n(ks[8], (DEPTH, D_MODEL), 0.02),
        "w_up": n(ks[9], (DEPTH, D_MODEL, 2 * D_FF), D_MODEL ** -0.5),
        "conv_w": n(ks[10], (DEPTH, CONV_WIDTH, 2 * D_FF), CONV_WIDTH ** -0.5),
        "conv_b": n(ks[11], (DEPTH, 2 * D_FF), 0.01),
        "w_down": n(ks[12], (DEPTH, D_FF, D_MODEL), D_FF ** -0.5),
        "normf_g": 1.0 + n(ks[13], (D_MODEL,), 0.02),
    }

def reference(x, meta_tokens, norm1_g, w_in, b_f, w_pool, pool_scale, w_out,
              norm2_g, w_up, conv_w, conv_b, w_down, normf_g):
    B = x.shape[0]
    meta = jnp.broadcast_to(meta_tokens.astype(x.dtype)[None], (B, N_META, D_MODEL))
    h = jnp.concatenate([meta, x], axis=1)
    L = h.shape[1]
    o_k = ATTN_WIDTH
    o_v = 2 * ATTN_WIDTH
    o_f = 3 * ATTN_WIDTH
    o_p = o_f + N_HEADS
    for l in range(DEPTH):
        z = rmsnorm(h, norm1_g[l]) @ w_in[l]
        q = z[..., :o_k].reshape(B, L, N_HEADS, HEAD_DIM)
        k = z[..., o_k:o_v].reshape(B, L, N_HEADS, HEAD_DIM)
        v = z[..., o_v:o_f].reshape(B, L, N_HEADS, HEAD_DIM)
        f_logit = z[..., o_f:o_p] + b_f[l]
        u = z[..., o_p:]
        a = forgetting_attention(q, k, v, f_logit).reshape(B, L, ATTN_WIDTH)
        p = multiscale_pool(u, w_pool[l], pool_scale[l])
        h = h + jnp.concatenate([a, p], axis=-1) @ w_out[l]
        up = causal_dwconv(rmsnorm(h, norm2_g[l]) @ w_up[l], conv_w[l], conv_b[l])
        gate, val = up[..., :D_FF], up[..., D_FF:]
        h = h + (jax.nn.silu(gate) * val) @ w_down[l]
    y = rmsnorm(h, normf_g)
    return y[:, N_META:]


_drawn_inputs = setup_inputs


def setup_inputs(seed=0):
    import zlib

    import numpy as np

    out = dict(_drawn_inputs(seed))
    spreads = {}
    factors = {'meta_tokens': 2.872, 'norm1_g': 4.256, 'norm2_g': 4.548, 'conv_b': 8.0, 'normf_g': 2.741}
    for name, (base, spread) in spreads.items():
        noise = np.random.default_rng([zlib.crc32(name.encode()), seed]).standard_normal(out[name].shape)
        drawn = base * np.exp(spread * noise) if base else spread * noise
        out[name] = __import__('jax').numpy.asarray(drawn.astype(out[name].dtype))
    for name, factor in factors.items():
        out[name] = (out[name] * factor).astype(out[name].dtype)
    return out
```

```python
from contextlib import ExitStack

import concourse.bass as bass
from concourse import mybir

ALU = mybir.AluOpType
ACT = mybir.ActivationFunctionType
AX_X = mybir.AxisListType.X
F32 = mybir.dt.float32
F32R = mybir.dt.float32r
BF16 = mybir.dt.bfloat16

P = 128
D = 1024
KT = D // P
SEQ = 2048
META = 16
L = META + SEQ
TILES = SEQ // P
HEADS = 8
HD = 64
AW = HEADS * HD
GROUPS = 4
WINDOWS = (2, 4, 8, 16)
FF = 2688
FT = FF // P
EPS = 1e-6
NEG = -1e30
BLK = 416
BLKS = [(b * BLK, min(BLK, L - b * BLK)) for b in range(-(-L // BLK))]
NB = len(BLKS)
PASSES = (("hi", "hi"), ("hi", "lo"), ("lo", "hi"))


def frames(t):
    if isinstance(t, int) and t == 0:
        return 0, META
    return (t - 1) * P + META, P


def cols(t):
    f0, n = frames(t)
    return bass.ds(f0, n)


def row(ap, i):
    return ap[bass.ds(i, 1), :, :].rearrange("o p c -> (o p) c")


class Pair:

    def __init__(self, hi, lo):
        self.hi, self.lo = hi, lo

    def part(self, name):
        return self.hi if name == "hi" else self.lo


def tools(nc, ctx, tag):
    def sb(name, shape, dt=F32):
        return ctx.enter_context(nc.sbuf_tensor(f"{tag}_{name}", shape, dt))

    def ps(name, shape, dt=F32):
        return ctx.enter_context(nc.psum_tensor(f"{tag}_{name}", shape, dt))

    def sem(name):
        return ctx.enter_context(nc.semaphore(f"{tag}_{name}"))

    def pair(name, shape):
        return Pair(sb(name + "_hi", shape, F32R), sb(name + "_lo", shape, F32R))

    return sb, ps, sem, pair


def in_projection(nc, x, meta, g1, w_item, w_v, w_f, b_f, z_hi, z_lo, v_aug, g_rows):
    ITEMS = 2 + 6
    VH = AW // 2
    VA = 2 * HD + 2
    with ExitStack() as ctx:
        sb, ps, sem, pair = tools(nc, ctx, "in")
        ident = sb("ident", [P, P])
        x_both = sb("x_both", [P, L])
        x_in = [x_both[:, s * D:(s + 1) * D] for s in range(2)]
        xs_g = sb("xs_g", [P, L])
        xs, g_row = xs_g[:, 0:D], xs_g[:, D:2 * D]
        xT = pair("xT", [P, KT, L])
        w_raw = sb("w_raw", [P, 2048])
        w = [pair(f"w{s}", [P, 2048]) for s in range(2)]
        wf_raw = w_raw[:, 0:KT * P]
        stage = [sb(f"stage{s}", [P, L]) for s in range(2)]
        bf_col = sb("bf_col", [HEADS, 1])
        stat = sb("stat", [P, 2, 4])

        turn = ps("turn", [P, 2, 512])
        acc = [ps(f"acc{b}", [P, 512]) for b in range(NB)]
        junk = sb("junk", [P, D], BF16)

        ident_ready = sem("ident_ready")
        x_landed = [sem(f"x_landed{s}") for s in range(2)]
        g_landed = sem("g_landed")
        bf_landed = sem("bf_landed")
        square_done = sem("square_done")
        mean_done = sem("mean_done")
        root_done = sem("root_done")
        rstd_done = sem("rstd_done")
        xs_done = sem("xs_done")
        turn_done = sem("turn_done")
        xhi_done = sem("xhi_done")
        xlo_done = sem("xlo_done")
        w_landed = sem("w_landed")
        whi_done = sem("whi_done")
        wlo_done = sem("wlo_done")
        v_done = sem("v_done")
        vhi_done = sem("vhi_done")
        vlo_done = sem("vlo_done")
        ones_done = sem("ones_done")
        v_stored = [sem(f"v_stored{s}") for s in range(2)]
        f_done = sem("f_done")
        f_chain = sem("f_chain")
        f_act = sem("f_act")
        f_ready = sem("f_ready")
        f_stored = sem("f_stored")
        z_done = sem("z_done")
        zhi_done = sem("zhi_done")
        zlo_done = sem("zlo_done")
        z_stored = [sem(f"z_stored{b}") for b in range(NB)]
        block = ctx.enter_context(nc.Block())

        def v_stage(t):
            return stage[t % 2][:, 0:4 * VA].rearrange("p (h c) -> p h c", c=VA)

        @block.sync
        def _(sp):
            def load_x(t, slot, peeled):
                if not peeled:
                    sp.wait_ge(xs_done, t - 1)
                src = meta if isinstance(t, int) and t == 0 else x[bass.ds((t - 1) * P, P), :]
                sp.dma_start(x_in[slot][0:src.shape[0], :], src).then_inc(x_landed[slot], 16)

            load_x(0, 0, True)
            sp.dma_start(w_raw[:, :], w_v[0, :, :]).then_inc(w_landed, 16)
            sp.dma_start(g_row[:, :], g1).then_inc(g_landed, 16)
            load_x(1, 1, True)
            load_x(2, 0, False)
            sp.dma_start(bf_col[:, :], b_f).then_inc(bf_landed, 16)
            sp.wait_ge(wlo_done, 1)
            sp.wait_ge(whi_done, 1)
            sp.dma_start(w_raw[:, 0:KT * P], w_f).then_inc(w_landed, 16)

            def store_v(t, slot, half, n):
                _, rows = frames(t)
                sp.wait_ge(vhi_done, n + 1)
                sp.wait_ge(vlo_done, n + 1)
                dst = v_aug[4 * half:4 * half + 4, bass.ds(t, 1), 0:rows, :].rearrange("h o p c -> (o p) h c")
                sp.dma_start(dst, v_stage(slot)[0:rows, :, :]).then_inc(v_stored[slot], 16)

            load_x(3, 1, False)
            store_v(0, 0, 0, 0)
            with sp.Fori(0, TILES // 2 - 2) as i:
                for s in range(2):
                    load_x(2 * i + 4 + s, s, False)
                    store_v(2 * i + 1 + s, (1 + s) % 2, 0, 2 * i + 1 + s)
            load_x(TILES, 0, False)
            for t in range(TILES - 3, TILES + 1):
                store_v(t, t % 2, 0, t)
            sp.wait_ge(wlo_done, 2)
            sp.wait_ge(whi_done, 2)
            sp.dma_start(w_raw[:, :], w_v[1, :, :]).then_inc(w_landed, 16)
            sp.wait_ge(wlo_done, 3)
            sp.wait_ge(whi_done, 3)
            sp.dma_start(w_raw[:, :], w_item[0, :, :]).then_inc(w_landed, 16)
            sp.wait_ge(f_ready, 1)
            sp.dma_start(g_rows[0, :, :], xs_g[0:HEADS, :]).then_inc(f_stored, 16)
            sp.wait_ge(f_ready, 2)
            sp.dma_start(g_rows[1, :, :], x_both[0:HEADS, :]).then_inc(f_stored, 16)
            store_v(0, 1, 1, TILES + 1)
            with sp.Fori(0, TILES // 2) as i:
                for s in range(2):
                    store_v(2 * i + 1 + s, s, 1, 2 * i + 2 + s + TILES)

            def store_z(ct, b):
                c0, n = BLKS[b]
                sp.wait_ge(zlo_done, NB * ct + b + 1)
                for part, dst in ((0, z_hi), (1, z_lo)):
                    sp.dma_start(row(dst, ct)[:, c0:c0 + n],
                                 stage[part][:, c0:c0 + n]).then_inc(z_stored[b], 16)

            def pair_stores(k, more):
                for half in range(2):
                    for b in range(NB):
                        store_z(2 * k + half, b)
                    if half == 0 and more:
                        sp.wait_ge(wlo_done, k + 5)
                        sp.wait_ge(whi_done, k + 5)
                        sp.dma_start(w_raw[:, :], row(w_item, k + 2)).then_inc(w_landed, 16)

            sp.wait_ge(wlo_done, 4)
            sp.wait_ge(whi_done, 4)
            sp.dma_start(w_raw[:, :], w_item[1, :, :]).then_inc(w_landed, 16)
            with sp.Fori(0, 4) as k:
                pair_stores(k, True)
            for k in (4, 5):
                pair_stores(k, False)
            sp.wait_ge(f_stored, 32)
            for s in range(2):
                sp.wait_ge(v_stored[s], 16 * (TILES + 1))
            for b in range(NB):
                sp.wait_ge(z_stored[b], 2 * 16 * 12)

        @block.gpsimd
        def _(pool):
            nc.gpsimd.memset(ident[:, :], 0.0).then_inc(ident_ready, 1)
            pool.wait_ge(ident_ready, 1)
            nc.gpsimd.affine_select(out=ident[:, :], in_=ident[:, :], compare_op=ALU.not_equal, fill=1.0,
                                    base=0, pattern=[[-1, P]], channel_multiplier=1).then_inc(ident_ready, 1)
            for s in range(2):
                for c, value in ((HD, 1.0), (HD + 1, 0.0)):
                    nc.gpsimd.memset(v_stage(s)[:, :, c:c + 1], value).then_inc(ones_done, 1)

            def split_lo(item, slot, n):
                pool.wait_ge(whi_done, item + 1)
                nc.gpsimd.tensor_tensor(w[slot].lo[:, 0:n], w_raw[:, 0:n], w[slot].hi[:, 0:n].bitcast(F32),
                                        ALU.subtract).then_inc(wlo_done, 1)

            split_lo(0, 0, 2048)
            split_lo(1, 1, KT * P)
            split_lo(2, 0, 2048)
            split_lo(3, 1, 2048)
            split_lo(4, 0, 2048)
            with pool.Fori(0, 2) as i:
                for s in range(2):
                    split_lo(2 * i + 5 + s, (1 + s) % 2, 2048)

        def split_hi(act, item, slot, n):
            act.wait_ge(w_landed, 16 * (item + 1))
            if not isinstance(item, int) or item > 4:
                act.wait_ge(z_done, 2 * NB * (item - 4))
            elif item in (2, 4):
                act.wait_ge(v_done, (TILES + 1) * (item // 2))
            elif item == 3:
                act.wait_ge(f_done, NB)
            nc.scalar.activation(w[slot].hi[:, 0:n], w_raw[:, 0:n], ACT.Copy).then_inc(whi_done, 1)

        @block.scalar
        def _(act):
            def squares(t, slot):
                _, n = frames(t)
                act.wait_ge(x_landed[slot], 8 * t + (16 - 8 * slot))
                nc.scalar.activation(junk[0:n, :], x_in[slot][0:n, :], ACT.Square,
                                     accum_out=stat[0:n, slot, 0:1]).then_inc(square_done, 1)
                act.wait_ge(mean_done, t + 1)
                nc.scalar.activation(stat[0:n, slot, 2:3], stat[0:n, slot, 1:2], ACT.Sqrt).then_inc(root_done, 1)

            def turned(t):
                _, n = frames(t)
                for h in range(2):
                    act.wait_ge(turn_done, 2 * t + h + 1)
                    nc.scalar.activation(xT.hi[:, 4 * h:4 * h + 4, cols(t)],
                                         turn[:, h, :].rearrange("p (k c) -> p k c", k=4)[:, :, 0:n],
                                         ACT.Copy).then_inc(xhi_done, 1)

            def v_hi(t, slot, n, peeled):
                _, rows = frames(t)
                act.wait_ge(v_done, n + 1)
                if not peeled:
                    act.wait_ge(v_stored[slot], 8 * n - 8 * slot)
                nc.scalar.activation(v_stage(slot)[0:rows, :, 0:HD].bitcast(F32R),
                                     acc[slot][0:rows, 0:VH].rearrange("p (h c) -> p h c", c=HD),
                                     ACT.Copy).then_inc(vhi_done, 1)

            split_hi(act, 0, 0, 2048)
            for t in range(5):
                squares(t, t % 2)
                turned(t)
                if t == 1:
                    split_hi(act, 1, 1, KT * P)
                    act.wait_ge(ones_done, 4)
                if t >= 2:
                    v_hi(t - 2, t % 2, t - 2, t < 4)
            with act.Fori(0, TILES // 2 - 2) as i:
                for s in range(2):
                    t = 2 * i + 5 + s
                    squares(t, (3 + s) % 2)
                    turned(t)
                    v_hi(t - 2, (1 + s) % 2, t - 2, False)
            for t in (TILES - 1, TILES):
                v_hi(t, t % 2, t, False)
            split_hi(act, 2, 0, 2048)

            y, e = x_both[0:HEADS, :], xs_g[0:HEADS, :]
            act.wait_ge(bf_landed, 16)
            act.wait_ge(turn_done, 2 * (TILES + 1))
            for b, (c0, n) in enumerate(BLKS):
                act.wait_ge(f_done, b + 1)
                nc.scalar.activation(y[:, c0:c0 + n], acc[b][0:HEADS, 0:n], ACT.Identity,
                                     bias=bf_col[:, 0:1]).then_inc(f_act, 1)
            act.wait_ge(f_act, NB)
            nc.scalar.activation(e, y, ACT.Abs).then_inc(f_act, 1)
            act.wait_ge(f_act, NB + 1)
            nc.scalar.activation(e, e, ACT.Exp, scale=-1.0).then_inc(f_act, 1)
            act.wait_ge(f_act, NB + 2)
            nc.scalar.activation(e, e, ACT.Ln, bias=1.0).then_inc(f_act, 1)

            def v_second(t, slot, n):
                v_hi(t, slot, n, False)

            split_hi(act, 3, 1, 2048)
            v_second(0, 1, TILES + 1)
            with act.Fori(0, TILES // 2) as i:
                for s in range(2):
                    v_second(2 * i + 1 + s, s, 2 * i + 2 + s + TILES)

            def z_hi_block(ct, b, peeled):
                c0, n = BLKS[b]
                act.wait_ge(z_done, NB * ct + b + 1)
                if peeled:
                    if b == 0:
                        for s in range(2):
                            act.wait_ge(v_stored[s], 16 * (TILES + 1))
                else:
                    act.wait_ge(z_stored[b], 32 * ct)
                nc.scalar.activation(stage[0][:, c0:c0 + n].bitcast(F32R), acc[b][:, 0:n],
                                     ACT.Copy).then_inc(zhi_done, 1)

            def pair_hi(k, slot, first, more):
                for half in range(2):
                    for b in range(NB):
                        z_hi_block(2 * k + half, b, first and half == 0)
                    if half == 0 and more:
                        split_hi(act, k + 4, slot, 2048)

            pair_hi(0, 0, True, True)
            with act.Fori(0, 2) as i:
                for s in range(2):
                    pair_hi(2 * i + 1 + s, (1 + s) % 2, False, True)
            pair_hi(5, 1, False, False)

        @block.vector
        def _(dve):
            def means(t, slot):
                _, n = frames(t)
                dve.wait_ge(square_done, t + 1)
                nc.vector.tensor_scalar(stat[0:n, slot, 1:2], stat[0:n, slot, 0:1], 1.0 / D, EPS,
                                        ALU.mult, ALU.add).then_inc(mean_done, 1)
                dve.wait_ge(root_done, t + 1)
                nc.vector.reciprocal(stat[0:n, slot, 3:4], stat[0:n, slot, 2:3]).then_inc(rstd_done, 1)
                dve.wait_ge(rstd_done, t + 1)
                if isinstance(t, int) and t == 0:
                    dve.wait_ge(g_landed, 16)
                else:
                    dve.wait_ge(turn_done, 2 * t)
                nc.vector.scalar_tensor_tensor(xs[0:n, :], x_in[slot][0:n, :], stat[0:n, slot, 3:4],
                                               g_row[0:n, :], ALU.mult, ALU.mult).then_inc(xs_done, 1)

            def lows(t):
                _, n = frames(t)
                for h in range(2):
                    dve.wait_ge(xhi_done, 2 * t + h + 1)
                    part = (slice(None), slice(4 * h, 4 * h + 4), cols(t))
                    nc.vector.tensor_tensor(xT.lo[part], turn[:, h, :].rearrange("p (k c) -> p k c", k=4)[:, :, 0:n],
                                            xT.hi[part].bitcast(F32), ALU.subtract).then_inc(xlo_done, 1)

            def v_lo(t, slot, n):
                _, rows = frames(t)
                dve.wait_ge(vhi_done, n + 1)
                st = v_stage(slot)
                nc.vector.tensor_tensor(st[0:rows, :, HD + 2:VA].bitcast(F32R),
                                        acc[slot][0:rows, 0:VH].rearrange("p (h c) -> p h c", c=HD),
                                        st[0:rows, :, 0:HD], ALU.subtract).then_inc(vlo_done, 1)

            for t in (0, 1, 2):
                means(t, t % 2)
                lows(t)
            v_lo(0, 0, 0)
            with dve.Fori(0, TILES // 2 - 1) as i:
                for s in range(2):
                    t = 2 * i + 3 + s
                    means(t, (3 + s) % 2)
                    lows(t)
                    v_lo(t - 2, (1 + s) % 2, t - 2)
            for t in (TILES - 1, TILES):
                v_lo(t, t % 2, t)

            y, e = x_both[0:HEADS, :], xs_g[0:HEADS, :]
            dve.wait_ge(f_act, NB + 3)
            nc.vector.tensor_scalar(y, y, 0.0, None, ALU.min).then_inc(f_chain, 1)
            dve.wait_ge(f_chain, 1)
            nc.vector.tensor_tensor(e, e, y, ALU.subtract).then_inc(f_chain, 1)
            dve.wait_ge(f_chain, 2)
            nc.vector.tensor_tensor_scan(y, e, e, 0.0, ALU.add, ALU.max).then_inc(f_chain, 1)
            dve.wait_ge(f_chain, 3)
            nc.vector.tensor_scalar(y, y, float(HD) ** 0.5, None, ALU.mult).then_inc(f_chain, 1)
            dve.wait_ge(f_chain, 4)
            nc.vector.tensor_copy(e.bitcast(F32R), y).then_inc(f_ready, 1)
            dve.wait_ge(f_ready, 1)
            nc.vector.tensor_tensor(y.bitcast(F32R), y, e, ALU.subtract).then_inc(f_ready, 1)

            v_lo(0, 1, TILES + 1)
            with dve.Fori(0, TILES // 2) as i:
                for s in range(2):
                    v_lo(2 * i + 1 + s, s, 2 * i + 2 + s + TILES)

            with dve.Fori(0, 12) as ct:
                for b, (c0, n) in enumerate(BLKS):
                    dve.wait_ge(zhi_done, NB * ct + b + 1)
                    nc.vector.tensor_tensor(stage[1][:, c0:c0 + n].bitcast(F32R), acc[b][:, 0:n],
                                            stage[0][:, c0:c0 + n], ALU.subtract).then_inc(zlo_done, 1)

        @block.tensor
        def _(pe):
            def turns(t):
                _, n = frames(t)
                pe.wait_ge(xs_done, t + 1)
                for h in range(2):
                    if not (isinstance(t, int) and t == 0):
                        pe.wait_ge(xlo_done, 2 * t + h - 1)
                    for k in range(4):
                        mm = nc.tensor.transpose(turn[:, h, k * P:k * P + n],
                                                 xs[0:n, (4 * h + k) * P:(4 * h + k + 1) * P], ident[0:n, 0:n])
                    mm.then_inc(turn_done, 1)

            def v_tile(t, slot, wslot, n, peeled):
                f0 = frames(t)[0]
                if not peeled:
                    pe.wait_ge(vlo_done, n - 1)
                for j, (a, b) in enumerate(PASSES):
                    for k in range(KT):
                        mm = nc.tensor.matmul(acc[slot][:, 0:VH], xT.part(a)[:, k, f0:f0 + P],
                                              w[wslot].part(b)[:, k * VH:(k + 1) * VH],
                                              start=(j == 0 and k == 0), stop=(j == 2 and k == KT - 1))
                mm.then_inc(v_done, 1)

            pe.wait_ge(ident_ready, 2)
            turns(0)
            turns(1)
            for t in range(2, TILES + 2):
                if t <= TILES:
                    turns(t)
                if t == 2:
                    pe.wait_ge(wlo_done, 1)
                pe.wait_ge(xlo_done, 2 * t)
                if t == 2:
                    v_tile(0, 0, 0, 0, True)
                v_tile(t - 1, (t - 1) % 2, 0, t - 1, t == 2)

            def channel_tile(wslot, offset, done, free):
                for b, (c0, n) in enumerate(BLKS):
                    free(b)
                    for k in range(KT):
                        for j, (a, c) in enumerate(PASSES):
                            mm = nc.tensor.matmul(acc[b][:, 0:n],
                                                  w[wslot].part(a)[:, offset + k * P:offset + (k + 1) * P],
                                                  xT.part(c)[:, k, c0:c0 + n],
                                                  start=(k == 0 and j == 0), stop=(k == KT - 1 and j == 2))
                    mm.then_inc(done, 1)

            pe.wait_ge(wlo_done, 2)

            def f_free(b):
                if b < 2:
                    pe.wait_ge(vlo_done, TILES + 1)
            channel_tile(1, 0, f_done, f_free)
            pe.wait_ge(f_act, NB)
            pe.wait_ge(wlo_done, 3)
            for t in range(TILES + 1):
                n = TILES + 1 + t
                v_tile(t, n % 2, 0, n, t < 2)

            def z_free(ct, peeled):
                def free(b):
                    if not peeled:
                        pe.wait_ge(zlo_done, NB * (ct - 1) + b + 1)
                    elif b < 2:
                        pe.wait_ge(vlo_done, 2 * (TILES + 1))
                return free

            def pair_mm(k, slot, peeled):
                pe.wait_ge(wlo_done, k + 4)
                for half in range(2):
                    channel_tile(slot, half * D, z_done, z_free(2 * k + half, peeled and half == 0))

            pair_mm(0, 1, True)
            with pe.Fori(0, 2) as i:
                for s in range(2):
                    pair_mm(2 * i + 1 + s, s, False)
            pair_mm(5, 0, False)


AB = 3
A_BLOCKS = [(b, min(b + AB, TILES + 1)) for b in range(0, TILES + 1, AB)]
A_STEPS = [(j, kt) for j, (_, last) in enumerate(A_BLOCKS) for kt in range(last)]
A_ENDS = [max(s for s, (b, _) in enumerate(A_STEPS) if b == j) for j in range(len(A_BLOCKS))]
M_CHUNKS = [(i, 0 if c == 0 else META + (4 * c - 1) * P, META + P * min(i, 4 * c + 3), c, c == i // 4)
            for i in range(TILES + 1) for c in range(i // 4 + 1)]
MC = 5
M_FIRST = 10
LAG = 2
AUG = HD + 4
VA = 2 * HD + 2


def attention(nc, z_hi, z_lo, v_aug, g_rows, c_rows, a_out, d_out):
    NS, NM = len(A_STEPS), len(M_CHUNKS)
    with ExitStack() as ctx:
        sb, ps, sem, pair = tools(nc, ctx, "at")
        K1 = [sb(f"K1{s}", [P, L], F32R) for s in range(2)]
        Q1 = [sb(f"Q1{s}", [P, L], F32R) for s in range(2)]
        K2 = [sb(f"K2{s}", [AUG, L], F32R) for s in range(2)]
        Q2 = [sb(f"Q2{s}", [AUG, L], F32R) for s in range(2)]
        QM = [sb(f"QM{s}", [AUG, L], F32R) for s in range(2)]
        V = [sb(f"V{s}", [P, TILES + 1, VA], F32R) for s in range(2)]
        ident = sb("ident", [P, P])
        mask = sb("mask", [P, P])
        ident_r = sb("ident_r", [P, P], F32R)
        mask_r = sb("mask_r", [P, P], F32R)
        prob = [sb(f"prob{s}", [P, AB * P]) for s in range(2)]
        prob_r = [pair(f"prob_r{s}", [P, AB * P]) for s in range(3)]
        peak = sb("peak", [P, TILES + 1, MC])
        top = sb("top", [P, TILES + 1])
        shift = sb("shift", [P, 2, P // 2])
        shift_T = sb("shift_T", [P, P])
        lsum = [sb(f"lsum{s}", [P, AB]) for s in range(2)]
        o_sb = [sb(f"o_sb{s}", [P, AB, HD]) for s in range(2)]
        PAD = 16
        U = sb("U", [P, PAD + L])
        W = [sb(f"W{s}", [P, PAD + L]) for s in range(2)]

        score = [ps(f"score{s}", [P, 512]) for s in range(3)]
        mlog = [ps(f"mlog{s}", [P, 512]) for s in range(2)]
        o_ps = [ps(f"o_ps{s}", [P, 512]) for s in range(2)]
        turn = ps("turn", [P, 512])

        consts = sem("consts")
        consts_r = sem("consts_r")
        cleared = sem("cleared")
        rows_set = sem("rows_set")
        first_landed = [sem(f"first_landed{s}") for s in range(2)]
        rest_landed = [sem(f"rest_landed{s}") for s in range(2)]
        mlog_done = sem("mlog_done")
        peak_done = sem("peak_done")
        top_done = sem("top_done")
        shift_done = sem("shift_done")
        turn_done = sem("turn_done")
        shift_T_done = sem("shift_T_done")
        c_stored = sem("c_stored")
        c_landed = [sem(f"c_landed{s}") for s in range(2)]
        score_done = sem("score_done")
        exp_done = sem("exp_done")
        phi_done = sem("phi_done")
        plo_done = sem("plo_done")
        pv_done = sem("pv_done")
        o_copied = sem("o_copied")
        lsum_done = sem("lsum_done")
        o_added = sem("o_added")
        o_done = sem("o_done")
        o_stored = [sem(f"o_stored{s}") for s in range(2)]
        pool_step = sem("pool_step")
        u_landed = sem("u_landed")
        d_stored = sem("d_stored")
        block = ctx.enter_context(nc.Block())
        NJ = len(A_BLOCKS)

        def before(h, s, ring, total):
            if s >= ring:
                return total * h + s - ring + 1
            last = max(x for x in range(total) if x % ring == s % ring)
            return total * (h - 1) + last + 1

        def heads(eng, body):
            body(0, 0, True, False)
            with eng.Fori(0, HEADS // 2 - 1) as i:
                for s in range(2):
                    body(2 * i + 1 + s, (1 + s) % 2, False, False)
            body(HEADS - 1, (HEADS - 1) % 2, False, True)

        def used_rows(kt):
            return META if kt == 0 else P

        def step_shape(s):
            j, kt = A_STEPS[s]
            a, b = A_BLOCKS[j]
            q0 = frames(max(a, kt))[0]
            q1 = sum(frames(b - 1))
            return q0, q1 - q0, kt >= a

        @block.sync
        def _(sp):
            def load(dst, src, done):
                sp.dma_start(dst.bitcast(F32), src).then_inc(done, 16)

            def load_head(h, s, fresh):
                if not fresh:
                    sp.wait_ge(pv_done, NS * (h - 1))
                qh, kh, ql, kl = (row(z, h)[r:r + HD, :] for z in (z_hi, z_lo) for r in (0, HD))
                load(K2[s][0:HD, :], kh, first_landed[s])
                load(QM[s][0:HD, :], qh, first_landed[s])
                for i in range(2):
                    load(K2[s][HD + 2 + i:HD + 3 + i, :], g_rows[i, bass.ds(h, 1), :], first_landed[s])
                load(K1[s][0:HD, :], kh, rest_landed[s])
                load(K1[s][HD:P, :], kl, rest_landed[s])
                for i in range(2):
                    load(Q1[s][i * HD:(i + 1) * HD, :], qh, rest_landed[s])
                load(Q2[s][0:HD, :], ql, rest_landed[s])
                v = v_aug[bass.ds(h, 1), :, :, :].rearrange("o t p c -> p (o t) c")
                load(V[s][0:META, 0:1, :], v[0:META, 0:1, :], rest_landed[s])
                load(V[s][:, 1:, :], v[:, 1:, :], rest_landed[s])

            def spread_shift(h, s):
                sp.wait_ge(shift_T_done, h + 1)
                sp.dma_start(c_rows, shift_T[:, :]).then_inc(c_stored, 16)
                sp.wait_ge(c_stored, 16 * (h + 1))
                for i in range(2):
                    t0 = i * P // 2
                    load(Q2[s][HD + i:HD + i + 1, 0:META], c_rows[t0:t0 + 1, 0:META], c_landed[s])
                    load(Q2[s][HD + i:HD + i + 1, META:], c_rows[t0 + 1:t0 + TILES + 1, :]
                         .rearrange("(o t) c -> o (t c)", o=1), c_landed[s])

            def store_o(h, j):
                a, b = A_BLOCKS[j]
                sp.wait_ge(o_done, NJ * h + j + 1)
                for i, t in enumerate(range(a, b)):
                    f0, n = frames(t)
                    sp.dma_start(a_out[f0:f0 + n, bass.ds(h * HD, HD)], o_sb[j % 2][0:n, i, :]) \
                        .then_inc(o_stored[j % 2], 16)

            def head(h, s, first, last):
                if not last:
                    load_head(h + 1, 1 - s, first)
                for j in range(NJ):
                    if j == NJ - 1 and not last:
                        spread_shift(h + 1, 1 - s)
                    store_o(h, j)

            sp.wait_ge(rows_set, 8)
            load_head(0, 0, True)
            spread_shift(0, 0)
            heads(sp, head)
            n_stored = [HEADS * sum(b - a for j, (a, b) in enumerate(A_BLOCKS) if j % 2 == s) for s in range(2)]
            for s in range(2):
                sp.wait_ge(o_stored[s], 16 * n_stored[s])

        @block.gpsimd
        def _(pool):
            for n, (t, value) in enumerate(((ident, 0.0), (mask, 0.0))):
                nc.gpsimd.memset(t[:, :], value).then_inc(consts, 1)
            pool.wait_ge(consts, 2)
            nc.gpsimd.affine_select(out=ident[:, :], in_=ident[:, :], compare_op=ALU.not_equal, fill=1.0,
                                    base=0, pattern=[[-1, P]], channel_multiplier=1).then_inc(consts, 1)
            nc.gpsimd.affine_select(out=mask[:, :], in_=mask[:, :], compare_op=ALU.is_ge, fill=NEG,
                                    base=0, pattern=[[-1, P]], channel_multiplier=1).then_inc(consts, 1)
            pool.wait_ge(consts, 4)
            done = 0

            def then(instruction):
                nonlocal done
                done += 1
                instruction.then_inc(pool_step, 1)
                pool.wait_ge(pool_step, done)

            for t in (U, W[0], W[1]):
                then(nc.gpsimd.memset(t[:, 0:PAD], 0.0))
            for g, window in enumerate(WINDOWS):
                if g:
                    pool.wait_ge(d_stored, 16 * g)
                pool.dma_start(U[:, PAD:], z_hi[HEADS + g, :, :]).then_inc(u_landed, 16)
                pool.dma_start(W[0][:, PAD:], z_lo[HEADS + g, :, :]).then_inc(u_landed, 16)
                pool.wait_ge(u_landed, 32 * (g + 1))
                then(nc.gpsimd.tensor_tensor(U[:, PAD:], U[:, PAD:], W[0][:, PAD:], ALU.add))
                cur, width, k = U, 1, 0
                while width < window:
                    nxt = W[k % 2]
                    then(nc.gpsimd.tensor_tensor(nxt[:, PAD:], cur[:, PAD:], cur[:, PAD - width:PAD - width + L],
                                                 ALU.add))
                    cur, width, k = nxt, 2 * width, k + 1
                out = W[k % 2]
                then(nc.gpsimd.tensor_scalar(out[:, PAD:], cur[:, PAD:], 1.0 / window, None, ALU.mult))
                for t in range(window - 1):
                    then(nc.gpsimd.tensor_scalar(out[:, PAD + t:PAD + t + 1], cur[:, PAD + t:PAD + t + 1],
                                                 1.0 / (t + 1), None, ALU.mult))
                then(nc.gpsimd.tensor_tensor(out[:, PAD:], out[:, PAD:], U[:, PAD:], ALU.subtract))
                pool.dma_start(d_out[g, :, :], out[:, PAD:]).then_inc(d_stored, 16)
            pool.wait_ge(d_stored, 16 * GROUPS)

        @block.tensor
        def _(pe):
            def maxima(h, s, m):
                i, k0, k1, _, diagonal = M_CHUNKS[m]
                q0, n = frames(i)[0], k1 - k0
                if m == 0:
                    pe.wait_ge(first_landed[s], 64 * ((h - s) // 2 + 1) if isinstance(h, int) else 32 * (h - s) + 64)
                if not (isinstance(h, int) and h == 0 and m < 2):
                    pe.wait_ge(peak_done, before(h, m, 2, NM))
                mm = nc.tensor.matmul(mlog[m % 2][:, 0:n], QM[s][:, q0:q0 + P], K2[s][:, k0:k1],
                                      start=True, stop=True)
                if diagonal:
                    d = frames(i)[1]
                    mm = nc.tensor.matmul(mlog[m % 2][:, n - d:n], ident_r[:, :], mask_r[:, 0:d],
                                          start=False, stop=True, skip_group_check=True)
                mm.then_inc(mlog_done, 1)

            def turn_shift(h):
                pe.wait_ge(shift_done, 2 * (h + 1))
                nc.tensor.transpose(turn[:, 0:P], shift[:, :, :].rearrange("p a t -> p (a t)"),
                                    ident[:, :]).then_inc(turn_done, 1)

            def scores(h, s, n):
                j, kt = A_STEPS[n]
                q0, nq, diagonal = step_shape(n)
                k0 = frames(kt)[0]
                bank = score[n % 3]
                if not (isinstance(h, int) and h == 0 and n < 3):
                    pe.wait_ge(exp_done, before(h, n, 3, NS))
                nc.tensor.matmul(bank[:, 0:nq], K1[s][:, k0:k0 + P], Q1[s][:, q0:q0 + nq], start=True, stop=False)
                mm = nc.tensor.matmul(bank[:, 0:nq], K2[s][:, k0:k0 + P], Q2[s][:, q0:q0 + nq],
                                      start=False, stop=True)
                if diagonal:
                    d = frames(kt)[1]
                    mm = nc.tensor.matmul(bank[:, 0:d], mask_r[:, :], ident_r[:, 0:d], start=False, stop=True,
                                          skip_group_check=True)
                mm.then_inc(score_done, 1)

            def values(h, s, n):
                j, kt = A_STEPS[n]
                a, b = A_BLOCKS[j]
                q0, nq, _ = step_shape(n)
                r = used_rows(kt)
                if kt == 0 and not (isinstance(h, int) and h == 0 and j < 2):
                    pe.wait_ge(o_added, NJ * h + j - 1)
                pe.wait_ge(plo_done, NS * h + n + 1)
                first = kt == 0
                for t in reversed(range(max(a, kt), b)):
                    off = frames(t)[0] - q0
                    for part, width in ((prob_r[n % 3].hi, VA), (prob_r[n % 3].lo, HD + 2)):
                        mm = nc.tensor.matmul(o_ps[j % 2][:, (t - a) * VA:(t - a) * VA + width],
                                              part[0:r, off:off + P], V[s][0:r, kt, 0:width],
                                              start=first, stop=True, skip_group_check=True)
                        first = False
                mm.then_inc(pv_done, 1)

            def head(h, s, first, last):
                half = (h - s) // 2 if isinstance(h, int) else None
                pe.wait_ge(rest_landed[s], 112 * (half + 1) if half is not None else 56 * (h - s) + 112)
                pe.wait_ge(c_landed[s], 64 * (half + 1) if half is not None else 32 * (h - s) + 64)
                for n in range(NS + LAG):
                    if not last and 0 <= n - M_FIRST < NM:
                        maxima(h + 1, 1 - s, n - M_FIRST)
                    if not last and n == M_FIRST + NM + 2:
                        turn_shift(h + 1)
                    if n < NS:
                        scores(h, s, n)
                    if n >= LAG:
                        values(h, s, n - LAG)

            pe.wait_ge(consts_r, 2)
            for m in range(NM):
                maxima(0, 0, m)
            turn_shift(0)
            heads(pe, head)

        @block.scalar
        def _(act):
            def turned(h):
                act.wait_ge(turn_done, h + 1)
                if not (isinstance(h, int) and h == 0):
                    act.wait_ge(c_stored, 16 * h)
                nc.scalar.activation(shift_T[:, :], turn[:, 0:P], ACT.Copy).then_inc(shift_T_done, 1)

            def exps(h, n):
                _, kt = A_STEPS[n]
                _, nq, _ = step_shape(n)
                r = used_rows(kt)
                act.wait_ge(score_done, NS * h + n + 1)
                if not (isinstance(h, int) and h == 0 and n < 2):
                    act.wait_ge(plo_done, before(h, n, 2, NS))
                nc.scalar.activation(prob[n % 2][0:r, 0:nq], score[n % 3][0:r, 0:nq], ACT.Exp,
                                     scale=float(HD) ** -0.5).then_inc(exp_done, 1)
                act.wait_ge(exp_done, NS * h + n + 1)
                if not (isinstance(h, int) and h == 0 and n < 3):
                    act.wait_ge(pv_done, before(h, n, 3, NS))
                nc.scalar.activation(prob_r[n % 3].hi[0:r, 0:nq], prob[n % 2][0:r, 0:nq], ACT.Copy) \
                    .then_inc(phi_done, 1)

            def copy_o(h, j):
                a, b = A_BLOCKS[j]
                act.wait_ge(pv_done, NS * h + A_ENDS[j] + 1)
                if not (isinstance(h, int) and h == 0 and j < 2):
                    per_head = 16 * sum(y - x for i, (x, y) in enumerate(A_BLOCKS) if i % 2 == j % 2)
                    in_head = 16 * sum(y - x for i, (x, y) in enumerate(A_BLOCKS) if i % 2 == j % 2 and i < j)
                    act.wait_ge(o_stored[j % 2], per_head * h + in_head)
                o = o_ps[j % 2][:, 0:(b - a) * VA].rearrange("p (t c) -> p t c", c=VA)
                nc.scalar.activation(o_sb[j % 2][:, 0:b - a, :], o[:, :, HD + 2:VA], ACT.Copy).then_inc(o_copied, 1)

            def head(h, s, first, last):
                for n in range(NS):
                    exps(h, n)
                    for j in range(NJ - 1):
                        if n == A_ENDS[j] + LAG + 1:
                            copy_o(h, j)
                    if not last and n == M_FIRST + NM + 4:
                        turned(h + 1)
                copy_o(h, NJ - 1)

            act.wait_ge(consts, 4)
            for src, dst in ((ident, ident_r), (mask, mask_r)):
                nc.scalar.activation(dst[:, :], src[:, :], ACT.Copy).then_inc(consts_r, 1)
            turned(0)
            heads(act, head)

        @block.vector
        def _(dve):
            def peaks(h, m):
                i, k0, k1, c, _ = M_CHUNKS[m]
                r = frames(i)[1]
                dve.wait_ge(mlog_done, NM * h + m + 1)
                if m == 0 and not (isinstance(h, int) and h == 0):
                    dve.wait_ge(top_done, h)
                nc.vector.tensor_reduce(peak[0:r, i, c:c + 1], mlog[m % 2][0:r, 0:k1 - k0], AX_X,
                                        ALU.max).then_inc(peak_done, 1)

            def shifts(h):
                dve.wait_ge(peak_done, NM * (h + 1))
                nc.vector.tensor_reduce(top[:, :], peak[:, :, :], AX_X, ALU.max).then_inc(top_done, 1)
                dve.wait_ge(top_done, h + 1)
                if not (isinstance(h, int) and h == 0):
                    dve.wait_ge(turn_done, h)
                nc.vector.tensor_scalar(shift[:, 0, 0:TILES + 1].bitcast(F32R), top[:, :], -1.0, None, ALU.mult) \
                    .then_inc(shift_done, 1)
                dve.wait_ge(shift_done, 2 * h + 1)
                nc.vector.scalar_tensor_tensor(shift[:, 1, 0:TILES + 1].bitcast(F32R), top[:, :], -1.0, shift[:, 0, 0:TILES + 1],
                                               ALU.mult, ALU.subtract).then_inc(shift_done, 1)

            def lows(h, n):
                _, kt = A_STEPS[n]
                _, nq, _ = step_shape(n)
                r = used_rows(kt)
                dve.wait_ge(phi_done, NS * h + n + 1)
                nc.vector.tensor_tensor(prob_r[n % 3].lo[0:r, 0:nq], prob[n % 2][0:r, 0:nq],
                                        prob_r[n % 3].hi[0:r, 0:nq].bitcast(F32), ALU.subtract) \
                    .then_inc(plo_done, 1)

            def normalise(h, j):
                a, b = A_BLOCKS[j]
                k, n = j % 2, b - a
                o = o_ps[k][:, 0:n * VA].rearrange("p (t c) -> p t c", c=VA)
                dve.wait_ge(o_copied, NJ * h + j + 1)
                parts = [(META, 0, 1), (P, 1, n)] if a == 0 else [(P, 0, n)]
                for r, t0, t1 in parts:
                    inv = nc.vector.reciprocal(lsum[k][0:r, t0:t1],
                                               o[0:r, t0:t1, HD:HD + 1].rearrange("p t c -> p (t c)"))
                inv.then_inc(lsum_done, 1)
                nc.vector.tensor_tensor(o_sb[k][:, 0:n, :], o[:, :, 0:HD], o_sb[k][:, 0:n, :], ALU.add) \
                    .then_inc(o_added, 1)
                dve.wait_ge(o_added, NJ * h + j + 1)
                dve.wait_ge(lsum_done, NJ * h + j + 1)
                for r, t0, t1 in parts:
                    scale = lsum[k][0:r, t0:t1].rearrange("p (t c) -> p t c", c=1).to_broadcast([r, t1 - t0, HD])
                    o_n = o_sb[k][0:r, t0:t1, :]
                    last = nc.vector.tensor_tensor(o_n, o_n, scale, ALU.mult)
                last.then_inc(o_done, 1)

            def head(h, s, first, last):
                for n in range(NS):
                    if not last and 0 <= n - M_FIRST < NM:
                        peaks(h + 1, n - M_FIRST)
                    if not last and n == M_FIRST + NM:
                        shifts(h + 1)
                    lows(h, n)
                    for j in range(NJ - 1):
                        if n == A_ENDS[j] + LAG + 1:
                            normalise(h, j)
                normalise(h, NJ - 1)

            for s in range(2):
                for t in (K2[s], Q2[s]):
                    nc.vector.memset(t[HD:AUG, :].bitcast(F32), 1.0).then_inc(rows_set, 1)
                nc.vector.memset(QM[s][HD:AUG, :].bitcast(F32), 1.0).then_inc(rows_set, 1)
                dve.wait_ge(rows_set, 4 * s + 3)
                nc.vector.memset(QM[s][HD:HD + 2, :].bitcast(F32), 0.0).then_inc(rows_set, 1)
            nc.vector.memset(peak[:, :, :], NEG).then_inc(cleared, 1)
            nc.vector.memset(shift[:, :, :], 0.0).then_inc(cleared, 1)
            dve.wait_ge(cleared, 2)
            for m in range(NM):
                peaks(0, m)
            shifts(0)
            heads(dve, head)


def out_projection(nc, x, meta, g2, w_out, w_pool, p_scale, a_in, d_in, p_hi, p_lo, h2_out, n_hi, n_lo):
    with ExitStack() as ctx:
        sb, ps, sem, pair = tools(nc, ctx, "out")
        ident = sb("ident", [P, P])
        g_row = sb("g_row", [P, D])
        wp_raw = sb("wp_raw", [P, GROUPS * P])
        wp = pair("wp", [P, GROUPS * P])
        scale = sb("scale", [P, GROUPS])
        d_raw = [sb(f"d_raw{s}", [P, BLK]) for s in range(2)]
        dd = [pair(f"dd{s}", [P, BLK]) for s in range(2)]
        p_st = [[sb(f"p_st{s}{i}", [P, BLK]) for i in range(2)] for s in range(2)]
        w_raw = [sb(f"w_raw{s}", [P, D]) for s in range(2)]
        w = pair("w", [P, KT, D])
        h_in = [sb(f"h_in{s}", [P, D]) for s in range(2)]
        a_nat = [sb(f"a_nat{s}", [P, AW]) for s in range(2)]
        cat = [pair(f"cat{s}", [P, KT, P]) for s in range(2)]
        h2 = [sb(f"h2{s}", [P, D]) for s in range(2)]
        xs = sb("xs", [P, D])
        junk = sb("junk", [P, D], BF16)
        nT = [pair(f"nT{s}", [P, KT, P]) for s in range(2)]
        stat = sb("stat", [P, 2, 4])

        acc = ps("acc", [P, 2, 2, 512])
        turn = ps("turn", [P, 2, 512])
        a_turn = [ps(f"a_turn{s}", [P, 512]) for s in range(2)]

        consts, cleared = sem("consts"), sem("cleared")
        small_landed = sem("small_landed")
        wp_hi_done, wp_lo_done = sem("wp_hi_done"), sem("wp_lo_done")
        d_landed = [sem(f"d_landed{s}") for s in range(2)]
        d_hi_done, d_lo_done = sem("d_hi_done"), sem("d_lo_done")
        map_done, p_hi_done, p_lo_done = sem("map_done"), sem("p_hi_done"), sem("p_lo_done")
        p_stored = [sem(f"p_stored{s}") for s in range(2)]
        w_landed = [sem(f"w_landed{s}") for s in range(2)]
        w_hi_done, w_lo_done = sem("w_hi_done"), sem("w_lo_done")
        h_landed = [sem(f"h_landed{s}") for s in range(2)]
        a_landed = [sem(f"a_landed{s}") for s in range(2)]
        cat_landed = [sem(f"cat_landed{s}") for s in range(2)]
        a_turned, a_hi_done, a_lo_done = sem("a_turned"), sem("a_hi_done"), sem("a_lo_done")
        out_done, h2_done = sem("out_done"), sem("h2_done")
        square_done, mean_done, root_done = sem("square_done"), sem("mean_done"), sem("root_done")
        rstd_done, xs_done = sem("rstd_done"), sem("xs_done")
        turn_done, n_hi_done, n_lo_done = sem("turn_done"), sem("n_hi_done"), sem("n_lo_done")
        h2_stored = [sem(f"h2_stored{s}") for s in range(2)]
        n_stored = [sem(f"n_stored{s}") for s in range(2)]
        block = ctx.enter_context(nc.Block())
        UNITS = [(g, b) for g in range(GROUPS) for b in range(NB)]
        NU = len(UNITS)

        def early(t, n=2):
            return isinstance(t, int) and t < n

        @block.sync
        def _(sp):
            sp.dma_start(wp_raw[:, :], w_pool).then_inc(small_landed, 16)
            sp.dma_start(scale[:, :], p_scale).then_inc(small_landed, 16)
            sp.dma_start(g_row[:, :], g2).then_inc(small_landed, 16)

            def load_d(n):
                g, b = UNITS[n]
                c0, m = BLKS[b]
                if n >= 2:
                    sp.wait_ge(d_lo_done, n - 1)
                sp.dma_start(d_raw[n % 2][:, 0:m], d_in[g, :, c0:c0 + m]).then_inc(d_landed[n % 2], 16)

            def load_w(k):
                if k >= 2:
                    sp.wait_ge(w_lo_done, k - 1)
                sp.dma_start(w_raw[k % 2][:, :], w_out[k, :, :]).then_inc(w_landed[k % 2], 16)

            load_d(0)
            load_d(1)
            for n in range(NU):
                g, b = UNITS[n]
                c0, m = BLKS[b]
                if n + 2 < NU:
                    load_d(n + 2)
                if n < KT:
                    load_w(n)
                sp.wait_ge(p_lo_done, n + 1)
                for i, dst in enumerate((p_hi, p_lo)):
                    sp.dma_start(dst[g, :, c0:c0 + m], p_st[n % 2][i][:, 0:m]).then_inc(p_stored[n % 2], 16)
            for s in range(2):
                sp.wait_ge(p_stored[s], 32 * (NU // 2))

            def load(t, s):
                f0, n = frames(t)
                if not early(t):
                    sp.wait_ge(a_hi_done, 1)
                    sp.wait_ge(h2_done, 2 * t - 2)
                src = meta if isinstance(t, int) and t == 0 else x[bass.ds((t - 1) * P, P), :]
                sp.dma_start(h_in[s][0:n, :], src).then_inc(h_landed[s], 16)
                sp.dma_start(a_nat[s][0:n, :], a_in[bass.ds(f0, n), :]).then_inc(a_landed[s], 16)
                for part, src in ((cat[s].hi, p_hi), (cat[s].lo, p_lo)):
                    sp.dma_start(part[:, GROUPS:KT, 0:n].bitcast(F32),
                                 src[:, :, bass.ds(f0, n)].rearrange("g p c -> p g c")).then_inc(cat_landed[s], 16)

            def store_h2(t, s):
                f0, n = frames(t)
                sp.wait_ge(out_done, 2)
                sp.wait_ge(h2_done, 2 * t + 2)
                sp.dma_start(h2_out[bass.ds(f0, n), :], h2[s][0:n, :]).then_inc(h2_stored[s], 16)

            def store_n(t, s):
                f0, n = frames(t)
                sp.wait_ge(n_hi_done, 2)
                sp.wait_ge(n_lo_done, 2 * t + 2)
                for part, dst in ((nT[s].hi, n_hi), (nT[s].lo, n_lo)):
                    sp.dma_start(dst[:, :, bass.ds(f0, n)], part[:, :, 0:n].bitcast(F32)).then_inc(n_stored[s], 16)

            load(0, 0)
            load(1, 1)
            load(2, 0)
            store_h2(0, 0)
            def two(i):
                for s in range(2):
                    load(2 * i + 3 + s, (1 + s) % 2)
                    store_h2(2 * i + 1 + s, (1 + s) % 2)
                    store_n(2 * i + s, s)

            two(0)
            with sp.Fori(1, TILES // 2 - 1) as i:
                two(i)
            for t in (TILES - 1, TILES):
                store_h2(t, t % 2)
            for t in range(TILES - 2, TILES + 1):
                store_n(t, t % 2)
            for s in range(2):
                sp.wait_ge(h2_stored[s], 16 * ((TILES + 2 - s) // 2))
                sp.wait_ge(n_stored[s], 32 * ((TILES + 2 - s) // 2))

        @block.gpsimd
        def _(pool):
            nc.gpsimd.memset(ident[:, :], 0.0).then_inc(consts, 1)
            pool.wait_ge(consts, 1)
            nc.gpsimd.affine_select(out=ident[:, :], in_=ident[:, :], compare_op=ALU.not_equal, fill=1.0,
                                    base=0, pattern=[[-1, P]], channel_multiplier=1).then_inc(consts, 1)
            pool.wait_ge(consts, 2)
            for k in range(KT):
                pool.wait_ge(w_hi_done, k + 1)
                nc.gpsimd.tensor_tensor(w.lo[:, k, :], w_raw[k % 2][:, :], w.hi[:, k, :].bitcast(F32),
                                        ALU.subtract).then_inc(w_lo_done, 1)

        @block.scalar
        def _(act):
            act.wait_ge(small_landed, 48)
            nc.scalar.activation(wp.hi[:, :], wp_raw[:, :], ACT.Copy).then_inc(wp_hi_done, 1)

            def d_hi(n):
                _, b = UNITS[n]
                m = BLKS[b][1]
                act.wait_ge(d_landed[n % 2], 16 * (n // 2 + 1))
                if n >= 2:
                    act.wait_ge(map_done, n - 1)
                nc.scalar.activation(dd[n % 2].hi[:, 0:m], d_raw[n % 2][:, 0:m], ACT.Copy).then_inc(d_hi_done, 1)

            d_hi(0)
            d_hi(1)
            for n, (g, b) in enumerate(UNITS):
                m = BLKS[b][1]
                act.wait_ge(map_done, n + 1)
                if n >= 2:
                    act.wait_ge(p_stored[n % 2], 32 * (n // 2))
                nc.scalar.activation(p_st[n % 2][0][:, 0:m].bitcast(F32R), a_turn[n % 2][:, 0:m], ACT.Copy,
                                     scale=scale[:, g:g + 1]).then_inc(p_hi_done, 1)
                if n + 2 < NU:
                    d_hi(n + 2)
                if n < KT:
                    act.wait_ge(w_landed[n % 2], 16 * (n // 2 + 1))
                    nc.scalar.activation(w.hi[:, n, :], w_raw[n % 2][:, :], ACT.Copy).then_inc(w_hi_done, 1)

            def a_his(t, s):
                _, n = frames(t)
                act.wait_ge(a_turned, t + 1)
                if not early(t):
                    act.wait_ge(out_done, 2 * t - 2)
                nc.scalar.activation(cat[s].hi[:, 0:GROUPS, 0:n],
                                     a_turn[s][:, :].rearrange("p (k c) -> p k c", k=4)[:, :, 0:n],
                                     ACT.Copy).then_inc(a_hi_done, 1)

            def norms(t, s):
                _, n = frames(t)
                act.wait_ge(h2_done, 2 * t + 2)
                nc.scalar.activation(junk[0:n, :], h2[s][0:n, :], ACT.Square,
                                     accum_out=stat[0:n, s, 0:1]).then_inc(square_done, 1)
                act.wait_ge(mean_done, t + 1)
                nc.scalar.activation(stat[0:n, s, 2:3], stat[0:n, s, 1:2], ACT.Sqrt).then_inc(root_done, 1)
                for h in range(2):
                    act.wait_ge(turn_done, 2 * t + h + 1)
                    if not early(t) and h == 0:
                        act.wait_ge(n_stored[s], 16 * (t - s))
                    nc.scalar.activation(nT[s].hi[:, 4 * h:4 * h + 4, 0:n],
                                         turn[:, h, :].rearrange("p (k c) -> p k c", k=4)[:, :, 0:n],
                                         ACT.Copy).then_inc(n_hi_done, 1)

            a_his(0, 0)
            a_his(1, 1)
            norms(0, 0)
            def two(i):
                for s in range(2):
                    a_his(2 * i + 2 + s, s)
                    norms(2 * i + 1 + s, (1 + s) % 2)

            two(0)
            with act.Fori(1, TILES // 2 - 1) as i:
                two(i)
            a_his(TILES, 0)
            norms(TILES - 1, 1)
            norms(TILES, 0)

        @block.vector
        def _(dve):
            dve.wait_ge(wp_hi_done, 1)
            nc.vector.tensor_tensor(wp.lo[:, :], wp_raw[:, :], wp.hi[:, :].bitcast(F32), ALU.subtract) \
                .then_inc(wp_lo_done, 1)

            def d_low(n):
                m = BLKS[UNITS[n][1]][1]
                dve.wait_ge(d_hi_done, n + 1)
                nc.vector.tensor_tensor(dd[n % 2].lo[:, 0:m], d_raw[n % 2][:, 0:m],
                                        dd[n % 2].hi[:, 0:m].bitcast(F32), ALU.subtract).then_inc(d_lo_done, 1)

            d_low(0)
            d_low(1)
            for n, (g, b) in enumerate(UNITS):
                m = BLKS[b][1]
                dve.wait_ge(p_hi_done, n + 1)
                nc.vector.scalar_tensor_tensor(p_st[n % 2][1][:, 0:m].bitcast(F32R), a_turn[n % 2][:, 0:m],
                                               scale[:, g:g + 1], p_st[n % 2][0][:, 0:m], ALU.mult,
                                               ALU.subtract).then_inc(p_lo_done, 1)
                if n + 2 < NU:
                    d_low(n + 2)

            def a_lows(t, s):
                _, n = frames(t)
                dve.wait_ge(a_hi_done, t + 1)
                nc.vector.tensor_tensor(cat[s].lo[:, 0:GROUPS, 0:n],
                                        a_turn[s][:, :].rearrange("p (k c) -> p k c", k=4)[:, :, 0:n],
                                        cat[s].hi[:, 0:GROUPS, 0:n].bitcast(F32), ALU.subtract) \
                    .then_inc(a_lo_done, 1)

            def residual(t, s):
                _, n = frames(t)
                dve.wait_ge(h_landed[s], 8 * t + (16 - 8 * s))
                if not early(t):
                    dve.wait_ge(h2_stored[s], 8 * (t - s))
                for h in range(2):
                    dve.wait_ge(out_done, 2 * t + h + 1)
                    nc.vector.tensor_tensor(h2[s][0:n, h * 512:(h + 1) * 512], acc[0:n, s, h, :],
                                            h_in[s][0:n, h * 512:(h + 1) * 512], ALU.add).then_inc(h2_done, 1)

            def norms(t, s):
                _, n = frames(t)
                dve.wait_ge(square_done, t + 1)
                nc.vector.tensor_scalar(stat[0:n, s, 1:2], stat[0:n, s, 0:1], 1.0 / D, EPS,
                                        ALU.mult, ALU.add).then_inc(mean_done, 1)
                dve.wait_ge(root_done, t + 1)
                nc.vector.reciprocal(stat[0:n, s, 3:4], stat[0:n, s, 2:3]).then_inc(rstd_done, 1)
                dve.wait_ge(rstd_done, t + 1)
                if not early(t, 1):
                    dve.wait_ge(turn_done, 2 * t)
                nc.vector.scalar_tensor_tensor(xs[0:n, :], h2[s][0:n, :], stat[0:n, s, 3:4], g_row[0:n, :],
                                               ALU.mult, ALU.mult).then_inc(xs_done, 1)

            def n_lows(t, s):
                _, n = frames(t)
                for h in range(2):
                    dve.wait_ge(n_hi_done, 2 * t + h + 1)
                    part = (slice(None), slice(4 * h, 4 * h + 4), slice(0, n))
                    nc.vector.tensor_tensor(nT[s].lo[part], turn[:, h, :].rearrange("p (k c) -> p k c", k=4)[:, :, 0:n],
                                            nT[s].hi[part].bitcast(F32), ALU.subtract).then_inc(n_lo_done, 1)

            def rest(t, s):
                residual(t, s)
                norms(t, s)
                n_lows(t, s)

            nc.vector.memset(cat[0].hi[:, :, META:].bitcast(F32), 0.0).then_inc(cleared, 1)
            nc.vector.memset(cat[0].lo[:, :, META:].bitcast(F32), 0.0).then_inc(cleared, 1)
            dve.wait_ge(small_landed, 48)
            a_lows(0, 0)
            a_lows(1, 1)
            rest(0, 0)
            def two(i):
                for s in range(2):
                    a_lows(2 * i + 2 + s, s)
                    rest(2 * i + 1 + s, (1 + s) % 2)

            two(0)
            with dve.Fori(1, TILES // 2 - 1) as i:
                two(i)
            a_lows(TILES, 0)
            rest(TILES - 1, 1)
            rest(TILES, 0)

        @block.tensor
        def _(pe):
            pe.wait_ge(wp_lo_done, 1)
            for n, (g, b) in enumerate(UNITS):
                m = BLKS[b][1]
                pe.wait_ge(d_lo_done, n + 1)
                if n >= 2:
                    pe.wait_ge(p_lo_done, n - 1)
                for j, (u, v) in enumerate(PASSES):
                    mm = nc.tensor.matmul(a_turn[n % 2][:, 0:m], wp.part(u)[:, g * P:(g + 1) * P],
                                          dd[n % 2].part(v)[:, 0:m], start=j == 0, stop=j == 2)
                mm.then_inc(map_done, 1)

            def a_turns(t, s):
                _, n = frames(t)
                pe.wait_ge(a_landed[s], 8 * t + (16 - 8 * s))
                if early(t):
                    pe.wait_ge(p_lo_done, NU)
                else:
                    pe.wait_ge(a_lo_done, t - 1)
                for k in range(4):
                    mm = nc.tensor.transpose(a_turn[s][:, k * P:k * P + n], a_nat[s][0:n, k * P:(k + 1) * P],
                                             ident[0:n, 0:n])
                mm.then_inc(a_turned, 1)

            def products(t, s):
                pe.wait_ge(cat_landed[s], 16 * t + (32 - 16 * s))
                pe.wait_ge(a_lo_done, t + 1)
                if not early(t):
                    pe.wait_ge(h2_done, 2 * t - 2)
                for h in range(2):
                    for k in range(KT):
                        for j, (u, v) in enumerate(PASSES):
                            mm = nc.tensor.matmul(acc[:, s, h, :], cat[s].part(u)[:, k, :],
                                                  w.part(v)[:, k, h * 512:(h + 1) * 512],
                                                  start=k == 0 and j == 0, stop=k == KT - 1 and j == 2)
                    mm.then_inc(out_done, 1)

            def turns(t, s):
                _, n = frames(t)
                pe.wait_ge(xs_done, t + 1)
                for h in range(2):
                    if not early(t, 1):
                        pe.wait_ge(n_lo_done, 2 * t + h - 1)
                    for k in range(4):
                        mm = nc.tensor.transpose(turn[:, h, k * P:k * P + n],
                                                 xs[0:n, (4 * h + k) * P:(4 * h + k + 1) * P], ident[0:n, 0:n])
                    mm.then_inc(turn_done, 1)

            pe.wait_ge(consts, 2)
            a_turns(0, 0)
            a_turns(1, 1)
            pe.wait_ge(w_lo_done, KT)
            pe.wait_ge(cleared, 2)
            products(0, 0)
            def two(i):
                for s in range(2):
                    a_turns(2 * i + 2 + s, s)
                    products(2 * i + 1 + s, (1 + s) % 2)
                    turns(2 * i + s, s)

            two(0)
            with pe.Fori(1, TILES // 2 - 1) as i:
                two(i)
            a_turns(TILES, 0)
            products(TILES - 1, 1)
            turns(TILES - 2, 0)
            products(TILES, 0)
            turns(TILES - 1, 1)
            turns(TILES, 0)


def mlp(nc, n_hi, n_lo, h2_in, w_mlp, conv, gf, out):
    CJ = 3
    NC = FT // CJ
    HALF = SEQ // 2
    UB = (HALF + 2) // 3
    TH = HALF // P
    POS = {"g0": 0, "v0": 1, "g1": 2, "v1": 3, "d0": 4, "d1": 5, "d2": 6, "g2": 7, "v2": 8}
    NP = len(POS)
    with ExitStack() as ctx:
        sb, ps, sem, pair = tools(nc, ctx, "mlp")
        xn = pair("xn", [P, KT, HALF + 2])
        y = sb("y", [P, TH, D])
        raw = [sb(f"raw{s}", [P, D]) for s in range(3)]
        up_w = [pair(f"up_w{s}", [P, D]) for s in range(3)]
        down_w = [pair(f"down_w{j}", [P, D]) for j in range(CJ)]
        hid = [pair(f"hid{j}", [P, HALF]) for j in range(CJ)]
        up = [sb(f"up{w}", [P, HALF + 2]) for w in range(2)]
        cv = [sb(f"cv{w}", [P, HALF]) for w in range(2)]
        cp = sb("cp", [P, 2 * CJ, 4])
        gf_row = sb("gf_row", [P, D])
        junk = sb("junk", [P, D], BF16)
        stat = sb("stat", [P, TH, 4])

        up_ps = [ps(f"up_ps{b}", [P, 512]) for b in range(3)]
        dn_ps = [ps(f"dn_ps{b}", [P, 512]) for b in range(4)]

        xn_landed, y_landed = sem("xn_landed"), sem("y_landed")
        gf_landed, cp_landed = sem("gf_landed"), sem("cp_landed")
        raw_landed = [sem(f"raw_landed{s}") for s in range(3)]
        split_hi, split_lo = sem("split_hi"), sem("split_lo")
        up_done, up_copied = sem("up_done"), sem("up_copied")
        tap_done = sem("tap_done")
        conv_done = [sem(f"conv_done{w}") for w in range(2)]
        silu_done, prod_done = sem("silu_done"), sem("prod_done")
        hid_hi, hid_lo = sem("hid_hi"), sem("hid_lo")
        dn_done, y_added = sem("dn_done"), sem("y_added")
        square_done, mean_done, root_done = sem("square_done"), sem("mean_done"), sem("root_done")
        rstd_done, y_normed, y_stored = sem("rstd_done"), sem("y_normed"), sem("y_stored")
        block = ctx.enter_context(nc.Block())
        UNITS = 2 * TH

        def chunks(eng, body, tail):
            for half in range(2):
                body(0, NC * half, half)
                with eng.Fori(1, NC) as c:
                    body(c, c + NC * half, half)
                tail(half)

        def target(pos):
            if 4 <= pos <= 6:
                return down_w[pos - 4]
            u = pos if pos < 4 else pos - CJ
            return up_w[u % 3]

        @block.sync
        def _(sp):
            sp.dma_start(gf_row[:, :], gf).then_inc(gf_landed, 16)

            def body(c, C, half):
                for pos in range(NP):
                    if not (half == 0 and isinstance(c, int) and pos < 3):
                        sp.wait_ge(split_lo, NP * C + pos - 2)
                    src = w_mlp[bass.ds(c, 1), pos, :, :].rearrange("o p n -> (o p) n")
                    sp.dma_start(raw[pos % 3][:, :], src).then_inc(raw_landed[pos % 3], 16)
                    if pos == 2:
                        if not (half == 0 and isinstance(c, int)):
                            sp.wait_ge(conv_done[1], CJ * C)
                        sp.dma_start(cp[:, :, :], row(conv, c).rearrange("p (t k) -> p t k", k=4)) \
                            .then_inc(cp_landed, 16)

            chunks(sp, body, lambda half: None)

        @block.gpsimd
        def _(pool):
            def load_xn(half):
                f0 = META - 2 + HALF * half
                if half:
                    pool.wait_ge(up_done, 3 * 6 * NC)
                for part, src in ((xn.hi, n_hi), (xn.lo, n_lo)):
                    pool.dma_start(part[:, :, :].bitcast(F32), src[:, :, f0:f0 + HALF + 2]).then_inc(xn_landed, 16)

            def load_y(half):
                if half:
                    pool.wait_ge(y_stored, 16 * TH)
                f0 = META + HALF * half
                pool.dma_start(y[:, :, :], h2_in[f0:f0 + HALF, :].rearrange("(t p) d -> p t d", p=P)) \
                    .then_inc(y_landed, 16)

            def lo(C, pos, dst):
                pool.wait_ge(split_hi, NP * C + pos + 1)
                nc.gpsimd.tensor_tensor(dst.lo[:, :], raw[pos % 3][:, :], dst.hi[:, :].bitcast(F32),
                                        ALU.subtract).then_inc(split_lo, 1)

            def body(c, C, half):
                for pos in range(NP):
                    lo(C, pos, target(pos))
                if half and isinstance(c, int):
                    load_y(1)

            load_xn(0)
            load_y(0)
            chunks(pool, body, lambda half: load_xn(1) if half == 0 else None)

        @block.scalar
        def _(act):
            def hi(C, pos, k=0):
                act.wait_ge(raw_landed[pos % 3], 16 * (3 * (C + k) + pos // 3 + 1))
                if 4 <= pos <= 6:
                    if not (isinstance(C, int) and C == 0):
                        act.wait_ge(dn_done, UNITS * C)
                else:
                    u = (pos if pos < 4 else pos - CJ) + 6 * k
                    if not (isinstance(C, int) and C == 0 and u < 3):
                        act.wait_ge(up_done, 3 * (6 * C + u - 2))
                dst = target(pos)
                nc.scalar.activation(dst.hi[:, :], raw[pos % 3][:, :], ACT.Copy).then_inc(split_hi, 1)

            def copy_up(C, j, w):
                if not (isinstance(C, int) and C == 0 and j == 0):
                    act.wait_ge(conv_done[w], CJ * C + j)
                for b in range(3):
                    act.wait_ge(up_done, 3 * (6 * C + 2 * j + w) + b + 1)
                    nc.scalar.activation(up[w][:, b * UB:(b + 1) * UB], up_ps[b][:, 0:UB], ACT.Copy) \
                        .then_inc(up_copied, 1)

            def gate(C, j):
                act.wait_ge(conv_done[0], CJ * C + j + 1)
                nc.scalar.activation(cv[0][:, :], cv[0][:, :], ACT.Silu).then_inc(silu_done, 1)
                if j == 0 and not (isinstance(C, int) and C == 0):
                    act.wait_ge(dn_done, UNITS * C)
                act.wait_ge(prod_done, CJ * C + j + 1)
                nc.scalar.activation(hid[j].hi[:, :], cv[1][:, :], ACT.Copy).then_inc(hid_hi, 1)

            def body_with(last):
                def body(c, C, half):
                    ahead = ((2, 3), (7, 8), (0, 1))
                    for j in range(CJ):
                        for w in range(2):
                            if j < 2:
                                hi(C, ahead[j][w])
                            elif not (last and isinstance(C, int) and C == 2 * NC - 1):
                                hi(C, ahead[j][w], 1)
                            copy_up(C, j, w)
                        gate(C, j)
                        if j == 0:
                            for pos in (4, 5, 6):
                                hi(C, pos)
                return body

            def tail(half):
                C = NC * (half + 1)
                for t in range(TH):
                    act.wait_ge(y_added, 4 + UNITS * (C - 1) + 2 * t + 2)
                    nc.scalar.activation(junk[:, :], y[:, t, :], ACT.Square,
                                         accum_out=stat[:, t, 0:1]).then_inc(square_done, 1)
                    act.wait_ge(mean_done, TH * half + t + 1)
                    nc.scalar.activation(stat[:, t, 2:3], stat[:, t, 1:2], ACT.Sqrt).then_inc(root_done, 1)
                    if t:
                        store(half, t - 1)
                store(half, TH - 1)

            def store(half, t):
                act.wait_ge(y_normed, TH * half + t + 1)
                f0 = HALF * half + t * P
                act.dma_start(out[f0:f0 + P, :], y[:, t, :]).then_inc(y_stored, 16)

            hi(0, 0)
            hi(0, 1)
            body = body_with(True)
            body(0, 0, 0)
            with act.Fori(1, NC) as c:
                body(c, c, 0)
            tail(0)
            body(0, NC, 1)
            with act.Fori(1, NC - 1) as c:
                body(c, c + NC, 1)
            body(NC - 1, 2 * NC - 1, 1)
            tail(1)
            act.wait_ge(y_stored, 2 * 16 * TH)

        @block.vector
        def _(dve):
            def convolve(C, j, w):
                i, T = 2 * j + w, CJ * C + j
                if j == 0 and w == 0:
                    dve.wait_ge(cp_landed, 16 * (C + 1))
                dve.wait_ge(up_copied, 3 * (6 * C + i) + 3)
                if w == 1 and not (isinstance(C, int) and C == 0 and j == 0):
                    dve.wait_ge(hid_hi, T)
                k = 2 * (6 * C + i)
                nc.vector.tensor_scalar(cv[w][:, :], up[w][:, 2:HALF + 2], cp[:, i, 2:3], cp[:, i, 3:4],
                                        ALU.mult, ALU.add).then_inc(tap_done, 1)
                for tap in (1, 0):
                    dve.wait_ge(tap_done, k + 2 - tap)
                    nc.vector.scalar_tensor_tensor(cv[w][:, :], up[w][:, tap:HALF + tap], cp[:, i, tap:tap + 1],
                                                   cv[w][:, :], ALU.mult, ALU.add) \
                        .then_inc(tap_done if tap else conv_done[w], 1)

            def product(C, j):
                T = CJ * C + j
                dve.wait_ge(silu_done, T + 1)
                dve.wait_ge(conv_done[1], T + 1)
                nc.vector.tensor_tensor(cv[1][:, :], cv[0][:, :], cv[1][:, :], ALU.mult).then_inc(prod_done, 1)

            def lows(C, j):
                dve.wait_ge(hid_hi, CJ * C + j + 1)
                nc.vector.tensor_tensor(hid[j].lo[:, :], cv[1][:, :], hid[j].hi[:, :].bitcast(F32),
                                        ALU.subtract).then_inc(hid_lo, 1)

            def add(C, u):
                t, e = u // 2, u % 2
                dve.wait_ge(dn_done, UNITS * C + u + 1)
                part = y[:, t, e * 512:(e + 1) * 512]
                nc.vector.tensor_tensor(part, dn_ps[u % 4][:, :], part, ALU.add).then_inc(y_added, 1)

            def body(c, C, half):
                for j in range(CJ):
                    for w in range(2):
                        convolve(C, j, w)
                    product(C, j)
                    if j == 0 and not isinstance(c, int):
                        dve.wait_ge(y_landed, 16 * (half + 1))
                        for u in range(UNITS):
                            add(C - 1, u)
                    lows(C, j)

            def norm(half, t):
                n = TH * half + t + 1
                dve.wait_ge(square_done, n)
                nc.vector.tensor_scalar(stat[:, t, 1:2], stat[:, t, 0:1], 1.0 / D, EPS,
                                        ALU.mult, ALU.add).then_inc(mean_done, 1)
                dve.wait_ge(root_done, n)
                nc.vector.reciprocal(stat[:, t, 3:4], stat[:, t, 2:3]).then_inc(rstd_done, 1)
                dve.wait_ge(rstd_done, n)
                nc.vector.scalar_tensor_tensor(y[:, t, :], y[:, t, :], stat[:, t, 3:4], gf_row[:, :],
                                               ALU.mult, ALU.mult).then_inc(y_normed, 1)

            def tail(half):
                C = NC * (half + 1) - 1
                for t in range(TH):
                    add(C, 2 * t)
                    add(C, 2 * t + 1)
                    if t:
                        norm(half, t - 1)
                norm(half, TH - 1)

            nc.vector.memset(stat[:, :, :], 0.0).then_inc(y_added, 4)
            dve.wait_ge(gf_landed, 16)
            chunks(dve, body, tail)

        @block.tensor
        def _(pe):
            def up_tile(C, i):
                j, w = divmod(i, 2)
                pos = POS["gv"[w] + str(j)]
                U = 6 * C + i
                pe.wait_ge(split_lo, NP * C + pos + 1)
                first = isinstance(C, int) and C == 0 and i == 0
                for b in range(3):
                    if not first:
                        pe.wait_ge(up_copied, 3 * U + b - 2)
                    for k in range(KT):
                        for n, (u, v) in enumerate(PASSES):
                            mm = nc.tensor.matmul(up_ps[b][:, 0:UB], up_w[i % 3].part(u)[:, k * P:(k + 1) * P],
                                                  xn.part(v)[:, k, b * UB:(b + 1) * UB],
                                                  start=k == 0 and n == 0, stop=k == KT - 1 and n == 2)
                    mm.then_inc(up_done, 1)

            def down(C):
                pe.wait_ge(hid_lo, CJ * C + CJ)
                pe.wait_ge(split_lo, NP * C + 7)
                for u in range(UNITS):
                    t, e = divmod(u, 2)
                    pe.wait_ge(y_added, 4 + UNITS * C + u - 3)
                    for j in range(CJ):
                        for n, (a, b) in enumerate(PASSES):
                            mm = nc.tensor.matmul(dn_ps[u % 4][:, :], hid[j].part(a)[:, t * P:(t + 1) * P],
                                                  down_w[j].part(b)[:, e * 512:(e + 1) * 512],
                                                  start=j == 0 and n == 0, stop=j == CJ - 1 and n == 2)
                    mm.then_inc(dn_done, 1)

            def body(c, C, half):
                if isinstance(c, int):
                    pe.wait_ge(xn_landed, 32 * (half + 1))
                for i in range(2 * CJ):
                    up_tile(C, i)
                    if i == 1 and not isinstance(c, int):
                        down(C - 1)

            chunks(pe, body, lambda half: down(NC * (half + 1) - 1))


def host(inputs):
    import numpy as np

    a = {k: np.asarray(v) for k, v in inputs.items()}
    w_in, o_f, o_p = a["w_in"][0], 3 * AW, 3 * AW + HEADS

    def tiled(w):
        return w.reshape(-1, P, w.shape[1]).transpose(1, 0, 2)

    q, k, v = (tiled(w_in[:, i * AW:(i + 1) * AW]) for i in range(3))
    u = tiled(w_in[:, o_p:])
    chans = [np.concatenate([q[:, :, h * HD:(h + 1) * HD], k[:, :, h * HD:(h + 1) * HD]], axis=2)
             for h in range(HEADS)]
    chans += [u[:, :, g * P:(g + 1) * P] for g in range(GROUPS)]
    chans = [c.reshape(P, KT * P) for c in chans]
    w_up, w_down = a["w_up"][0], a["w_down"][0].reshape(FT, P, D)
    gate, value = (w_up[:, i * FF:(i + 1) * FF].reshape(KT, P, FT, P).transpose(2, 1, 0, 3).reshape(FT, P, D)
                   for i in range(2))
    order = [(gate, 0), (value, 0), (gate, 1), (value, 1), (w_down, 0), (w_down, 1), (w_down, 2),
             (gate, 2), (value, 2)]
    w_mlp = np.stack([np.stack([w[3 * c + j] for w, j in order]) for c in range(FT // 3)])
    taps = np.concatenate([a["conv_w"][0], a["conv_b"]], axis=0).reshape(4, 2, FT // 3, 3, P)
    conv = taps.transpose(2, 4, 3, 1, 0).reshape(FT // 3, P, 24)
    return {
        "x": a["x"][0], "meta": a["meta_tokens"],
        "g1": np.broadcast_to(a["norm1_g"][0], (P, D)),
        "w_item": np.stack([np.concatenate(chans[2 * i:2 * i + 2], axis=1) for i in range(6)]),
        "w_v": np.stack([v[:, :, h * AW // 2:(h + 1) * AW // 2].reshape(P, -1) for h in range(2)]),
        "w_f": tiled(w_in[:, o_f:o_f + P]).reshape(P, KT * P),
        "b_f": a["b_f"][0][:, None],
        "g2": np.broadcast_to(a["norm2_g"][0], (P, D)),
        "w_out": a["w_out"][0].reshape(KT, P, D),
        "w_pool": a["w_pool"][0].transpose(1, 0, 2).reshape(P, GROUPS * P),
        "p_scale": a["pool_scale"][0].reshape(GROUPS, P).T,
        "w_mlp": w_mlp, "conv": conv,
        "gf": np.broadcast_to(a["normf_g"], (P, D)),
    }


SCRATCH = {
    "z_hi": (HEADS + GROUPS, P, L), "z_lo": (HEADS + GROUPS, P, L),
    "v_aug": (HEADS, TILES + 1, P, VA), "g_rows": (2, HEADS, L), "c_rows": (P, P),
    "a_nat": (L, AW), "d_rows": (GROUPS, P, L),
    "p_hi": (GROUPS, P, L), "p_lo": (GROUPS, P, L),
    "h2": (L, D), "n_hi": (P, KT, L), "n_lo": (P, KT, L),
}


def encoder_block(nc, i, o):
    t = {k: nc.dram_tensor(k, shape, F32).ap() for k, shape in SCRATCH.items()}
    in_projection(nc, i["x"], i["meta"], i["g1"], i["w_item"], i["w_v"], i["w_f"], i["b_f"],
                  t["z_hi"], t["z_lo"], t["v_aug"], t["g_rows"])
    attention(nc, t["z_hi"], t["z_lo"], t["v_aug"], t["g_rows"], t["c_rows"], t["a_nat"], t["d_rows"])
    out_projection(nc, i["x"], i["meta"], i["g2"], i["w_out"], i["w_pool"], i["p_scale"],
                   t["a_nat"], t["d_rows"], t["p_hi"], t["p_lo"], t["h2"], t["n_hi"], t["n_lo"])
    mlp(nc, t["n_hi"], t["n_lo"], t["h2"], i["w_mlp"], i["conv"], i["gf"], o)


def kernel(**inputs):
    import numpy as np
    import concourse.bacc as bacc
    from concourse.bass_utils import run_bass_kernel_spmd

    nc = bacc.Bacc("TRN2", target_bir_lowering=False, num_devices=1)
    arrays = {k: np.ascontiguousarray(v) for k, v in host(inputs).items()}
    ins = {k: nc.dram_tensor("in_" + k, v.shape, F32, kind="ExternalInput").ap() for k, v in arrays.items()}
    out = nc.dram_tensor("out", (SEQ, D), F32, kind="ExternalOutput").ap()
    encoder_block(nc, ins, out)
    r = run_bass_kernel_spmd(nc, [{"in_" + k: v for k, v in arrays.items()}], core_ids=[0])
    return r.results[0]["out"].reshape(1, SEQ, D)
```

```python
from contextlib import ExitStack

import concourse.bass as bass
from concourse import mybir

ALU = mybir.AluOpType
ACT = mybir.ActivationFunctionType
AX_X = mybir.AxisListType.X
F32 = mybir.dt.float32
F32R = mybir.dt.float32r
BF16 = mybir.dt.bfloat16

P = 128
D = 1024
KT = D // P
SEQ = 2048
META = 16
L = META + SEQ
TILES = SEQ // P
HEADS = 8
HD = 64
AW = HEADS * HD
GROUPS = 4
WINDOWS = (2, 4, 8, 16)
FF = 2688
FT = FF // P
EPS = 1e-6
NEG = -1e30
BLK = 416
BLKS = [(b * BLK, min(BLK, L - b * BLK)) for b in range(-(-L // BLK))]
NB = len(BLKS)
VA = 2 * HD
PASSES = (("hi", "hi"), ("hi", "lo"), ("lo", "hi"))


def frames(t):
    if isinstance(t, int) and t == 0:
        return 0, META
    return (t - 1) * P + META, P


def cols(t):
    f0, n = frames(t)
    return bass.ds(f0, n)


def row(ap, i):
    return ap[bass.ds(i, 1), :, :].rearrange("o p c -> (o p) c")


class Pair:

    def __init__(self, hi, lo):
        self.hi, self.lo = hi, lo

    def part(self, name):
        return self.hi if name == "hi" else self.lo


def tools(nc, ctx, tag):
    def sb(name, shape, dt=F32):
        return ctx.enter_context(nc.sbuf_tensor(f"{tag}_{name}", shape, dt))

    def ps(name, shape, dt=F32):
        return ctx.enter_context(nc.psum_tensor(f"{tag}_{name}", shape, dt))

    def sem(name):
        return ctx.enter_context(nc.semaphore(f"{tag}_{name}"))

    def pair(name, shape):
        return Pair(sb(name + "_hi", shape, F32R), sb(name + "_lo", shape, F32R))

    return sb, ps, sem, pair


def in_projection(nc, x, meta, g1, w_item, w_v, w_f, b_f, z_hi, z_lo, v_aug, g_rows):
    ITEMS = 2 + 6
    VH = AW // 2
    with ExitStack() as ctx:
        sb, ps, sem, pair = tools(nc, ctx, "in")
        ident = sb("ident", [P, P])
        x_both = sb("x_both", [P, L])
        x_in = [x_both[:, s * D:(s + 1) * D] for s in range(2)]
        xs_g = sb("xs_g", [P, L])
        xs, g_row = xs_g[:, 0:D], xs_g[:, D:2 * D]
        xT = pair("xT", [P, KT, L])
        w_raw = sb("w_raw", [P, 2048])
        w = [pair(f"w{s}", [P, 2048]) for s in range(2)]
        wf_raw = w_raw[:, 0:KT * P]
        stage = [sb(f"stage{s}", [P, L]) for s in range(2)]
        bf_col = sb("bf_col", [HEADS, 1])
        stat = sb("stat", [P, 2, 4])

        turn = ps("turn", [P, 2, 512])
        acc = [ps(f"acc{b}", [P, 512]) for b in range(NB)]
        junk = sb("junk", [P, D], BF16)

        ident_ready = sem("ident_ready")
        x_landed = [sem(f"x_landed{s}") for s in range(2)]
        g_landed = sem("g_landed")
        bf_landed = sem("bf_landed")
        square_done = sem("square_done")
        mean_done = sem("mean_done")
        root_done = sem("root_done")
        rstd_done = sem("rstd_done")
        xs_done = sem("xs_done")
        turn_done = sem("turn_done")
        xhi_done = sem("xhi_done")
        xlo_done = sem("xlo_done")
        w_landed = sem("w_landed")
        whi_done = sem("whi_done")
        wlo_done = sem("wlo_done")
        v_done = sem("v_done")
        vhi_done = sem("vhi_done")
        vlo_done = sem("vlo_done")
        v_stored = [sem(f"v_stored{s}") for s in range(2)]
        f_done = sem("f_done")
        f_chain = sem("f_chain")
        f_act = sem("f_act")
        f_ready = sem("f_ready")
        f_stored = sem("f_stored")
        z_done = sem("z_done")
        zhi_done = sem("zhi_done")
        zlo_done = sem("zlo_done")
        z_stored = [sem(f"z_stored{b}") for b in range(NB)]
        block = ctx.enter_context(nc.Block())

        def v_stage(t):
            return stage[t % 2][:, 0:4 * VA].rearrange("p (h c) -> p h c", c=VA)

        @block.sync
        def _(sp):
            def load_x(t, slot, peeled):
                if not peeled:
                    sp.wait_ge(xs_done, t - 1)
                src = meta if isinstance(t, int) and t == 0 else x[bass.ds((t - 1) * P, P), :]
                sp.dma_start(x_in[slot][0:src.shape[0], :], src).then_inc(x_landed[slot], 16)

            load_x(0, 0, True)
            sp.dma_start(w_raw[:, :], w_v[0, :, :]).then_inc(w_landed, 16)
            sp.dma_start(g_row[:, :], g1).then_inc(g_landed, 16)
            load_x(1, 1, True)
            load_x(2, 0, False)
            sp.dma_start(bf_col[:, :], b_f).then_inc(bf_landed, 16)
            sp.wait_ge(wlo_done, 1)
            sp.wait_ge(whi_done, 1)
            sp.dma_start(w_raw[:, 0:KT * P], w_f).then_inc(w_landed, 16)

            def store_v(t, slot, half, n):
                _, rows = frames(t)
                sp.wait_ge(vhi_done, n + 1)
                sp.wait_ge(vlo_done, n + 1)
                dst = v_aug[4 * half:4 * half + 4, bass.ds(t, 1), 0:rows, :].rearrange("h o p c -> (o p) h c")
                sp.dma_start(dst, v_stage(slot)[0:rows, :, :]).then_inc(v_stored[slot], 16)

            load_x(3, 1, False)
            store_v(0, 0, 0, 0)
            with sp.Fori(0, TILES // 2 - 2) as i:
                for s in range(2):
                    load_x(2 * i + 4 + s, s, False)
                    store_v(2 * i + 1 + s, (1 + s) % 2, 0, 2 * i + 1 + s)
            load_x(TILES, 0, False)
            for t in range(TILES - 3, TILES + 1):
                store_v(t, t % 2, 0, t)
            sp.wait_ge(wlo_done, 2)
            sp.wait_ge(whi_done, 2)
            sp.dma_start(w_raw[:, :], w_v[1, :, :]).then_inc(w_landed, 16)
            sp.wait_ge(wlo_done, 3)
            sp.wait_ge(whi_done, 3)
            sp.dma_start(w_raw[:, :], w_item[0, :, :]).then_inc(w_landed, 16)
            sp.wait_ge(f_ready, 1)
            sp.dma_start(g_rows[0, :, :], xs_g[0:HEADS, :]).then_inc(f_stored, 16)
            sp.wait_ge(f_ready, 2)
            sp.dma_start(g_rows[1, :, :], x_both[0:HEADS, :]).then_inc(f_stored, 16)
            store_v(0, 1, 1, TILES + 1)
            with sp.Fori(0, TILES // 2) as i:
                for s in range(2):
                    store_v(2 * i + 1 + s, s, 1, 2 * i + 2 + s + TILES)

            def store_z(ct, b):
                c0, n = BLKS[b]
                sp.wait_ge(zlo_done, NB * ct + b + 1)
                for part, dst in ((0, z_hi), (1, z_lo)):
                    sp.dma_start(row(dst, ct)[:, c0:c0 + n],
                                 stage[part][:, c0:c0 + n]).then_inc(z_stored[b], 16)

            def pair_stores(k, more):
                for half in range(2):
                    for b in range(NB):
                        store_z(2 * k + half, b)
                    if half == 0 and more:
                        sp.wait_ge(wlo_done, k + 5)
                        sp.wait_ge(whi_done, k + 5)
                        sp.dma_start(w_raw[:, :], row(w_item, k + 2)).then_inc(w_landed, 16)

            sp.wait_ge(wlo_done, 4)
            sp.wait_ge(whi_done, 4)
            sp.dma_start(w_raw[:, :], w_item[1, :, :]).then_inc(w_landed, 16)
            with sp.Fori(0, 4) as k:
                pair_stores(k, True)
            for k in (4, 5):
                pair_stores(k, False)
            sp.wait_ge(f_stored, 32)
            for s in range(2):
                sp.wait_ge(v_stored[s], 16 * (TILES + 1))
            for b in range(NB):
                sp.wait_ge(z_stored[b], 2 * 16 * 12)

        @block.gpsimd
        def _(pool):
            nc.gpsimd.memset(ident[:, :], 0.0).then_inc(ident_ready, 1)
            pool.wait_ge(ident_ready, 1)
            nc.gpsimd.affine_select(out=ident[:, :], in_=ident[:, :], compare_op=ALU.not_equal, fill=1.0,
                                    base=0, pattern=[[-1, P]], channel_multiplier=1).then_inc(ident_ready, 1)

            def split_lo(item, slot, n):
                pool.wait_ge(whi_done, item + 1)
                nc.gpsimd.tensor_tensor(w[slot].lo[:, 0:n], w_raw[:, 0:n], w[slot].hi[:, 0:n].bitcast(F32),
                                        ALU.subtract).then_inc(wlo_done, 1)

            split_lo(0, 0, 2048)
            split_lo(1, 1, KT * P)
            split_lo(2, 0, 2048)
            split_lo(3, 1, 2048)
            split_lo(4, 0, 2048)
            with pool.Fori(0, 2) as i:
                for s in range(2):
                    split_lo(2 * i + 5 + s, (1 + s) % 2, 2048)

        def split_hi(act, item, slot, n):
            act.wait_ge(w_landed, 16 * (item + 1))
            if not isinstance(item, int) or item > 4:
                act.wait_ge(z_done, 2 * NB * (item - 4))
            elif item in (2, 4):
                act.wait_ge(v_done, (TILES + 1) * (item // 2))
            elif item == 3:
                act.wait_ge(f_done, NB)
            nc.scalar.activation(w[slot].hi[:, 0:n], w_raw[:, 0:n], ACT.Copy).then_inc(whi_done, 1)

        @block.scalar
        def _(act):
            def squares(t, slot):
                _, n = frames(t)
                act.wait_ge(x_landed[slot], 8 * t + (16 - 8 * slot))
                nc.scalar.activation(junk[0:n, :], x_in[slot][0:n, :], ACT.Square,
                                     accum_out=stat[0:n, slot, 0:1]).then_inc(square_done, 1)
                act.wait_ge(mean_done, t + 1)
                nc.scalar.activation(stat[0:n, slot, 2:3], stat[0:n, slot, 1:2], ACT.Sqrt).then_inc(root_done, 1)

            def turned(t):
                _, n = frames(t)
                for h in range(2):
                    act.wait_ge(turn_done, 2 * t + h + 1)
                    nc.scalar.activation(xT.hi[:, 4 * h:4 * h + 4, cols(t)],
                                         turn[:, h, :].rearrange("p (k c) -> p k c", k=4)[:, :, 0:n],
                                         ACT.Copy).then_inc(xhi_done, 1)

            def v_hi(t, slot, n, peeled):
                _, rows = frames(t)
                act.wait_ge(v_done, n + 1)
                if not peeled:
                    act.wait_ge(v_stored[slot], 8 * n - 8 * slot)
                nc.scalar.activation(v_stage(slot)[0:rows, :, 0:HD].bitcast(F32R),
                                     acc[slot][0:rows, 0:VH].rearrange("p (h c) -> p h c", c=HD),
                                     ACT.Copy).then_inc(vhi_done, 1)

            split_hi(act, 0, 0, 2048)
            for t in range(5):
                squares(t, t % 2)
                turned(t)
                if t == 1:
                    split_hi(act, 1, 1, KT * P)
                if t >= 2:
                    v_hi(t - 2, t % 2, t - 2, t < 4)
            with act.Fori(0, TILES // 2 - 2) as i:
                for s in range(2):
                    t = 2 * i + 5 + s
                    squares(t, (3 + s) % 2)
                    turned(t)
                    v_hi(t - 2, (1 + s) % 2, t - 2, False)
            for t in (TILES - 1, TILES):
                v_hi(t, t % 2, t, False)
            split_hi(act, 2, 0, 2048)

            y, e = x_both[0:HEADS, :], xs_g[0:HEADS, :]
            act.wait_ge(bf_landed, 16)
            act.wait_ge(turn_done, 2 * (TILES + 1))
            for b, (c0, n) in enumerate(BLKS):
                act.wait_ge(f_done, b + 1)
                nc.scalar.activation(y[:, c0:c0 + n], acc[b][0:HEADS, 0:n], ACT.Identity,
                                     bias=bf_col[:, 0:1]).then_inc(f_act, 1)
            act.wait_ge(f_act, NB)
            nc.scalar.activation(e, y, ACT.Abs).then_inc(f_act, 1)
            act.wait_ge(f_act, NB + 1)
            nc.scalar.activation(e, e, ACT.Exp, scale=-1.0).then_inc(f_act, 1)
            act.wait_ge(f_act, NB + 2)
            nc.scalar.activation(e, e, ACT.Ln, bias=1.0).then_inc(f_act, 1)

            def v_second(t, slot, n):
                v_hi(t, slot, n, False)

            split_hi(act, 3, 1, 2048)
            v_second(0, 1, TILES + 1)
            with act.Fori(0, TILES // 2) as i:
                for s in range(2):
                    v_second(2 * i + 1 + s, s, 2 * i + 2 + s + TILES)

            def z_hi_block(ct, b, peeled):
                c0, n = BLKS[b]
                act.wait_ge(z_done, NB * ct + b + 1)
                if peeled:
                    if b == 0:
                        for s in range(2):
                            act.wait_ge(v_stored[s], 16 * (TILES + 1))
                else:
                    act.wait_ge(z_stored[b], 32 * ct)
                nc.scalar.activation(stage[0][:, c0:c0 + n].bitcast(F32R), acc[b][:, 0:n],
                                     ACT.Copy).then_inc(zhi_done, 1)

            def pair_hi(k, slot, first, more):
                for half in range(2):
                    for b in range(NB):
                        z_hi_block(2 * k + half, b, first and half == 0)
                    if half == 0 and more:
                        split_hi(act, k + 4, slot, 2048)

            pair_hi(0, 0, True, True)
            with act.Fori(0, 2) as i:
                for s in range(2):
                    pair_hi(2 * i + 1 + s, (1 + s) % 2, False, True)
            pair_hi(5, 1, False, False)

        @block.vector
        def _(dve):
            def means(t, slot):
                _, n = frames(t)
                dve.wait_ge(square_done, t + 1)
                nc.vector.tensor_scalar(stat[0:n, slot, 1:2], stat[0:n, slot, 0:1], 1.0 / D, EPS,
                                        ALU.mult, ALU.add).then_inc(mean_done, 1)
                dve.wait_ge(root_done, t + 1)
                nc.vector.reciprocal(stat[0:n, slot, 3:4], stat[0:n, slot, 2:3]).then_inc(rstd_done, 1)
                dve.wait_ge(rstd_done, t + 1)
                if isinstance(t, int) and t == 0:
                    dve.wait_ge(g_landed, 16)
                else:
                    dve.wait_ge(turn_done, 2 * t)
                nc.vector.scalar_tensor_tensor(xs[0:n, :], x_in[slot][0:n, :], stat[0:n, slot, 3:4],
                                               g_row[0:n, :], ALU.mult, ALU.mult).then_inc(xs_done, 1)

            def lows(t):
                _, n = frames(t)
                for h in range(2):
                    dve.wait_ge(xhi_done, 2 * t + h + 1)
                    part = (slice(None), slice(4 * h, 4 * h + 4), cols(t))
                    nc.vector.tensor_tensor(xT.lo[part], turn[:, h, :].rearrange("p (k c) -> p k c", k=4)[:, :, 0:n],
                                            xT.hi[part].bitcast(F32), ALU.subtract).then_inc(xlo_done, 1)

            def v_lo(t, slot, n):
                _, rows = frames(t)
                dve.wait_ge(vhi_done, n + 1)
                st = v_stage(slot)
                nc.vector.tensor_tensor(st[0:rows, :, HD:VA].bitcast(F32R),
                                        acc[slot][0:rows, 0:VH].rearrange("p (h c) -> p h c", c=HD),
                                        st[0:rows, :, 0:HD], ALU.subtract).then_inc(vlo_done, 1)

            for t in (0, 1, 2):
                means(t, t % 2)
                lows(t)
            v_lo(0, 0, 0)
            with dve.Fori(0, TILES // 2 - 1) as i:
                for s in range(2):
                    t = 2 * i + 3 + s
                    means(t, (3 + s) % 2)
                    lows(t)
                    v_lo(t - 2, (1 + s) % 2, t - 2)
            for t in (TILES - 1, TILES):
                v_lo(t, t % 2, t)

            y, e = x_both[0:HEADS, :], xs_g[0:HEADS, :]
            dve.wait_ge(f_act, NB + 3)
            nc.vector.tensor_scalar(y, y, 0.0, None, ALU.min).then_inc(f_chain, 1)
            dve.wait_ge(f_chain, 1)
            nc.vector.tensor_tensor(e, e, y, ALU.subtract).then_inc(f_chain, 1)
            dve.wait_ge(f_chain, 2)
            nc.vector.tensor_tensor_scan(y, e, e, 0.0, ALU.add, ALU.max).then_inc(f_chain, 1)
            dve.wait_ge(f_chain, 3)
            nc.vector.tensor_scalar(y, y, float(HD) ** 0.5, None, ALU.mult).then_inc(f_chain, 1)
            dve.wait_ge(f_chain, 4)
            nc.vector.tensor_copy(e.bitcast(F32R), y).then_inc(f_ready, 1)
            dve.wait_ge(f_ready, 1)
            nc.vector.tensor_tensor(y.bitcast(F32R), y, e, ALU.subtract).then_inc(f_ready, 1)

            v_lo(0, 1, TILES + 1)
            with dve.Fori(0, TILES // 2) as i:
                for s in range(2):
                    v_lo(2 * i + 1 + s, s, 2 * i + 2 + s + TILES)

            with dve.Fori(0, 12) as ct:
                for b, (c0, n) in enumerate(BLKS):
                    dve.wait_ge(zhi_done, NB * ct + b + 1)
                    nc.vector.tensor_tensor(stage[1][:, c0:c0 + n].bitcast(F32R), acc[b][:, 0:n],
                                            stage[0][:, c0:c0 + n], ALU.subtract).then_inc(zlo_done, 1)

        @block.tensor
        def _(pe):
            def turns(t):
                _, n = frames(t)
                pe.wait_ge(xs_done, t + 1)
                for h in range(2):
                    if not (isinstance(t, int) and t == 0):
                        pe.wait_ge(xlo_done, 2 * t + h - 1)
                    for k in range(4):
                        mm = nc.tensor.transpose(turn[:, h, k * P:k * P + n],
                                                 xs[0:n, (4 * h + k) * P:(4 * h + k + 1) * P], ident[0:n, 0:n])
                    mm.then_inc(turn_done, 1)

            def v_tile(t, slot, wslot, n, peeled):
                f0 = frames(t)[0]
                if not peeled:
                    pe.wait_ge(vlo_done, n - 1)
                for j, (a, b) in enumerate(PASSES):
                    for k in range(KT):
                        mm = nc.tensor.matmul(acc[slot][:, 0:VH], xT.part(a)[:, k, f0:f0 + P],
                                              w[wslot].part(b)[:, k * VH:(k + 1) * VH],
                                              start=(j == 0 and k == 0), stop=(j == 2 and k == KT - 1))
                mm.then_inc(v_done, 1)

            pe.wait_ge(ident_ready, 2)
            turns(0)
            turns(1)
            for t in range(2, TILES + 2):
                if t <= TILES:
                    turns(t)
                if t == 2:
                    pe.wait_ge(wlo_done, 1)
                pe.wait_ge(xlo_done, 2 * t)
                if t == 2:
                    v_tile(0, 0, 0, 0, True)
                v_tile(t - 1, (t - 1) % 2, 0, t - 1, t == 2)

            def channel_tile(wslot, offset, done, free):
                for b, (c0, n) in enumerate(BLKS):
                    free(b)
                    for k in range(KT):
                        for j, (a, c) in enumerate(PASSES):
                            mm = nc.tensor.matmul(acc[b][:, 0:n],
                                                  w[wslot].part(a)[:, offset + k * P:offset + (k + 1) * P],
                                                  xT.part(c)[:, k, c0:c0 + n],
                                                  start=(k == 0 and j == 0), stop=(k == KT - 1 and j == 2))
                    mm.then_inc(done, 1)

            pe.wait_ge(wlo_done, 2)

            def f_free(b):
                if b < 2:
                    pe.wait_ge(vlo_done, TILES + 1)
            channel_tile(1, 0, f_done, f_free)
            pe.wait_ge(f_act, NB)
            pe.wait_ge(wlo_done, 3)
            for t in range(TILES + 1):
                n = TILES + 1 + t
                v_tile(t, n % 2, 0, n, t < 2)

            def z_free(ct, peeled):
                def free(b):
                    if not peeled:
                        pe.wait_ge(zlo_done, NB * (ct - 1) + b + 1)
                    elif b < 2:
                        pe.wait_ge(vlo_done, 2 * (TILES + 1))
                return free

            def pair_mm(k, slot, peeled):
                pe.wait_ge(wlo_done, k + 4)
                for half in range(2):
                    channel_tile(slot, half * D, z_done, z_free(2 * k + half, peeled and half == 0))

            pair_mm(0, 1, True)
            with pe.Fori(0, 2) as i:
                for s in range(2):
                    pair_mm(2 * i + 1 + s, s, False)
            pair_mm(5, 0, False)


AB = 3
A_BLOCKS = [(b, min(b + AB, TILES + 1)) for b in range(0, TILES + 1, AB)]
A_STEPS = [(j, kt) for j, (_, last) in enumerate(A_BLOCKS) for kt in range(last)]
A_ENDS = [max(s for s, (b, _) in enumerate(A_STEPS) if b == j) for j in range(len(A_BLOCKS))]
M_CHUNKS = [(i, 0 if c == 0 else META + (4 * c - 1) * P, META + P * min(i, 4 * c + 3), c, c == i // 4)
            for i in range(TILES + 1) for c in range(i // 4 + 1)]
MC = 5
M_FIRST = 1
LAG = 5
LO_LAG = 2
EXPS, SPLITS = 5, 7
AUG = HD + 4


def attention(nc, z_hi, z_lo, v_aug, g_rows, c_rows, a_out, d_out):
    NS, NM = len(A_STEPS), len(M_CHUNKS)
    with ExitStack() as ctx:
        sb, ps, sem, pair = tools(nc, ctx, "at")
        K1 = [sb(f"K1{s}", [P, L], F32R) for s in range(2)]
        Q1 = [sb(f"Q1{s}", [P, L], F32R) for s in range(2)]
        K2 = [sb(f"K2{s}", [AUG, L], F32R) for s in range(2)]
        Q2 = [sb(f"Q2{s}", [AUG, L], F32R) for s in range(2)]
        KM, QM = sb("KM", [AUG, L], F32R), sb("QM", [AUG, L], F32R)
        V = [sb(f"V{s}", [P, TILES + 1, 2, P], F32R) for s in range(2)]
        ident = sb("ident", [P, P])
        mask = sb("mask", [P, P])
        ident_r = sb("ident_r", [P, P], F32R)
        mask_r = sb("mask_r", [P, P], F32R)
        prob = [sb(f"prob{s}", [P, AB * P]) for s in range(EXPS)]
        prob_r = [pair(f"prob_r{s}", [P, AB * P]) for s in range(SPLITS)]
        peak = sb("peak", [P, TILES + 1, MC])
        top = sb("top", [P, TILES + 1])
        shift = sb("shift", [P, 2, P // 2])
        shift_T = sb("shift_T", [P, P])
        o_sb = [sb(f"o_sb{j}", [HD + 1, AB * P]) for j in range(len(A_BLOCKS))]
        PAD = 16
        U = sb("U", [P, PAD + L])
        W = [sb(f"W{s}", [P, PAD + L]) for s in range(2)]

        score = [ps(f"score{s}", [P, 512]) for s in range(3)]
        mlog = [ps(f"mlog{s}", [P, 512]) for s in range(2)]
        o_ps = [ps(f"o_ps{s}", [P, 512]) for s in range(2)]
        turn = ps("turn", [P, 512])

        consts = sem("consts")
        consts_r = sem("consts_r")
        cleared = sem("cleared")
        max_rows_set, rows_set = sem("max_rows_set"), sem("rows_set")
        max_landed = sem("max_landed")
        rest_landed = [sem(f"rest_landed{s}") for s in range(2)]
        mlog_done = sem("mlog_done")
        peak_done = sem("peak_done")
        top_done = sem("top_done")
        shift_done = sem("shift_done")
        turn_done = sem("turn_done")
        shift_T_done = sem("shift_T_done")
        c_stored = sem("c_stored")
        c_landed = [sem(f"c_landed{s}") for s in range(2)]
        score_done = sem("score_done")
        exp_done = sem("exp_done")
        phi_done = sem("phi_done")
        plo_done = sem("plo_done")
        pv_done = sem("pv_done")
        o_copied = sem("o_copied")
        o_stored = [sem(f"o_stored{j}") for j in range(len(A_BLOCKS))]
        pool_step = sem("pool_step")
        u_landed = sem("u_landed")
        d_stored = sem("d_stored")
        block = ctx.enter_context(nc.Block())
        NJ = len(A_BLOCKS)

        def before(h, s, ring, total):
            if s >= ring:
                return total * h + s - ring + 1
            last = max(x for x in range(total) if x % ring == s % ring)
            return total * (h - 1) + last + 1

        def heads(eng, body):
            body(0, 0, True, False)
            with eng.Fori(0, HEADS // 2 - 1) as i:
                for s in range(2):
                    body(2 * i + 1 + s, (1 + s) % 2, False, False)
            body(HEADS - 1, (HEADS - 1) % 2, False, True)

        def used_rows(kt):
            return META if kt == 0 else P

        def step_shape(s):
            j, kt = A_STEPS[s]
            a, b = A_BLOCKS[j]
            q0 = frames(max(a, kt))[0]
            q1 = sum(frames(b - 1))
            return q0, q1 - q0, kt >= a

        def block_frames(j):
            a, b = A_BLOCKS[j]
            q0 = frames(a)[0]
            return q0, sum(frames(b - 1)) - q0

        def load_on(eng, dst, src, done):
            eng.dma_start(dst.bitcast(F32), src).then_inc(done, 16)

        @block.sync
        def _(sp):
            def load(dst, src, done):
                load_on(sp, dst, src, done)

            def load_maxima(h, fresh):
                if not fresh:
                    sp.wait_ge(mlog_done, NM * h)
                load(KM[0:HD, :], row(z_hi, h)[HD:P, :], max_landed)
                load(QM[0:HD, :], row(z_hi, h)[0:HD, :], max_landed)
                for i in range(2):
                    load(KM[HD + 2 + i:HD + 3 + i, :], g_rows[i, bass.ds(h, 1), :], max_landed)

            def load_head(h, s, fresh):
                if not fresh:
                    sp.wait_ge(score_done, NS * (h - 1))
                qh, kh, ql, kl = (row(z, h)[r:r + HD, :] for z in (z_hi, z_lo) for r in (0, HD))
                load(K2[s][0:HD, :], kh, rest_landed[s])
                for i in range(2):
                    load(K2[s][HD + 2 + i:HD + 3 + i, :], g_rows[i, bass.ds(h, 1), :], rest_landed[s])
                load(K1[s][0:HD, :], kh, rest_landed[s])
                load(K1[s][HD:P, :], kl, rest_landed[s])
                for i in range(2):
                    load(Q1[s][i * HD:(i + 1) * HD, :], qh, rest_landed[s])
                load(Q2[s][0:HD, :], ql, rest_landed[s])
                if not fresh:
                    sp.wait_ge(pv_done, NS * (h - 1))
                v = v_aug[bass.ds(h, 1), :, :, :].rearrange("o t p (k c) -> p (o t) k c", k=2)
                for k in range(2):
                    load(V[s][0:META, 0, k, 0:HD], v[0:META, 0, k, :], rest_landed[s])
                    load(V[s][:, 1:, k, 0:HD], v[:, 1:, k, :], rest_landed[s])

            def head(h, s, first, last):
                if not last:
                    load_maxima(h + 1, False)
                    if first:
                        sp.wait_ge(c_landed[0], 64)
                        sp.wait_ge(rows_set, 8)
                    load_head(h + 1, 1 - s, first)

            sp.wait_ge(max_rows_set, 3)
            load_maxima(0, True)
            sp.wait_ge(rows_set, 4)
            load_head(0, 0, True)
            heads(sp, head)
            for j in range(NJ):
                sp.wait_ge(o_stored[j], 16 * HEADS)

        @block.gpsimd
        def _(pool):
            for n, (t, value) in enumerate(((ident, 0.0), (mask, 0.0))):
                nc.gpsimd.memset(t[:, :], value).then_inc(consts, 1)
            pool.wait_ge(consts, 2)
            nc.gpsimd.affine_select(out=ident[:, :], in_=ident[:, :], compare_op=ALU.not_equal, fill=1.0,
                                    base=0, pattern=[[-1, P]], channel_multiplier=1).then_inc(consts, 1)
            nc.gpsimd.affine_select(out=mask[:, :], in_=mask[:, :], compare_op=ALU.is_ge, fill=NEG,
                                    base=0, pattern=[[-1, P]], channel_multiplier=1).then_inc(consts, 1)
            pool.wait_ge(consts, 4)
            fills = [fill for s in range(2) for fill in
                     ((K2[s][HD:AUG, :], 1.0), (Q2[s][HD:AUG, :], 1.0),
                      (V[s][:, :, 0, HD:P], 1.0), (V[s][:, :, 1, HD:P], 0.0))]
            for n, (part, value) in enumerate(fills):
                nc.gpsimd.memset(part.bitcast(F32), value).then_inc(rows_set, 1)
                pool.wait_ge(rows_set, n + 1)
            done = 0

            def then(instruction):
                nonlocal done
                done += 1
                instruction.then_inc(pool_step, 1)
                pool.wait_ge(pool_step, done)

            for t in (U, W[0], W[1]):
                then(nc.gpsimd.memset(t[:, 0:PAD], 0.0))
            for g, window in enumerate(WINDOWS):
                if g:
                    pool.wait_ge(d_stored, 16 * g)
                pool.dma_start(U[:, PAD:], z_hi[HEADS + g, :, :]).then_inc(u_landed, 16)
                pool.dma_start(W[0][:, PAD:], z_lo[HEADS + g, :, :]).then_inc(u_landed, 16)
                pool.wait_ge(u_landed, 32 * (g + 1))
                then(nc.gpsimd.tensor_tensor(U[:, PAD:], U[:, PAD:], W[0][:, PAD:], ALU.add))
                cur, width, k = U, 1, 0
                while width < window:
                    nxt = W[k % 2]
                    then(nc.gpsimd.tensor_tensor(nxt[:, PAD:], cur[:, PAD:], cur[:, PAD - width:PAD - width + L],
                                                 ALU.add))
                    cur, width, k = nxt, 2 * width, k + 1
                out = W[k % 2]
                then(nc.gpsimd.tensor_scalar(out[:, PAD:], cur[:, PAD:], 1.0 / window, None, ALU.mult))
                for t in range(window - 1):
                    then(nc.gpsimd.tensor_scalar(out[:, PAD + t:PAD + t + 1], cur[:, PAD + t:PAD + t + 1],
                                                 1.0 / (t + 1), None, ALU.mult))
                then(nc.gpsimd.tensor_tensor(out[:, PAD:], out[:, PAD:], U[:, PAD:], ALU.subtract))
                pool.dma_start(d_out[g, :, :], out[:, PAD:]).then_inc(d_stored, 16)
            pool.wait_ge(d_stored, 16 * GROUPS)

        @block.tensor
        def _(pe):
            def maxima(h, s, m):
                i, k0, k1, _, diagonal = M_CHUNKS[m]
                q0, n = frames(i)[0], k1 - k0
                if m == 0:
                    pe.wait_ge(max_landed, 64 * (h + 1))
                if not (isinstance(h, int) and h == 0 and m < 2):
                    pe.wait_ge(peak_done, before(h, m, 2, NM))
                mm = nc.tensor.matmul(mlog[m % 2][:, 0:n], QM[:, q0:q0 + P], KM[:, k0:k1],
                                      start=True, stop=True)
                if diagonal:
                    d = frames(i)[1]
                    mm = nc.tensor.matmul(mlog[m % 2][:, n - d:n], ident_r[:, :], mask_r[:, 0:d],
                                          start=False, stop=True, skip_group_check=True)
                mm.then_inc(mlog_done, 1)

            def turn_shift(h):
                pe.wait_ge(shift_done, 2 * (h + 1))
                nc.tensor.transpose(turn[:, 0:P], shift[:, :, :].rearrange("p a t -> p (a t)"),
                                    ident[:, :]).then_inc(turn_done, 1)

            def scores(h, s, n):
                j, kt = A_STEPS[n]
                q0, nq, diagonal = step_shape(n)
                k0 = frames(kt)[0]
                bank = score[n % 3]
                if not (isinstance(h, int) and h == 0 and n < 3):
                    pe.wait_ge(exp_done, before(h, n, 3, NS))
                nc.tensor.matmul(bank[:, 0:nq], K1[s][:, k0:k0 + P], Q1[s][:, q0:q0 + nq], start=True, stop=False)
                mm = nc.tensor.matmul(bank[:, 0:nq], K2[s][:, k0:k0 + P], Q2[s][:, q0:q0 + nq],
                                      start=False, stop=True)
                if diagonal:
                    d = frames(kt)[1]
                    mm = nc.tensor.matmul(bank[:, 0:d], mask_r[:, :], ident_r[:, 0:d], start=False, stop=True,
                                          skip_group_check=True)
                mm.then_inc(score_done, 1)

            def values(h, s, n):
                j, kt = A_STEPS[n]
                q0, nq, _ = step_shape(n)
                off, r = q0 - block_frames(j)[0], used_rows(kt)
                if kt == 0 and not (isinstance(h, int) and h == 0 and j < 2):
                    pe.wait_ge(o_copied, NJ * h + j - 1)
                pe.wait_ge(plo_done, NS * h + n + 1)
                p = prob_r[n % SPLITS]
                for i, (v, part) in enumerate(((0, p.hi), (0, p.lo), (1, p.hi))):
                    mm = nc.tensor.matmul(o_ps[j % 2][:, off:off + nq], V[s][0:r, kt, v, :], part[0:r, 0:nq],
                                          start=kt == 0 and i == 0, stop=True, skip_group_check=True)
                mm.then_inc(pv_done, 1)

            def head(h, s, first, last):
                half = (h - s) // 2 if isinstance(h, int) else None
                pe.wait_ge(rest_landed[s], 192 * (half + 1) if half is not None else 96 * (h - s) + 192)
                pe.wait_ge(c_landed[s], 64 * (half + 1) if half is not None else 32 * (h - s) + 64)
                for n in range(NS + LAG if last else NS):
                    if not last and 0 <= n - M_FIRST < NM:
                        maxima(h + 1, 1 - s, n - M_FIRST)
                    if not last and n == M_FIRST + NM + 1:
                        turn_shift(h + 1)
                    if n < NS:
                        scores(h, s, n)
                    if n >= LAG:
                        values(h, s, n - LAG)
                    elif not first:
                        values(h - 1, 1 - s, NS + n - LAG)

            pe.wait_ge(consts_r, 2)
            for m in range(NM):
                maxima(0, 0, m)
            turn_shift(0)
            heads(pe, head)

        @block.scalar
        def _(act):
            def turned(h):
                act.wait_ge(turn_done, h + 1)
                if not (isinstance(h, int) and h == 0):
                    act.wait_ge(c_stored, 16 * h)
                nc.scalar.activation(shift_T[:, :], turn[:, 0:P], ACT.Copy).then_inc(shift_T_done, 1)

            def store_shift(h):
                act.wait_ge(shift_T_done, h + 1)
                act.dma_start(c_rows, shift_T[:, :]).then_inc(c_stored, 16)

            def load_shift(h, s):
                act.wait_ge(c_stored, 16 * (h + 1))
                if isinstance(h, int) and h < 2:
                    act.wait_ge(rows_set, 4 * (h + 1))
                else:
                    act.wait_ge(score_done, NS * (h - 1))
                for i in range(2):
                    t0 = i * P // 2
                    load_on(act, Q2[s][HD + i:HD + i + 1, 0:META], c_rows[t0:t0 + 1, 0:META], c_landed[s])
                    load_on(act, Q2[s][HD + i:HD + i + 1, META:], c_rows[t0 + 1:t0 + TILES + 1, :]
                            .rearrange("(o t) c -> o (t c)", o=1), c_landed[s])

            def exps(h, n):
                _, kt = A_STEPS[n]
                _, nq, _ = step_shape(n)
                r = used_rows(kt)
                act.wait_ge(score_done, NS * h + n + 1)
                if not (isinstance(h, int) and h == 0 and n < EXPS):
                    act.wait_ge(plo_done, before(h, n, EXPS, NS))
                nc.scalar.activation(prob[n % EXPS][0:r, 0:nq], score[n % 3][0:r, 0:nq], ACT.Exp,
                                     scale=float(HD) ** -0.5).then_inc(exp_done, 1)

            def highs(h, n):
                _, kt = A_STEPS[n]
                _, nq, _ = step_shape(n)
                r = used_rows(kt)
                act.wait_ge(exp_done, NS * h + n + 1)
                if not (isinstance(h, int) and h == 0 and n < SPLITS):
                    act.wait_ge(pv_done, before(h, n, SPLITS, NS))
                nc.scalar.activation(prob_r[n % SPLITS].hi[0:r, 0:nq], prob[n % EXPS][0:r, 0:nq], ACT.Copy) \
                    .then_inc(phi_done, 1)

            def copy_o(h, j):
                n = block_frames(j)[1]
                act.wait_ge(pv_done, NS * h + A_ENDS[j] + 1)
                if not (isinstance(h, int) and h == 0):
                    act.wait_ge(o_stored[j], 16 * h)
                nc.scalar.activation(o_sb[j][:, 0:n], o_ps[j % 2][0:HD + 1, 0:n], ACT.Copy).then_inc(o_copied, 1)

            def store_o(h, j):
                q0, n = block_frames(j)
                act.wait_ge(o_copied, NJ * h + j + 1)
                act.dma_start(row(a_out, h)[:, q0:q0 + n], o_sb[j][:, 0:n]).then_inc(o_stored[j], 16)

            def head(h, s, first, last):
                for n in range(NS + 1 if last else NS):
                    if n < NS:
                        exps(h, n)
                    if n:
                        highs(h, n - 1)
                    elif not first:
                        highs(h - 1, NS - 1)
                    for j in range(NJ - 1):
                        if n == A_ENDS[j] + LAG + 1:
                            copy_o(h, j)
                        if n == A_ENDS[j] + LAG + 2:
                            store_o(h, j)
                    if not first and n == LAG:
                        copy_o(h - 1, NJ - 1)
                    if not first and n == LAG + 1:
                        store_o(h - 1, NJ - 1)
                    if not last and n == M_FIRST + NM + 3:
                        turned(h + 1)
                    if not last and n == M_FIRST + NM + 4:
                        store_shift(h + 1)
                    if not last and n == M_FIRST + NM + 8:
                        load_shift(h + 1, 1 - s)
                if last:
                    copy_o(h, NJ - 1)
                    store_o(h, NJ - 1)

            act.wait_ge(consts, 4)
            for src, dst in ((ident, ident_r), (mask, mask_r)):
                nc.scalar.activation(dst[:, :], src[:, :], ACT.Copy).then_inc(consts_r, 1)
            turned(0)
            store_shift(0)
            load_shift(0, 0)
            heads(act, head)

        @block.vector
        def _(dve):
            def peaks(h, m):
                i, k0, k1, c, _ = M_CHUNKS[m]
                r = frames(i)[1]
                dve.wait_ge(mlog_done, NM * h + m + 1)
                if m == 0 and not (isinstance(h, int) and h == 0):
                    dve.wait_ge(top_done, h)
                nc.vector.tensor_reduce(peak[0:r, i, c:c + 1], mlog[m % 2][0:r, 0:k1 - k0], AX_X,
                                        ALU.max).then_inc(peak_done, 1)

            def shifts(h):
                dve.wait_ge(peak_done, NM * (h + 1))
                nc.vector.tensor_reduce(top[:, :], peak[:, :, :], AX_X, ALU.max).then_inc(top_done, 1)
                dve.wait_ge(top_done, h + 1)
                if not (isinstance(h, int) and h == 0):
                    dve.wait_ge(turn_done, h)
                nc.vector.tensor_scalar(shift[:, 0, 0:TILES + 1].bitcast(F32R), top[:, :], -1.0, None, ALU.mult) \
                    .then_inc(shift_done, 1)
                dve.wait_ge(shift_done, 2 * h + 1)
                nc.vector.scalar_tensor_tensor(shift[:, 1, 0:TILES + 1].bitcast(F32R), top[:, :], -1.0, shift[:, 0, 0:TILES + 1],
                                               ALU.mult, ALU.subtract).then_inc(shift_done, 1)

            def lows(h, n):
                _, kt = A_STEPS[n]
                _, nq, _ = step_shape(n)
                r = used_rows(kt)
                dve.wait_ge(phi_done, NS * h + n + 1)
                nc.vector.tensor_tensor(prob_r[n % SPLITS].lo[0:r, 0:nq], prob[n % EXPS][0:r, 0:nq],
                                        prob_r[n % SPLITS].hi[0:r, 0:nq].bitcast(F32), ALU.subtract) \
                    .then_inc(plo_done, 1)

            def head(h, s, first, last):
                for n in range(NS + LO_LAG if last else NS):
                    if not last and 0 <= n - M_FIRST < NM:
                        peaks(h + 1, n - M_FIRST)
                    if not last and n == M_FIRST + NM:
                        shifts(h + 1)
                    if n >= LO_LAG:
                        lows(h, n - LO_LAG)
                    elif not first:
                        lows(h - 1, NS + n - LO_LAG)

            for t in (KM, QM):
                nc.vector.memset(t[HD:AUG, :].bitcast(F32), 1.0).then_inc(max_rows_set, 1)
            dve.wait_ge(max_rows_set, 2)
            nc.vector.memset(QM[HD:HD + 2, :].bitcast(F32), 0.0).then_inc(max_rows_set, 1)
            nc.vector.memset(peak[:, :, :], NEG).then_inc(cleared, 1)
            nc.vector.memset(shift[:, :, :], 0.0).then_inc(cleared, 1)
            dve.wait_ge(cleared, 2)
            for m in range(NM):
                peaks(0, m)
            shifts(0)
            heads(dve, head)


def out_projection(nc, x, meta, g2, w_out, w_pool, p_scale, a_in, d_in, inv_rows, p_hi, p_lo, h2_out, n_hi, n_lo):
    with ExitStack() as ctx:
        sb, ps, sem, pair = tools(nc, ctx, "out")
        ident = sb("ident", [P, P])
        g_row = sb("g_row", [P, D])
        wp_raw = sb("wp_raw", [P, GROUPS * P])
        wp = pair("wp", [P, GROUPS * P])
        scale = sb("scale", [P, GROUPS])
        DS = 4
        d_raw = [sb(f"d_raw{s}", [P, BLK]) for s in range(DS)]
        dd = [pair(f"dd{s}", [P, BLK]) for s in range(DS)]
        p_st = [[sb(f"p_st{s}{i}", [P, BLK]) for i in range(2)] for s in range(DS)]
        w_raw = [sb(f"w_raw{s}", [P, D]) for s in range(2)]
        w = pair("w", [P, KT, D])
        h_in = [sb(f"h_in{s}", [P, D]) for s in range(2)]
        a_raw = [sb(f"a_raw{s}", [P, AW // P, P]) for s in range(2)]
        inv = [sb(f"inv{s}", [P, AW // P, P]) for s in range(2)]
        sums = sb("sums", [P, HEADS * L // P])
        cat = [pair(f"cat{s}", [P, KT, P]) for s in range(2)]
        h2 = [sb(f"h2{s}", [P, D]) for s in range(2)]
        xs = sb("xs", [P, D])
        junk = sb("junk", [P, D], BF16)
        nT = [pair(f"nT{s}", [P, KT, P]) for s in range(2)]
        stat = sb("stat", [P, 2, 4])

        acc = ps("acc", [P, 2, 2, 512])
        turn = ps("turn", [P, 2, 512])
        mapped = [ps(f"mapped{s}", [P, 512]) for s in range(2)]

        consts, cleared = sem("consts"), sem("cleared")
        sums_landed, inv_done, inv_stored = sem("sums_landed"), sem("inv_done"), sem("inv_stored")
        small_landed, wp_landed = sem("small_landed"), sem("wp_landed")
        wp_hi_done, wp_lo_done = sem("wp_hi_done"), sem("wp_lo_done")
        d_landed = [sem(f"d_landed{s}") for s in range(DS)]
        d_hi_done, d_lo_done = sem("d_hi_done"), sem("d_lo_done")
        map_done, p_hi_done, p_lo_done = sem("map_done"), sem("p_hi_done"), sem("p_lo_done")
        p_stored = [sem(f"p_stored{s}") for s in range(DS)]
        w_landed = [sem(f"w_landed{s}") for s in range(2)]
        w_hi_done, w_lo_done = sem("w_hi_done"), sem("w_lo_done")
        h_landed = [sem(f"h_landed{s}") for s in range(2)]
        a_landed = [sem(f"a_landed{s}") for s in range(2)]
        cat_landed = [sem(f"cat_landed{s}") for s in range(2)]
        a_scaled, a_hi_done, a_lo_done = sem("a_scaled"), sem("a_hi_done"), sem("a_lo_done")
        out_done, h2_done = sem("out_done"), sem("h2_done")
        square_done, mean_done, root_done = sem("square_done"), sem("mean_done"), sem("root_done")
        rstd_done, xs_done = sem("rstd_done"), sem("xs_done")
        turn_done, n_hi_done, n_lo_done = sem("turn_done"), sem("n_hi_done"), sem("n_lo_done")
        h2_stored = [sem(f"h2_stored{s}") for s in range(2)]
        n_stored = [sem(f"n_stored{s}") for s in range(2)]
        block = ctx.enter_context(nc.Block())
        UNITS = [(g, b) for g in range(GROUPS) for b in range(NB)]
        NU = len(UNITS)

        def early(t, n=2):
            return isinstance(t, int) and t < n

        @block.sync
        def _(sp):
            def load_d(n):
                g, b = UNITS[n]
                c0, m = BLKS[b]
                if n >= DS:
                    sp.wait_ge(d_lo_done, n - DS + 1)
                sp.dma_start(d_raw[n % DS][:, 0:m], d_in[g, :, c0:c0 + m]).then_inc(d_landed[n % DS], 16)

            sp.dma_start(wp_raw[:, :], w_pool).then_inc(wp_landed, 16)
            for n in range(DS):
                load_d(n)
            rows = P // HEADS
            for h in range(HEADS):
                sp.dma_start(sums[h * rows:(h + 1) * rows, :],
                             a_in[h, HD:HD + 1, :].rearrange("o (r c) -> (o r) c", r=rows)).then_inc(sums_landed, 16)
            sp.dma_start(scale[:, :], p_scale).then_inc(small_landed, 16)
            sp.dma_start(g_row[:, :], g2).then_inc(small_landed, 16)

            def load_w(k):
                if k >= 2:
                    sp.wait_ge(w_lo_done, k - 1)
                sp.dma_start(w_raw[k % 2][:, :], w_out[k, :, :]).then_inc(w_landed[k % 2], 16)

            load_w(0)
            load_w(1)
            sp.wait_ge(inv_done, 1)
            sp.dma_start(inv_rows.rearrange("h (r c) -> (h r) c", r=rows), sums[:, :]).then_inc(inv_stored, 16)
            for n in range(NU):
                g, b = UNITS[n]
                c0, m = BLKS[b]
                if n + DS < NU:
                    load_d(n + DS)
                if n + 2 < KT:
                    load_w(n + 2)
                sp.wait_ge(p_lo_done, n + 1)
                for i, dst in enumerate((p_hi, p_lo)):
                    sp.dma_start(dst[g, :, c0:c0 + m], p_st[n % DS][i][:, 0:m]).then_inc(p_stored[n % DS], 16)
            sp.wait_ge(inv_stored, 16)
            for s in range(DS):
                sp.wait_ge(p_stored[s], 32 * (NU // DS))

            def load(t, s):
                f0, n = frames(t)
                if not early(t):
                    sp.wait_ge(a_hi_done, 1)
                    sp.wait_ge(h2_done, 2 * t - 2)
                src = meta if isinstance(t, int) and t == 0 else x[bass.ds((t - 1) * P, P), :]
                sp.dma_start(h_in[s][0:n, :], src).then_inc(h_landed[s], 16)
                for e in range(2):
                    part = slice(e * HD, (e + 1) * HD)
                    heads = a_in.rearrange("(k e) r c -> r e k c", e=2)
                    sp.dma_start(a_raw[s][part, :, 0:n], heads[0:HD, e, :, bass.ds(f0, n)]).then_inc(a_landed[s], 16)
                    scales = inv_rows.rearrange("(o k e) c -> o e k c", e=2, o=1)[:, e, :, bass.ds(f0, n)]
                    sp.dma_start(inv[s][part, :, 0:n], scales.to_broadcast([HD, AW // P, n])).then_inc(a_landed[s], 16)
                for part, src in ((cat[s].hi, p_hi), (cat[s].lo, p_lo)):
                    sp.dma_start(part[:, GROUPS:KT, 0:n].bitcast(F32),
                                 src[:, :, bass.ds(f0, n)].rearrange("g p c -> p g c")).then_inc(cat_landed[s], 16)

            def store_h2(t, s):
                f0, n = frames(t)
                sp.wait_ge(out_done, 2)
                sp.wait_ge(h2_done, 2 * t + 2)
                sp.dma_start(h2_out[bass.ds(f0, n), :], h2[s][0:n, :]).then_inc(h2_stored[s], 16)

            def store_n(t, s):
                f0, n = frames(t)
                sp.wait_ge(n_hi_done, 2)
                sp.wait_ge(n_lo_done, 2 * t + 2)
                for part, dst in ((nT[s].hi, n_hi), (nT[s].lo, n_lo)):
                    sp.dma_start(dst[:, :, bass.ds(f0, n)], part[:, :, 0:n].bitcast(F32)).then_inc(n_stored[s], 16)

            load(0, 0)
            load(1, 1)
            load(2, 0)
            store_h2(0, 0)
            def two(i):
                for s in range(2):
                    load(2 * i + 3 + s, (1 + s) % 2)
                    store_h2(2 * i + 1 + s, (1 + s) % 2)
                    store_n(2 * i + s, s)

            two(0)
            with sp.Fori(1, TILES // 2 - 1) as i:
                two(i)
            for t in (TILES - 1, TILES):
                store_h2(t, t % 2)
            for t in range(TILES - 2, TILES + 1):
                store_n(t, t % 2)
            for s in range(2):
                sp.wait_ge(h2_stored[s], 16 * ((TILES + 2 - s) // 2))
                sp.wait_ge(n_stored[s], 32 * ((TILES + 2 - s) // 2))

        @block.gpsimd
        def _(pool):
            nc.gpsimd.memset(ident[:, :], 0.0).then_inc(consts, 1)
            pool.wait_ge(consts, 1)
            nc.gpsimd.affine_select(out=ident[:, :], in_=ident[:, :], compare_op=ALU.not_equal, fill=1.0,
                                    base=0, pattern=[[-1, P]], channel_multiplier=1).then_inc(consts, 1)
            pool.wait_ge(consts, 2)
            for k in range(KT):
                pool.wait_ge(w_hi_done, k + 1)
                nc.gpsimd.tensor_tensor(w.lo[:, k, :], w_raw[k % 2][:, :], w.hi[:, k, :].bitcast(F32),
                                        ALU.subtract).then_inc(w_lo_done, 1)

        @block.scalar
        def _(act):
            act.wait_ge(wp_landed, 16)
            nc.scalar.activation(wp.hi[:, :], wp_raw[:, :], ACT.Copy).then_inc(wp_hi_done, 1)

            def d_hi(n):
                _, b = UNITS[n]
                m = BLKS[b][1]
                act.wait_ge(d_landed[n % DS], 16 * (n // DS + 1))
                if n >= DS:
                    act.wait_ge(map_done, n - DS + 1)
                nc.scalar.activation(dd[n % DS].hi[:, 0:m], d_raw[n % DS][:, 0:m], ACT.Copy).then_inc(d_hi_done, 1)

            for n in range(DS - 1):
                d_hi(n)
            act.wait_ge(small_landed, 32)
            for n, (g, b) in enumerate(UNITS):
                m = BLKS[b][1]
                act.wait_ge(map_done, n + 1)
                if n >= DS:
                    act.wait_ge(p_stored[n % DS], 32 * (n // DS))
                nc.scalar.activation(p_st[n % DS][0][:, 0:m].bitcast(F32R), mapped[n % 2][:, 0:m], ACT.Copy,
                                     scale=scale[:, g:g + 1]).then_inc(p_hi_done, 1)
                if n + DS - 1 < NU:
                    d_hi(n + DS - 1)
                if n < KT:
                    act.wait_ge(w_landed[n % 2], 16 * (n // 2 + 1))
                    nc.scalar.activation(w.hi[:, n, :], w_raw[n % 2][:, :], ACT.Copy).then_inc(w_hi_done, 1)

            def a_his(t, s):
                _, n = frames(t)
                act.wait_ge(a_scaled, t + 1)
                if not early(t):
                    act.wait_ge(out_done, 2 * t - 2)
                nc.scalar.activation(cat[s].hi[:, 0:GROUPS, 0:n],
                                     a_raw[s][:, :, 0:n], ACT.Copy).then_inc(a_hi_done, 1)

            def norms(t, s, ahead=True):
                _, n = frames(t)
                act.wait_ge(h2_done, 2 * t + 2)
                nc.scalar.activation(junk[0:n, :], h2[s][0:n, :], ACT.Square,
                                     accum_out=stat[0:n, s, 0:1]).then_inc(square_done, 1)
                act.wait_ge(mean_done, t + 1)
                nc.scalar.activation(stat[0:n, s, 2:3], stat[0:n, s, 1:2], ACT.Sqrt).then_inc(root_done, 1)
                if ahead:
                    a_his(t + 2, s)
                for h in range(2):
                    act.wait_ge(turn_done, 2 * t + h + 1)
                    if not early(t) and h == 0:
                        act.wait_ge(n_stored[s], 16 * (t - s))
                    nc.scalar.activation(nT[s].hi[:, 4 * h:4 * h + 4, 0:n],
                                         turn[:, h, :].rearrange("p (k c) -> p k c", k=4)[:, :, 0:n],
                                         ACT.Copy).then_inc(n_hi_done, 1)

            a_his(0, 0)
            a_his(1, 1)
            norms(0, 0)
            def two(i):
                for s in range(2):
                    norms(2 * i + 1 + s, (1 + s) % 2)

            two(0)
            with act.Fori(1, TILES // 2 - 1) as i:
                two(i)
            norms(TILES - 1, 1, False)
            norms(TILES, 0, False)

        @block.vector
        def _(dve):
            dve.wait_ge(wp_hi_done, 1)
            nc.vector.tensor_tensor(wp.lo[:, :], wp_raw[:, :], wp.hi[:, :].bitcast(F32), ALU.subtract) \
                .then_inc(wp_lo_done, 1)

            def d_low(n):
                m = BLKS[UNITS[n][1]][1]
                dve.wait_ge(d_hi_done, n + 1)
                nc.vector.tensor_tensor(dd[n % DS].lo[:, 0:m], d_raw[n % DS][:, 0:m],
                                        dd[n % DS].hi[:, 0:m].bitcast(F32), ALU.subtract).then_inc(d_lo_done, 1)

            for n in range(DS - 1):
                d_low(n)
            dve.wait_ge(sums_landed, 16 * HEADS)
            nc.vector.reciprocal(sums[:, :], sums[:, :]).then_inc(inv_done, 1)
            for n, (g, b) in enumerate(UNITS):
                m = BLKS[b][1]
                dve.wait_ge(p_hi_done, n + 1)
                nc.vector.scalar_tensor_tensor(p_st[n % DS][1][:, 0:m].bitcast(F32R), mapped[n % 2][:, 0:m],
                                               scale[:, g:g + 1], p_st[n % DS][0][:, 0:m], ALU.mult,
                                               ALU.subtract).then_inc(p_lo_done, 1)
                if n + DS - 1 < NU:
                    d_low(n + DS - 1)

            def a_lows(t, s):
                _, n = frames(t)
                dve.wait_ge(a_landed[s], 32 * t + (64 - 32 * s))
                nc.vector.tensor_tensor(a_raw[s][:, :, 0:n], a_raw[s][:, :, 0:n], inv[s][:, :, 0:n], ALU.mult) \
                    .then_inc(a_scaled, 1)
                dve.wait_ge(a_hi_done, t + 1)
                nc.vector.tensor_tensor(cat[s].lo[:, 0:GROUPS, 0:n],
                                        a_raw[s][:, :, 0:n],
                                        cat[s].hi[:, 0:GROUPS, 0:n].bitcast(F32), ALU.subtract) \
                    .then_inc(a_lo_done, 1)

            def residual(t, s):
                _, n = frames(t)
                dve.wait_ge(h_landed[s], 8 * t + (16 - 8 * s))
                if not early(t):
                    dve.wait_ge(h2_stored[s], 8 * (t - s))
                for h in range(2):
                    dve.wait_ge(out_done, 2 * t + h + 1)
                    nc.vector.tensor_tensor(h2[s][0:n, h * 512:(h + 1) * 512], acc[0:n, s, h, :],
                                            h_in[s][0:n, h * 512:(h + 1) * 512], ALU.add).then_inc(h2_done, 1)

            def norms(t, s):
                _, n = frames(t)
                dve.wait_ge(square_done, t + 1)
                nc.vector.tensor_scalar(stat[0:n, s, 1:2], stat[0:n, s, 0:1], 1.0 / D, EPS,
                                        ALU.mult, ALU.add).then_inc(mean_done, 1)
                dve.wait_ge(root_done, t + 1)
                nc.vector.reciprocal(stat[0:n, s, 3:4], stat[0:n, s, 2:3]).then_inc(rstd_done, 1)
                dve.wait_ge(rstd_done, t + 1)
                if not early(t, 1):
                    dve.wait_ge(turn_done, 2 * t)
                nc.vector.scalar_tensor_tensor(xs[0:n, :], h2[s][0:n, :], stat[0:n, s, 3:4], g_row[0:n, :],
                                               ALU.mult, ALU.mult).then_inc(xs_done, 1)

            def n_lows(t, s):
                _, n = frames(t)
                for h in range(2):
                    dve.wait_ge(n_hi_done, 2 * t + h + 1)
                    part = (slice(None), slice(4 * h, 4 * h + 4), slice(0, n))
                    nc.vector.tensor_tensor(nT[s].lo[part], turn[:, h, :].rearrange("p (k c) -> p k c", k=4)[:, :, 0:n],
                                            nT[s].hi[part].bitcast(F32), ALU.subtract).then_inc(n_lo_done, 1)

            def rest(t, s, ahead=True):
                residual(t, s)
                norms(t, s)
                if ahead:
                    a_lows(t + 2, s)
                n_lows(t, s)

            nc.vector.memset(cat[0].hi[:, :, META:].bitcast(F32), 0.0).then_inc(cleared, 1)
            nc.vector.memset(cat[0].lo[:, :, META:].bitcast(F32), 0.0).then_inc(cleared, 1)
            dve.wait_ge(small_landed, 32)
            a_lows(0, 0)
            a_lows(1, 1)
            rest(0, 0)
            def two(i):
                for s in range(2):
                    rest(2 * i + 1 + s, (1 + s) % 2)

            two(0)
            with dve.Fori(1, TILES // 2 - 1) as i:
                two(i)
            rest(TILES - 1, 1, False)
            rest(TILES, 0, False)

        @block.tensor
        def _(pe):
            pe.wait_ge(wp_lo_done, 1)
            for n, (g, b) in enumerate(UNITS):
                m = BLKS[b][1]
                pe.wait_ge(d_lo_done, n + 1)
                if n >= 2:
                    pe.wait_ge(p_lo_done, n - 1)
                for j, (u, v) in enumerate(PASSES):
                    mm = nc.tensor.matmul(mapped[n % 2][:, 0:m], wp.part(u)[:, g * P:(g + 1) * P],
                                          dd[n % DS].part(v)[:, 0:m], start=j == 0, stop=j == 2)
                mm.then_inc(map_done, 1)

            def products(t, s):
                pe.wait_ge(cat_landed[s], 16 * t + (32 - 16 * s))
                pe.wait_ge(a_lo_done, t + 1)
                if not early(t):
                    pe.wait_ge(h2_done, 2 * t - 2)
                for h in range(2):
                    for k in range(KT):
                        for j, (u, v) in enumerate(PASSES):
                            mm = nc.tensor.matmul(acc[:, s, h, :], cat[s].part(u)[:, k, :],
                                                  w.part(v)[:, k, h * 512:(h + 1) * 512],
                                                  start=k == 0 and j == 0, stop=k == KT - 1 and j == 2)
                    mm.then_inc(out_done, 1)

            def turns(t, s):
                _, n = frames(t)
                pe.wait_ge(xs_done, t + 1)
                for h in range(2):
                    if not early(t, 1):
                        pe.wait_ge(n_lo_done, 2 * t + h - 1)
                    for k in range(4):
                        mm = nc.tensor.transpose(turn[:, h, k * P:k * P + n],
                                                 xs[0:n, (4 * h + k) * P:(4 * h + k + 1) * P], ident[0:n, 0:n])
                    mm.then_inc(turn_done, 1)

            pe.wait_ge(consts, 2)
            pe.wait_ge(w_lo_done, KT)
            pe.wait_ge(cleared, 2)
            products(0, 0)
            def two(i):
                for s in range(2):
                    products(2 * i + 1 + s, (1 + s) % 2)
                    turns(2 * i + s, s)

            two(0)
            with pe.Fori(1, TILES // 2 - 1) as i:
                two(i)
            products(TILES - 1, 1)
            turns(TILES - 2, 0)
            products(TILES, 0)
            turns(TILES - 1, 1)
            turns(TILES, 0)


def mlp(nc, n_hi, n_lo, h2_in, w_mlp, conv, gf, out):
    CJ = 3
    NC = FT // CJ
    HALF = SEQ // 2
    UB = (HALF + 2) // 3
    TH = HALF // P
    POS = {"g0": 0, "v0": 1, "g1": 2, "v1": 3, "d0": 4, "d1": 5, "d2": 6, "g2": 7, "v2": 8}
    NP = len(POS)
    with ExitStack() as ctx:
        sb, ps, sem, pair = tools(nc, ctx, "mlp")
        xn = pair("xn", [P, KT, HALF + 2])
        y = sb("y", [P, TH, D])
        raw = [sb(f"raw{s}", [P, D]) for s in range(3)]
        up_w = [pair(f"up_w{s}", [P, D]) for s in range(3)]
        down_w = [pair(f"down_w{j}", [P, D]) for j in range(CJ)]
        hid = [pair(f"hid{j}", [P, HALF]) for j in range(CJ)]
        up = [sb(f"up{w}", [P, HALF + 2]) for w in range(2)]
        cv = [sb(f"cv{w}", [P, HALF]) for w in range(2)]
        cp = sb("cp", [P, 2 * CJ, 4])
        gf_row = sb("gf_row", [P, D])
        junk = sb("junk", [P, D], BF16)
        stat = sb("stat", [P, TH, 4])

        up_ps = [ps(f"up_ps{b}", [P, 512]) for b in range(3)]
        dn_ps = [ps(f"dn_ps{b}", [P, 512]) for b in range(4)]

        xn_landed, y_landed = sem("xn_landed"), sem("y_landed")
        gf_landed, cp_landed = sem("gf_landed"), sem("cp_landed")
        raw_landed = [sem(f"raw_landed{s}") for s in range(3)]
        split_hi, split_lo = sem("split_hi"), sem("split_lo")
        up_done, up_copied = sem("up_done"), sem("up_copied")
        tap_done = sem("tap_done")
        conv_done = [sem(f"conv_done{w}") for w in range(2)]
        silu_done, prod_done = sem("silu_done"), sem("prod_done")
        hid_hi, hid_lo = sem("hid_hi"), sem("hid_lo")
        dn_done, y_added = sem("dn_done"), sem("y_added")
        square_done, mean_done, root_done = sem("square_done"), sem("mean_done"), sem("root_done")
        rstd_done, y_normed, y_stored = sem("rstd_done"), sem("y_normed"), sem("y_stored")
        block = ctx.enter_context(nc.Block())
        UNITS = 2 * TH

        def chunks(eng, body, tail):
            for half in range(2):
                body(0, NC * half, half)
                with eng.Fori(1, NC) as c:
                    body(c, c + NC * half, half)
                tail(half)

        def target(pos):
            if 4 <= pos <= 6:
                return down_w[pos - 4]
            u = pos if pos < 4 else pos - CJ
            return up_w[u % 3]

        @block.sync
        def _(sp):
            sp.dma_start(gf_row[:, :], gf).then_inc(gf_landed, 16)

            def body(c, C, half):
                for pos in range(NP):
                    if not (half == 0 and isinstance(c, int) and pos < 3):
                        sp.wait_ge(split_lo, NP * C + pos - 2)
                    src = w_mlp[bass.ds(c, 1), pos, :, :].rearrange("o p n -> (o p) n")
                    sp.dma_start(raw[pos % 3][:, :], src).then_inc(raw_landed[pos % 3], 16)
                    if pos == 2:
                        if not (half == 0 and isinstance(c, int)):
                            sp.wait_ge(conv_done[1], CJ * C)
                        sp.dma_start(cp[:, :, :], row(conv, c).rearrange("p (t k) -> p t k", k=4)) \
                            .then_inc(cp_landed, 16)

            chunks(sp, body, lambda half: None)

        @block.gpsimd
        def _(pool):
            def load_xn(half):
                f0 = META - 2 + HALF * half
                if half:
                    pool.wait_ge(up_done, 3 * 6 * NC)
                for part, src in ((xn.hi, n_hi), (xn.lo, n_lo)):
                    pool.dma_start(part[:, :, :].bitcast(F32), src[:, :, f0:f0 + HALF + 2]).then_inc(xn_landed, 16)

            def load_y(half):
                if half:
                    pool.wait_ge(y_stored, 16 * TH)
                f0 = META + HALF * half
                pool.dma_start(y[:, :, :], h2_in[f0:f0 + HALF, :].rearrange("(t p) d -> p t d", p=P)) \
                    .then_inc(y_landed, 16)

            def lo(C, pos, dst):
                pool.wait_ge(split_hi, NP * C + pos + 1)
                nc.gpsimd.tensor_tensor(dst.lo[:, :], raw[pos % 3][:, :], dst.hi[:, :].bitcast(F32),
                                        ALU.subtract).then_inc(split_lo, 1)

            def body(c, C, half):
                for pos in range(NP):
                    lo(C, pos, target(pos))
                if half and isinstance(c, int):
                    load_y(1)

            load_xn(0)
            load_y(0)
            chunks(pool, body, lambda half: load_xn(1) if half == 0 else None)

        @block.scalar
        def _(act):
            def hi(C, pos, k=0):
                act.wait_ge(raw_landed[pos % 3], 16 * (3 * (C + k) + pos // 3 + 1))
                if 4 <= pos <= 6:
                    if not (isinstance(C, int) and C == 0):
                        act.wait_ge(dn_done, UNITS * C)
                else:
                    u = (pos if pos < 4 else pos - CJ) + 6 * k
                    if not (isinstance(C, int) and C == 0 and u < 3):
                        act.wait_ge(up_done, 3 * (6 * C + u - 2))
                dst = target(pos)
                nc.scalar.activation(dst.hi[:, :], raw[pos % 3][:, :], ACT.Copy).then_inc(split_hi, 1)

            def copy_up(C, j, w):
                if not (isinstance(C, int) and C == 0 and j == 0):
                    act.wait_ge(conv_done[w], CJ * C + j)
                for b in range(3):
                    act.wait_ge(up_done, 3 * (6 * C + 2 * j + w) + b + 1)
                    nc.scalar.activation(up[w][:, b * UB:(b + 1) * UB], up_ps[b][:, 0:UB], ACT.Copy) \
                        .then_inc(up_copied, 1)

            def gate(C, j):
                act.wait_ge(conv_done[0], CJ * C + j + 1)
                nc.scalar.activation(cv[0][:, :], cv[0][:, :], ACT.Silu).then_inc(silu_done, 1)
                if j == 0 and not (isinstance(C, int) and C == 0):
                    act.wait_ge(dn_done, UNITS * C)
                act.wait_ge(prod_done, CJ * C + j + 1)
                nc.scalar.activation(hid[j].hi[:, :], cv[1][:, :], ACT.Copy).then_inc(hid_hi, 1)

            def body_with(last):
                def body(c, C, half):
                    ahead = ((2, 3), (7, 8), (0, 1))
                    for j in range(CJ):
                        for w in range(2):
                            if j < 2:
                                hi(C, ahead[j][w])
                            elif not (last and isinstance(C, int) and C == 2 * NC - 1):
                                hi(C, ahead[j][w], 1)
                            copy_up(C, j, w)
                        gate(C, j)
                        if j == 0:
                            for pos in (4, 5, 6):
                                hi(C, pos)
                return body

            def tail(half):
                C = NC * (half + 1)
                for t in range(TH):
                    act.wait_ge(y_added, 4 + UNITS * (C - 1) + 2 * t + 2)
                    nc.scalar.activation(junk[:, :], y[:, t, :], ACT.Square,
                                         accum_out=stat[:, t, 0:1]).then_inc(square_done, 1)
                    act.wait_ge(mean_done, TH * half + t + 1)
                    nc.scalar.activation(stat[:, t, 2:3], stat[:, t, 1:2], ACT.Sqrt).then_inc(root_done, 1)
                    if t:
                        store(half, t - 1)
                store(half, TH - 1)

            def store(half, t):
                act.wait_ge(y_normed, TH * half + t + 1)
                f0 = HALF * half + t * P
                act.dma_start(out[f0:f0 + P, :], y[:, t, :]).then_inc(y_stored, 16)

            hi(0, 0)
            hi(0, 1)
            body = body_with(True)
            body(0, 0, 0)
            with act.Fori(1, NC) as c:
                body(c, c, 0)
            tail(0)
            body(0, NC, 1)
            with act.Fori(1, NC - 1) as c:
                body(c, c + NC, 1)
            body(NC - 1, 2 * NC - 1, 1)
            tail(1)
            act.wait_ge(y_stored, 2 * 16 * TH)

        @block.vector
        def _(dve):
            def convolve(C, j, w):
                i, T = 2 * j + w, CJ * C + j
                if j == 0 and w == 0:
                    dve.wait_ge(cp_landed, 16 * (C + 1))
                dve.wait_ge(up_copied, 3 * (6 * C + i) + 3)
                if w == 1 and not (isinstance(C, int) and C == 0 and j == 0):
                    dve.wait_ge(hid_hi, T)
                k = 2 * (6 * C + i)
                nc.vector.tensor_scalar(cv[w][:, :], up[w][:, 2:HALF + 2], cp[:, i, 2:3], cp[:, i, 3:4],
                                        ALU.mult, ALU.add).then_inc(tap_done, 1)
                for tap in (1, 0):
                    dve.wait_ge(tap_done, k + 2 - tap)
                    nc.vector.scalar_tensor_tensor(cv[w][:, :], up[w][:, tap:HALF + tap], cp[:, i, tap:tap + 1],
                                                   cv[w][:, :], ALU.mult, ALU.add) \
                        .then_inc(tap_done if tap else conv_done[w], 1)

            def product(C, j):
                T = CJ * C + j
                dve.wait_ge(silu_done, T + 1)
                dve.wait_ge(conv_done[1], T + 1)
                nc.vector.tensor_tensor(cv[1][:, :], cv[0][:, :], cv[1][:, :], ALU.mult).then_inc(prod_done, 1)

            def lows(C, j):
                dve.wait_ge(hid_hi, CJ * C + j + 1)
                nc.vector.tensor_tensor(hid[j].lo[:, :], cv[1][:, :], hid[j].hi[:, :].bitcast(F32),
                                        ALU.subtract).then_inc(hid_lo, 1)

            def add(C, u):
                t, e = u // 2, u % 2
                dve.wait_ge(dn_done, UNITS * C + u + 1)
                part = y[:, t, e * 512:(e + 1) * 512]
                nc.vector.tensor_tensor(part, dn_ps[u % 4][:, :], part, ALU.add).then_inc(y_added, 1)

            def body(c, C, half):
                for j in range(CJ):
                    for w in range(2):
                        convolve(C, j, w)
                    product(C, j)
                    if j == 0 and not isinstance(c, int):
                        dve.wait_ge(y_landed, 16 * (half + 1))
                        for u in range(UNITS):
                            add(C - 1, u)
                    lows(C, j)

            def norm(half, t):
                n = TH * half + t + 1
                dve.wait_ge(square_done, n)
                nc.vector.tensor_scalar(stat[:, t, 1:2], stat[:, t, 0:1], 1.0 / D, EPS,
                                        ALU.mult, ALU.add).then_inc(mean_done, 1)
                dve.wait_ge(root_done, n)
                nc.vector.reciprocal(stat[:, t, 3:4], stat[:, t, 2:3]).then_inc(rstd_done, 1)
                dve.wait_ge(rstd_done, n)
                nc.vector.scalar_tensor_tensor(y[:, t, :], y[:, t, :], stat[:, t, 3:4], gf_row[:, :],
                                               ALU.mult, ALU.mult).then_inc(y_normed, 1)

            def tail(half):
                C = NC * (half + 1) - 1
                for t in range(TH):
                    add(C, 2 * t)
                    add(C, 2 * t + 1)
                    if t:
                        norm(half, t - 1)
                norm(half, TH - 1)

            nc.vector.memset(stat[:, :, :], 0.0).then_inc(y_added, 4)
            dve.wait_ge(gf_landed, 16)
            chunks(dve, body, tail)

        @block.tensor
        def _(pe):
            def up_tile(C, i):
                j, w = divmod(i, 2)
                pos = POS["gv"[w] + str(j)]
                U = 6 * C + i
                pe.wait_ge(split_lo, NP * C + pos + 1)
                first = isinstance(C, int) and C == 0 and i == 0
                for b in range(3):
                    if not first:
                        pe.wait_ge(up_copied, 3 * U + b - 2)
                    for k in range(KT):
                        for n, (u, v) in enumerate(PASSES):
                            mm = nc.tensor.matmul(up_ps[b][:, 0:UB], up_w[i % 3].part(u)[:, k * P:(k + 1) * P],
                                                  xn.part(v)[:, k, b * UB:(b + 1) * UB],
                                                  start=k == 0 and n == 0, stop=k == KT - 1 and n == 2)
                    mm.then_inc(up_done, 1)

            def down(C):
                pe.wait_ge(hid_lo, CJ * C + CJ)
                pe.wait_ge(split_lo, NP * C + 7)
                for u in range(UNITS):
                    t, e = divmod(u, 2)
                    pe.wait_ge(y_added, 4 + UNITS * C + u - 3)
                    for j in range(CJ):
                        for n, (a, b) in enumerate(PASSES):
                            mm = nc.tensor.matmul(dn_ps[u % 4][:, :], hid[j].part(a)[:, t * P:(t + 1) * P],
                                                  down_w[j].part(b)[:, e * 512:(e + 1) * 512],
                                                  start=j == 0 and n == 0, stop=j == CJ - 1 and n == 2)
                    mm.then_inc(dn_done, 1)

            def body(c, C, half):
                if isinstance(c, int):
                    pe.wait_ge(xn_landed, 32 * (half + 1))
                for i in range(2 * CJ):
                    up_tile(C, i)
                    if i == 1 and not isinstance(c, int):
                        down(C - 1)

            chunks(pe, body, lambda half: down(NC * (half + 1) - 1))


def host(inputs):
    import numpy as np

    a = {k: np.asarray(v) for k, v in inputs.items()}
    w_in, o_f, o_p = a["w_in"][0], 3 * AW, 3 * AW + HEADS

    def tiled(w):
        return w.reshape(-1, P, w.shape[1]).transpose(1, 0, 2)

    q, k, v = (tiled(w_in[:, i * AW:(i + 1) * AW]) for i in range(3))
    u = tiled(w_in[:, o_p:])
    chans = [np.concatenate([q[:, :, h * HD:(h + 1) * HD], k[:, :, h * HD:(h + 1) * HD]], axis=2)
             for h in range(HEADS)]
    chans += [u[:, :, g * P:(g + 1) * P] for g in range(GROUPS)]
    chans = [c.reshape(P, KT * P) for c in chans]
    w_up, w_down = a["w_up"][0], a["w_down"][0].reshape(FT, P, D)
    gate, value = (w_up[:, i * FF:(i + 1) * FF].reshape(KT, P, FT, P).transpose(2, 1, 0, 3).reshape(FT, P, D)
                   for i in range(2))
    order = [(gate, 0), (value, 0), (gate, 1), (value, 1), (w_down, 0), (w_down, 1), (w_down, 2),
             (gate, 2), (value, 2)]
    w_mlp = np.stack([np.stack([w[3 * c + j] for w, j in order]) for c in range(FT // 3)])
    taps = np.concatenate([a["conv_w"][0], a["conv_b"]], axis=0).reshape(4, 2, FT // 3, 3, P)
    conv = taps.transpose(2, 4, 3, 1, 0).reshape(FT // 3, P, 24)
    return {
        "x": a["x"][0], "meta": a["meta_tokens"],
        "g1": np.broadcast_to(a["norm1_g"][0], (P, D)),
        "w_item": np.stack([np.concatenate(chans[2 * i:2 * i + 2], axis=1) for i in range(6)]),
        "w_v": np.stack([v[:, :, h * AW // 2:(h + 1) * AW // 2].reshape(P, -1) for h in range(2)]),
        "w_f": tiled(w_in[:, o_f:o_f + P]).reshape(P, KT * P),
        "b_f": a["b_f"][0][:, None],
        "g2": np.broadcast_to(a["norm2_g"][0], (P, D)),
        "w_out": a["w_out"][0].reshape(KT, P, D),
        "w_pool": a["w_pool"][0].transpose(1, 0, 2).reshape(P, GROUPS * P),
        "p_scale": a["pool_scale"][0].reshape(GROUPS, P).T,
        "w_mlp": w_mlp, "conv": conv,
        "gf": np.broadcast_to(a["normf_g"], (P, D)),
    }


SCRATCH = {
    "z_hi": (HEADS + GROUPS, P, L), "z_lo": (HEADS + GROUPS, P, L),
    "v_aug": (HEADS, TILES + 1, P, VA), "g_rows": (2, HEADS, L), "c_rows": (P, P),
    "a_rows": (HEADS, HD + 1, L), "d_rows": (GROUPS, P, L),
    "inv_rows": (HEADS, L),
    "p_hi": (GROUPS, P, L), "p_lo": (GROUPS, P, L),
    "h2": (L, D), "n_hi": (P, KT, L), "n_lo": (P, KT, L),
}


def encoder_block(nc, i, o):
    t = {k: nc.dram_tensor(k, shape, F32).ap() for k, shape in SCRATCH.items()}
    in_projection(nc, i["x"], i["meta"], i["g1"], i["w_item"], i["w_v"], i["w_f"], i["b_f"],
                  t["z_hi"], t["z_lo"], t["v_aug"], t["g_rows"])
    attention(nc, t["z_hi"], t["z_lo"], t["v_aug"], t["g_rows"], t["c_rows"], t["a_rows"], t["d_rows"])
    out_projection(nc, i["x"], i["meta"], i["g2"], i["w_out"], i["w_pool"], i["p_scale"],
                   t["a_rows"], t["d_rows"], t["inv_rows"], t["p_hi"], t["p_lo"], t["h2"], t["n_hi"], t["n_lo"])
    mlp(nc, t["n_hi"], t["n_lo"], t["h2"], i["w_mlp"], i["conv"], i["gf"], o)


def kernel(**inputs):
    import numpy as np
    import concourse.bacc as bacc
    from concourse.bass_utils import run_bass_kernel_spmd

    nc = bacc.Bacc("TRN2", target_bir_lowering=False, num_devices=1)
    arrays = {k: np.ascontiguousarray(v) for k, v in host(inputs).items()}
    ins = {k: nc.dram_tensor("in_" + k, v.shape, F32, kind="ExternalInput").ap() for k, v in arrays.items()}
    out = nc.dram_tensor("out", (SEQ, D), F32, kind="ExternalOutput").ap()
    encoder_block(nc, ins, out)
    r = run_bass_kernel_spmd(nc, [{"in_" + k: v for k, v in arrays.items()}], core_ids=[0])
    return r.results[0]["out"].reshape(1, SEQ, D)
```

```python
from contextlib import ExitStack

import concourse.bass as bass
from concourse import mybir

ALU = mybir.AluOpType
ACT = mybir.ActivationFunctionType
AX_X = mybir.AxisListType.X
F32 = mybir.dt.float32
F32R = mybir.dt.float32r
BF16 = mybir.dt.bfloat16

P = 128
D = 1024
KT = D // P
SEQ = 2048
META = 16
L = META + SEQ
TILES = SEQ // P
HEADS = 8
HD = 64
AW = HEADS * HD
GROUPS = 4
WINDOWS = (2, 4, 8, 16)
FF = 2688
FT = FF // P
EPS = 1e-6
NEG = -1e30
BLK = 416
BLKS = [(b * BLK, min(BLK, L - b * BLK)) for b in range(-(-L // BLK))]
NB = len(BLKS)
VA = 2 * HD
PASSES = (("hi", "hi"), ("hi", "lo"), ("lo", "hi"))


def frames(t):
    if isinstance(t, int) and t == 0:
        return 0, META
    return (t - 1) * P + META, P


def cols(t):
    f0, n = frames(t)
    return bass.ds(f0, n)


def row(ap, i):
    return ap[bass.ds(i, 1), :, :].rearrange("o p c -> (o p) c")


class Pair:

    def __init__(self, hi, lo):
        self.hi, self.lo = hi, lo

    def part(self, name):
        return self.hi if name == "hi" else self.lo


def tools(nc, ctx, tag):
    def sb(name, shape, dt=F32):
        return ctx.enter_context(nc.sbuf_tensor(f"{tag}_{name}", shape, dt))

    def ps(name, shape, dt=F32):
        return ctx.enter_context(nc.psum_tensor(f"{tag}_{name}", shape, dt))

    def sem(name):
        return ctx.enter_context(nc.semaphore(f"{tag}_{name}"))

    def pair(name, shape):
        return Pair(sb(name + "_hi", shape, F32R), sb(name + "_lo", shape, F32R))

    return sb, ps, sem, pair


def in_projection(nc, x, meta, g1, w_item, w_v, w_f, b_f, z_hi, z_lo, v_aug, g_rows):
    ITEMS = 2 + 6
    VH = AW // 2
    with ExitStack() as ctx:
        sb, ps, sem, pair = tools(nc, ctx, "in")
        ident = sb("ident", [P, P])
        x_both = sb("x_both", [P, L])
        x_in = [x_both[:, s * D:(s + 1) * D] for s in range(2)]
        xs_g = sb("xs_g", [P, L])
        g_row = xs_g[:, D:2 * D]
        xT = pair("xT", [P, KT, L])
        w_raw = sb("w_raw", [P, 2048])
        w = [pair(f"w{s}", [P, 2048]) for s in range(2)]
        wf_raw = w_raw[:, 0:KT * P]
        stage = [sb(f"stage{s}", [P, L]) for s in range(2)]
        xs = [xs_g[:, 0:D], stage[0][:, D:2 * D]]
        bf_col = sb("bf_col", [HEADS, 1])
        stat = sb("stat", [P, 2, 4])

        turn = ps("turn", [P, 2, 512])
        acc = [ps(f"acc{b}", [P, 512]) for b in range(NB)]
        junk = sb("junk", [P, D], BF16)

        ident_ready = sem("ident_ready")
        x_landed = [sem(f"x_landed{s}") for s in range(2)]
        g_landed = sem("g_landed")
        bf_landed = sem("bf_landed")
        square_done = sem("square_done")
        mean_done = sem("mean_done")
        root_done = sem("root_done")
        rstd_done = sem("rstd_done")
        xs_done = sem("xs_done")
        turn_done = sem("turn_done")
        xhi_done = sem("xhi_done")
        xlo_done = sem("xlo_done")
        w_landed = sem("w_landed")
        whi_done = sem("whi_done")
        wlo_done = sem("wlo_done")
        v_done = sem("v_done")
        vhi_done = sem("vhi_done")
        vlo_done = sem("vlo_done")
        v_stored = [sem(f"v_stored{s}") for s in range(2)]
        f_done = sem("f_done")
        f_chain = sem("f_chain")
        f_act = sem("f_act")
        f_ready = sem("f_ready")
        f_stored = sem("f_stored")
        z_done = sem("z_done")
        zhi_done = sem("zhi_done")
        zlo_done = sem("zlo_done")
        z_stored = [sem(f"z_stored{b}") for b in range(NB)]
        block = ctx.enter_context(nc.Block())

        def v_stage(t):
            return stage[t % 2][:, 0:4 * VA].rearrange("p (h c) -> p h c", c=VA)

        @block.sync
        def _(sp):
            def load_x(t, slot, peeled):
                if not peeled:
                    sp.wait_ge(xs_done, t - 1)
                src = meta if isinstance(t, int) and t == 0 else x[bass.ds((t - 1) * P, P), :]
                sp.dma_start(x_in[slot][0:src.shape[0], :], src).then_inc(x_landed[slot], 16)

            load_x(0, 0, True)
            sp.dma_start(w_raw[:, :], w_v[0, :, :]).then_inc(w_landed, 16)
            sp.dma_start(g_row[:, :], g1).then_inc(g_landed, 16)
            load_x(1, 1, True)
            load_x(2, 0, False)
            sp.dma_start(bf_col[:, :], b_f).then_inc(bf_landed, 16)
            sp.wait_ge(wlo_done, 1)
            sp.wait_ge(whi_done, 1)
            sp.dma_start(w_raw[:, 0:KT * P], w_f).then_inc(w_landed, 16)

            def store_v(t, slot, half, n):
                _, rows = frames(t)
                sp.wait_ge(vhi_done, n + 1)
                sp.wait_ge(vlo_done, n + 1)
                dst = v_aug[4 * half:4 * half + 4, bass.ds(t, 1), 0:rows, :].rearrange("h o p c -> (o p) h c")
                sp.dma_start(dst, v_stage(slot)[0:rows, :, :]).then_inc(v_stored[slot], 16)

            load_x(3, 1, False)
            for t in range(2):
                load_x(t + 4, t, False)
                store_v(t, t, 0, t)
            sp.wait_ge(wlo_done, 2)
            sp.wait_ge(whi_done, 2)
            sp.dma_start(w_raw[:, :], w_v[1, :, :]).then_inc(w_landed, 16)
            with sp.Fori(1, TILES // 2 - 2) as i:
                for s in range(2):
                    load_x(2 * i + 4 + s, s, False)
                    store_v(2 * i + s, s, 0, 2 * i + s)
            load_x(TILES, 0, False)
            for t in range(TILES - 4, TILES + 1):
                store_v(t, t % 2, 0, t)
            sp.wait_ge(wlo_done, 3)
            sp.wait_ge(whi_done, 3)
            sp.dma_start(w_raw[:, :], w_item[0, :, :]).then_inc(w_landed, 16)
            def second(t):
                store_v(t, (t + 1) % 2, 1, TILES + 1 + t)

            for t in range(9):
                second(t)
                if t == 7:
                    sp.wait_ge(f_ready, 1)
                    sp.dma_start(g_rows[0, :, :], xs_g[0:HEADS, :]).then_inc(f_stored, 16)
            sp.wait_ge(f_ready, 2)
            sp.dma_start(g_rows[1, :, :], x_both[0:HEADS, :]).then_inc(f_stored, 16)
            with sp.Fori(4, TILES // 2) as i:
                for s in range(2):
                    store_v(2 * i + 1 + s, s, 1, 2 * i + 2 + s + TILES)

            def store_z(ct, b):
                c0, n = BLKS[b]
                sp.wait_ge(zlo_done, NB * ct + b + 1)
                for part, dst in ((0, z_hi), (1, z_lo)):
                    sp.dma_start(row(dst, ct)[:, c0:c0 + n],
                                 stage[part][:, c0:c0 + n]).then_inc(z_stored[b], 16)

            def pair_stores(k, more):
                for half in range(2):
                    for b in range(NB):
                        store_z(2 * k + half, b)
                    if half == 0 and more:
                        sp.wait_ge(wlo_done, k + 5)
                        sp.wait_ge(whi_done, k + 5)
                        sp.dma_start(w_raw[:, :], row(w_item, k + 2)).then_inc(w_landed, 16)

            sp.wait_ge(wlo_done, 4)
            sp.wait_ge(whi_done, 4)
            sp.dma_start(w_raw[:, :], w_item[1, :, :]).then_inc(w_landed, 16)
            with sp.Fori(0, 4) as k:
                pair_stores(k, True)
            for k in (4, 5):
                pair_stores(k, False)
            sp.wait_ge(f_stored, 32)
            for s in range(2):
                sp.wait_ge(v_stored[s], 16 * (TILES + 1))
            for b in range(NB):
                sp.wait_ge(z_stored[b], 2 * 16 * 12)

        @block.gpsimd
        def _(pool):
            nc.gpsimd.memset(ident[:, :], 0.0).then_inc(ident_ready, 1)
            pool.wait_ge(ident_ready, 1)
            nc.gpsimd.affine_select(out=ident[:, :], in_=ident[:, :], compare_op=ALU.not_equal, fill=1.0,
                                    base=0, pattern=[[-1, P]], channel_multiplier=1).then_inc(ident_ready, 1)

            def split_lo(item, slot, n):
                pool.wait_ge(whi_done, item + 1)
                nc.gpsimd.tensor_tensor(w[slot].lo[:, 0:n], w_raw[:, 0:n], w[slot].hi[:, 0:n].bitcast(F32),
                                        ALU.subtract).then_inc(wlo_done, 1)

            split_lo(0, 0, 2048)
            split_lo(1, 1, KT * P)
            split_lo(2, 0, 2048)
            split_lo(3, 1, 2048)
            split_lo(4, 0, 2048)
            with pool.Fori(0, 2) as i:
                for s in range(2):
                    split_lo(2 * i + 5 + s, (1 + s) % 2, 2048)

        def split_hi(act, item, slot, n):
            act.wait_ge(w_landed, 16 * (item + 1))
            if not isinstance(item, int) or item > 4:
                act.wait_ge(z_done, 2 * NB * (item - 4))
            elif item in (2, 4):
                act.wait_ge(v_done, (TILES + 1) * (item // 2))
            elif item == 3:
                act.wait_ge(f_done, NB)
            nc.scalar.activation(w[slot].hi[:, 0:n], w_raw[:, 0:n], ACT.Copy).then_inc(whi_done, 1)

        @block.scalar
        def _(act):
            def squares(t, slot):
                _, n = frames(t)
                act.wait_ge(x_landed[slot], 8 * t + (16 - 8 * slot))
                nc.scalar.activation(junk[0:n, :], x_in[slot][0:n, :], ACT.Square,
                                     accum_out=stat[0:n, slot, 0:1]).then_inc(square_done, 1)
                act.wait_ge(mean_done, t + 1)
                nc.scalar.activation(stat[0:n, slot, 2:3], stat[0:n, slot, 1:2], ACT.Sqrt).then_inc(root_done, 1)

            def turned(t):
                _, n = frames(t)
                for h in range(2):
                    act.wait_ge(turn_done, 2 * t + h + 1)
                    nc.scalar.activation(xT.hi[:, 4 * h:4 * h + 4, cols(t)],
                                         turn[:, h, :].rearrange("p (k c) -> p k c", k=4)[:, :, 0:n],
                                         ACT.Copy).then_inc(xhi_done, 1)

            def v_hi(t, slot, n, peeled):
                _, rows = frames(t)
                act.wait_ge(v_done, n + 1)
                if not peeled:
                    act.wait_ge(v_stored[slot], 8 * n - 8 * slot)
                nc.scalar.activation(v_stage(slot)[0:rows, :, 0:HD].bitcast(F32R),
                                     acc[slot][0:rows, 0:VH].rearrange("p (h c) -> p h c", c=HD),
                                     ACT.Copy).then_inc(vhi_done, 1)

            split_hi(act, 0, 0, 2048)
            squares(0, 0)
            for t in range(5):
                squares(t + 1, (t + 1) % 2)
                turned(t)
                if t == 1:
                    split_hi(act, 1, 1, KT * P)
                if t >= 2:
                    v_hi(t - 2, t % 2, t - 2, t < 4)
            with act.Fori(0, TILES // 2 - 3) as i:
                for s in range(2):
                    t = 2 * i + 5 + s
                    squares(t + 1, s)
                    turned(t)
                    v_hi(t - 2, (1 + s) % 2, t - 2, False)
            squares(TILES, 0)
            for t in (TILES - 1, TILES):
                turned(t)
                v_hi(t - 2, t % 2, t - 2, False)
            for t in (TILES - 1, TILES):
                v_hi(t, t % 2, t, False)
            split_hi(act, 2, 0, 2048)

            y, e = x_both[0:HEADS, :], xs_g[0:HEADS, :]
            act.wait_ge(bf_landed, 16)
            act.wait_ge(turn_done, 2 * (TILES + 1))
            for b, (c0, n) in enumerate(BLKS):
                act.wait_ge(f_done, b + 1)
                nc.scalar.activation(y[:, c0:c0 + n], acc[b][0:HEADS, 0:n], ACT.Identity,
                                     bias=bf_col[:, 0:1]).then_inc(f_act, 1)
            def v_second(t, slot, n):
                v_hi(t, slot, n, False)

            for n, (out, src, function, scale, bias) in enumerate((
                    (e, y, ACT.Abs, 1.0, 0.0), (e, e, ACT.Exp, -1.0, 0.0), (e, e, ACT.Ln, 1.0, 1.0))):
                act.wait_ge(f_act, NB + n)
                nc.scalar.activation(out, src, function, scale=scale, bias=bias).then_inc(f_act, 1)
                v_second(n, (n + 1) % 2, TILES + 1 + n)
            split_hi(act, 3, 1, 2048)
            for t in (3, 4):
                v_second(t, (t + 1) % 2, TILES + 1 + t)
            with act.Fori(2, TILES // 2) as i:
                for s in range(2):
                    v_second(2 * i + 1 + s, s, 2 * i + 2 + s + TILES)

            def z_hi_block(ct, b, peeled):
                c0, n = BLKS[b]
                act.wait_ge(z_done, NB * ct + b + 1)
                if peeled:
                    if b == 0:
                        for s in range(2):
                            act.wait_ge(v_stored[s], 16 * (TILES + 1))
                else:
                    act.wait_ge(z_stored[b], 32 * ct)
                nc.scalar.activation(stage[0][:, c0:c0 + n].bitcast(F32R), acc[b][:, 0:n],
                                     ACT.Copy).then_inc(zhi_done, 1)

            def pair_hi(k, slot, first, more):
                for half in range(2):
                    for b in range(NB):
                        z_hi_block(2 * k + half, b, first and half == 0)
                    if half == 0 and more:
                        split_hi(act, k + 4, slot, 2048)

            pair_hi(0, 0, True, True)
            with act.Fori(0, 2) as i:
                for s in range(2):
                    pair_hi(2 * i + 1 + s, (1 + s) % 2, False, True)
            pair_hi(5, 1, False, False)

        @block.vector
        def _(dve):
            def means(t, slot):
                _, n = frames(t)
                dve.wait_ge(square_done, t + 1)
                nc.vector.tensor_scalar(stat[0:n, slot, 1:2], stat[0:n, slot, 0:1], 1.0 / D, EPS,
                                        ALU.mult, ALU.add).then_inc(mean_done, 1)
                dve.wait_ge(root_done, t + 1)
                nc.vector.reciprocal(stat[0:n, slot, 3:4], stat[0:n, slot, 2:3]).then_inc(rstd_done, 1)
                dve.wait_ge(rstd_done, t + 1)
                if isinstance(t, int) and t == 0:
                    dve.wait_ge(g_landed, 16)
                else:
                    if not (isinstance(t, int) and t == 1):
                        dve.wait_ge(turn_done, 2 * t - 2)
                nc.vector.scalar_tensor_tensor(xs[slot][0:n, :], x_in[slot][0:n, :], stat[0:n, slot, 3:4],
                                               g_row[0:n, :], ALU.mult, ALU.mult).then_inc(xs_done, 1)

            def lows(t):
                _, n = frames(t)
                for h in range(2):
                    dve.wait_ge(xhi_done, 2 * t + h + 1)
                    part = (slice(None), slice(4 * h, 4 * h + 4), cols(t))
                    nc.vector.tensor_tensor(xT.lo[part], turn[:, h, :].rearrange("p (k c) -> p k c", k=4)[:, :, 0:n],
                                            xT.hi[part].bitcast(F32), ALU.subtract).then_inc(xlo_done, 1)

            def v_lo(t, slot, n):
                _, rows = frames(t)
                dve.wait_ge(vhi_done, n + 1)
                st = v_stage(slot)
                nc.vector.tensor_tensor(st[0:rows, :, HD:VA].bitcast(F32R),
                                        acc[slot][0:rows, 0:VH].rearrange("p (h c) -> p h c", c=HD),
                                        st[0:rows, :, 0:HD], ALU.subtract).then_inc(vlo_done, 1)

            means(0, 0)
            for t in (0, 1, 2):
                means(t + 1, (t + 1) % 2)
                lows(t)
            v_lo(0, 0, 0)
            with dve.Fori(0, TILES // 2 - 2) as i:
                for s in range(2):
                    t = 2 * i + 3 + s
                    means(t + 1, s)
                    lows(t)
                    v_lo(t - 2, (1 + s) % 2, t - 2)
            means(TILES, 0)
            for t in (TILES - 1, TILES):
                lows(t)
                v_lo(t - 2, t % 2, t - 2)
            for t in (TILES - 1, TILES):
                v_lo(t, t % 2, t)

            y, e = x_both[0:HEADS, :], xs_g[0:HEADS, :]
            def v_second(t):
                v_lo(t, (t + 1) % 2, TILES + 1 + t)

            for t in range(3):
                v_second(t)
            dve.wait_ge(f_act, NB + 3)
            nc.vector.tensor_scalar(y, y, 0.0, None, ALU.min).then_inc(f_chain, 1)
            v_second(3)
            dve.wait_ge(f_chain, 1)
            nc.vector.tensor_tensor(e, e, y, ALU.subtract).then_inc(f_chain, 1)
            v_second(4)
            dve.wait_ge(f_chain, 2)
            nc.vector.tensor_tensor_scan(y, e, e, 0.0, ALU.add, ALU.max).then_inc(f_chain, 1)
            v_second(5)
            dve.wait_ge(f_chain, 3)
            nc.vector.tensor_scalar(y, y, float(HD) ** 0.5, None, ALU.mult).then_inc(f_chain, 1)
            v_second(6)
            dve.wait_ge(f_chain, 4)
            nc.vector.tensor_copy(e.bitcast(F32R), y).then_inc(f_ready, 1)
            v_second(7)
            dve.wait_ge(f_ready, 1)
            nc.vector.tensor_tensor(y.bitcast(F32R), y, e, ALU.subtract).then_inc(f_ready, 1)
            v_second(8)
            with dve.Fori(4, TILES // 2) as i:
                for s in range(2):
                    v_lo(2 * i + 1 + s, s, 2 * i + 2 + s + TILES)

            with dve.Fori(0, 12) as ct:
                for b, (c0, n) in enumerate(BLKS):
                    dve.wait_ge(zhi_done, NB * ct + b + 1)
                    nc.vector.tensor_tensor(stage[1][:, c0:c0 + n].bitcast(F32R), acc[b][:, 0:n],
                                            stage[0][:, c0:c0 + n], ALU.subtract).then_inc(zlo_done, 1)

        @block.tensor
        def _(pe):
            def turns(t):
                _, n = frames(t)
                pe.wait_ge(xs_done, t + 1)
                for h in range(2):
                    if not (isinstance(t, int) and t == 0):
                        pe.wait_ge(xlo_done, 2 * t + h - 1)
                    for k in range(4):
                        mm = nc.tensor.transpose(turn[:, h, k * P:k * P + n],
                                                 xs[t % 2][0:n, (4 * h + k) * P:(4 * h + k + 1) * P],
                                                 ident[0:n, 0:n])
                    mm.then_inc(turn_done, 1)

            def v_tile(t, slot, wslot, n, peeled):
                f0 = frames(t)[0]
                if not peeled:
                    pe.wait_ge(vlo_done, n - 1)
                for j, (a, b) in enumerate(PASSES):
                    for k in range(KT):
                        mm = nc.tensor.matmul(acc[slot][:, 0:VH], xT.part(a)[:, k, f0:f0 + P],
                                              w[wslot].part(b)[:, k * VH:(k + 1) * VH],
                                              start=(j == 0 and k == 0), stop=(j == 2 and k == KT - 1))
                mm.then_inc(v_done, 1)

            pe.wait_ge(ident_ready, 2)
            turns(0)
            turns(1)
            for t in range(2, TILES + 2):
                if t <= TILES:
                    turns(t)
                if t == 2:
                    pe.wait_ge(wlo_done, 1)
                pe.wait_ge(xlo_done, 2 * t)
                if t == 2:
                    v_tile(0, 0, 0, 0, True)
                v_tile(t - 1, (t - 1) % 2, 0, t - 1, t == 2)

            def channel_tile(wslot, offset, done, free):
                for b, (c0, n) in enumerate(BLKS):
                    free(b)
                    for k in range(KT):
                        for j, (a, c) in enumerate(PASSES):
                            mm = nc.tensor.matmul(acc[b][:, 0:n],
                                                  w[wslot].part(a)[:, offset + k * P:offset + (k + 1) * P],
                                                  xT.part(c)[:, k, c0:c0 + n],
                                                  start=(k == 0 and j == 0), stop=(k == KT - 1 and j == 2))
                    mm.then_inc(done, 1)

            pe.wait_ge(wlo_done, 2)

            def f_free(b):
                if b < 2:
                    pe.wait_ge(vlo_done, TILES + 1)
            channel_tile(1, 0, f_done, f_free)
            pe.wait_ge(f_act, NB)
            pe.wait_ge(wlo_done, 3)
            for t in range(TILES + 1):
                n = TILES + 1 + t
                v_tile(t, n % 2, 0, n, t < 2)

            def z_free(ct, peeled):
                def free(b):
                    if not peeled:
                        pe.wait_ge(zlo_done, NB * (ct - 1) + b + 1)
                    elif b < 2:
                        pe.wait_ge(vlo_done, 2 * (TILES + 1))
                return free

            def pair_mm(k, slot, peeled):
                pe.wait_ge(wlo_done, k + 4)
                for half in range(2):
                    channel_tile(slot, half * D, z_done, z_free(2 * k + half, peeled and half == 0))

            pair_mm(0, 1, True)
            with pe.Fori(0, 2) as i:
                for s in range(2):
                    pair_mm(2 * i + 1 + s, s, False)
            pair_mm(5, 0, False)


AB = 3
A_BLOCKS = [(b, min(b + AB, TILES + 1)) for b in range(0, TILES + 1, AB)]
A_STEPS = [(j, kt) for j, (_, last) in enumerate(A_BLOCKS) for kt in range(last)]
A_ENDS = [max(s for s, (b, _) in enumerate(A_STEPS) if b == j) for j in range(len(A_BLOCKS))]
M_CHUNKS = [(i, 0 if c == 0 else META + (4 * c - 1) * P, META + P * min(i, 4 * c + 3), c, c == i // 4)
            for i in range(TILES + 1) for c in range(i // 4 + 1)]
MC = 5
M_FIRST = 1
LAG = 5
LO_LAG = 2
EXPS, SPLITS = 5, 7
AUG = HD + 4


def attention(nc, z_hi, z_lo, v_aug, g_rows, c_rows, a_out, d_out):
    NS, NM = len(A_STEPS), len(M_CHUNKS)
    with ExitStack() as ctx:
        sb, ps, sem, pair = tools(nc, ctx, "at")
        K1 = [sb(f"K1{s}", [P, L], F32R) for s in range(2)]
        Q1 = [sb(f"Q1{s}", [P, L], F32R) for s in range(2)]
        K2 = [sb(f"K2{s}", [AUG, L], F32R) for s in range(2)]
        Q2 = [sb(f"Q2{s}", [AUG, L], F32R) for s in range(2)]
        KM, QM = sb("KM", [AUG, L], F32R), sb("QM", [AUG, L], F32R)
        V = [sb(f"V{s}", [P, TILES + 1, 2, P], F32R) for s in range(2)]
        ident = sb("ident", [P, P])
        mask = sb("mask", [P, P])
        ident_r = sb("ident_r", [P, P], F32R)
        mask_r = sb("mask_r", [P, P], F32R)
        prob = [sb(f"prob{s}", [P, AB * P]) for s in range(EXPS)]
        prob_r = [pair(f"prob_r{s}", [P, AB * P]) for s in range(SPLITS)]
        peak = sb("peak", [P, TILES + 1, MC])
        top = sb("top", [P, TILES + 1])
        shift = sb("shift", [P, 2, P // 2])
        shift_T = sb("shift_T", [P, P])
        o_sb = [sb(f"o_sb{j}", [HD + 1, AB * P]) for j in range(len(A_BLOCKS))]
        PAD = 16
        U = sb("U", [P, PAD + L])
        W = [sb(f"W{s}", [P, PAD + L]) for s in range(2)]

        score = [ps(f"score{s}", [P, 512]) for s in range(3)]
        mlog = [ps(f"mlog{s}", [P, 512]) for s in range(2)]
        o_ps = [ps(f"o_ps{s}", [P, 512]) for s in range(2)]
        turn = ps("turn", [P, 512])

        consts = sem("consts")
        consts_r = sem("consts_r")
        cleared = sem("cleared")
        max_rows_set, rows_set = sem("max_rows_set"), sem("rows_set")
        max_landed = sem("max_landed")
        rest_landed = [sem(f"rest_landed{s}") for s in range(2)]
        mlog_done = sem("mlog_done")
        peak_done = sem("peak_done")
        top_done = sem("top_done")
        shift_done = sem("shift_done")
        turn_done = sem("turn_done")
        shift_T_done = sem("shift_T_done")
        c_stored = sem("c_stored")
        c_landed = [sem(f"c_landed{s}") for s in range(2)]
        score_done = sem("score_done")
        exp_done = sem("exp_done")
        phi_done = sem("phi_done")
        plo_done = sem("plo_done")
        pv_done = sem("pv_done")
        o_copied = sem("o_copied")
        o_stored = [sem(f"o_stored{j}") for j in range(len(A_BLOCKS))]
        pool_step = sem("pool_step")
        u_landed = sem("u_landed")
        d_stored = sem("d_stored")
        block = ctx.enter_context(nc.Block())
        NJ = len(A_BLOCKS)

        def before(h, s, ring, total):
            if s >= ring:
                return total * h + s - ring + 1
            last = max(x for x in range(total) if x % ring == s % ring)
            return total * (h - 1) + last + 1

        def heads(eng, body):
            body(0, 0, True, False)
            with eng.Fori(0, HEADS // 2 - 1) as i:
                for s in range(2):
                    body(2 * i + 1 + s, (1 + s) % 2, False, False)
            body(HEADS - 1, (HEADS - 1) % 2, False, True)

        def used_rows(kt):
            return META if kt == 0 else P

        def step_shape(s):
            j, kt = A_STEPS[s]
            a, b = A_BLOCKS[j]
            q0 = frames(max(a, kt))[0]
            q1 = sum(frames(b - 1))
            return q0, q1 - q0, kt >= a

        def block_frames(j):
            a, b = A_BLOCKS[j]
            q0 = frames(a)[0]
            return q0, sum(frames(b - 1)) - q0

        def load_on(eng, dst, src, done):
            eng.dma_start(dst.bitcast(F32), src).then_inc(done, 16)

        @block.sync
        def _(sp):
            def load(dst, src, done):
                load_on(sp, dst, src, done)

            def load_maxima(h, fresh):
                if not fresh:
                    sp.wait_ge(mlog_done, NM * h)
                load(KM[0:HD, :], row(z_hi, h)[HD:P, :], max_landed)
                load(QM[0:HD, :], row(z_hi, h)[0:HD, :], max_landed)
                for i in range(2):
                    load(KM[HD + 2 + i:HD + 3 + i, :], g_rows[i, bass.ds(h, 1), :], max_landed)

            def load_head(h, s, fresh):
                if not fresh:
                    sp.wait_ge(score_done, NS * (h - 1))
                qh, kh, ql, kl = (row(z, h)[r:r + HD, :] for z in (z_hi, z_lo) for r in (0, HD))
                load(K2[s][0:HD, :], kh, rest_landed[s])
                for i in range(2):
                    load(K2[s][HD + 2 + i:HD + 3 + i, :], g_rows[i, bass.ds(h, 1), :], rest_landed[s])
                load(K1[s][0:HD, :], kh, rest_landed[s])
                load(K1[s][HD:P, :], kl, rest_landed[s])
                for i in range(2):
                    load(Q1[s][i * HD:(i + 1) * HD, :], qh, rest_landed[s])
                load(Q2[s][0:HD, :], ql, rest_landed[s])
                if not fresh:
                    sp.wait_ge(pv_done, NS * (h - 1))
                v = v_aug[bass.ds(h, 1), :, :, :].rearrange("o t p (k c) -> p (o t) k c", k=2)
                for k in range(2):
                    load(V[s][0:META, 0, k, 0:HD], v[0:META, 0, k, :], rest_landed[s])
                    load(V[s][:, 1:, k, 0:HD], v[:, 1:, k, :], rest_landed[s])

            def head(h, s, first, last):
                if not last:
                    load_maxima(h + 1, False)
                    if first:
                        sp.wait_ge(c_landed[0], 64)
                        sp.wait_ge(rows_set, 8)
                    load_head(h + 1, 1 - s, first)

            sp.wait_ge(max_rows_set, 3)
            load_maxima(0, True)
            sp.wait_ge(rows_set, 4)
            load_head(0, 0, True)
            heads(sp, head)
            for j in range(NJ):
                sp.wait_ge(o_stored[j], 16 * HEADS)

        @block.gpsimd
        def _(pool):
            for n, (t, value) in enumerate(((ident, 0.0), (mask, 0.0))):
                nc.gpsimd.memset(t[:, :], value).then_inc(consts, 1)
            pool.wait_ge(consts, 2)
            nc.gpsimd.affine_select(out=ident[:, :], in_=ident[:, :], compare_op=ALU.not_equal, fill=1.0,
                                    base=0, pattern=[[-1, P]], channel_multiplier=1).then_inc(consts, 1)
            nc.gpsimd.affine_select(out=mask[:, :], in_=mask[:, :], compare_op=ALU.is_ge, fill=NEG,
                                    base=0, pattern=[[-1, P]], channel_multiplier=1).then_inc(consts, 1)
            pool.wait_ge(consts, 4)
            fills = [fill for s in range(2) for fill in
                     ((K2[s][HD:AUG, :], 1.0), (Q2[s][HD:AUG, :], 1.0),
                      (V[s][:, :, 0, HD:P], 1.0), (V[s][:, :, 1, HD:P], 0.0))]
            for n, (part, value) in enumerate(fills):
                nc.gpsimd.memset(part.bitcast(F32), value).then_inc(rows_set, 1)
                pool.wait_ge(rows_set, n + 1)
            done = 0

            def then(instruction):
                nonlocal done
                done += 1
                instruction.then_inc(pool_step, 1)
                pool.wait_ge(pool_step, done)

            for t in (U, W[0], W[1]):
                then(nc.gpsimd.memset(t[:, 0:PAD], 0.0))
            for g, window in enumerate(WINDOWS):
                if g:
                    pool.wait_ge(d_stored, 16 * g)
                pool.dma_start(U[:, PAD:], z_hi[HEADS + g, :, :]).then_inc(u_landed, 16)
                pool.dma_start(W[0][:, PAD:], z_lo[HEADS + g, :, :]).then_inc(u_landed, 16)
                pool.wait_ge(u_landed, 32 * (g + 1))
                then(nc.gpsimd.tensor_tensor(U[:, PAD:], U[:, PAD:], W[0][:, PAD:], ALU.add))
                cur, width, k = U, 1, 0
                while width < window:
                    nxt = W[k % 2]
                    then(nc.gpsimd.tensor_tensor(nxt[:, PAD:], cur[:, PAD:], cur[:, PAD - width:PAD - width + L],
                                                 ALU.add))
                    cur, width, k = nxt, 2 * width, k + 1
                out = W[k % 2]
                then(nc.gpsimd.tensor_scalar(out[:, PAD:], cur[:, PAD:], 1.0 / window, None, ALU.mult))
                for t in range(window - 1):
                    then(nc.gpsimd.tensor_scalar(out[:, PAD + t:PAD + t + 1], cur[:, PAD + t:PAD + t + 1],
                                                 1.0 / (t + 1), None, ALU.mult))
                then(nc.gpsimd.tensor_tensor(out[:, PAD:], out[:, PAD:], U[:, PAD:], ALU.subtract))
                pool.dma_start(d_out[g, :, :], out[:, PAD:]).then_inc(d_stored, 16)
            pool.wait_ge(d_stored, 16 * GROUPS)

        @block.tensor
        def _(pe):
            def maxima(h, s, m):
                i, k0, k1, _, diagonal = M_CHUNKS[m]
                q0, n = frames(i)[0], k1 - k0
                if m == 0:
                    pe.wait_ge(max_landed, 64 * (h + 1))
                if not (isinstance(h, int) and h == 0 and m < 2):
                    pe.wait_ge(peak_done, before(h, m, 2, NM))
                mm = nc.tensor.matmul(mlog[m % 2][:, 0:n], QM[:, q0:q0 + P], KM[:, k0:k1],
                                      start=True, stop=True)
                if diagonal:
                    d = frames(i)[1]
                    mm = nc.tensor.matmul(mlog[m % 2][:, n - d:n], ident_r[:, :], mask_r[:, 0:d],
                                          start=False, stop=True, skip_group_check=True)
                mm.then_inc(mlog_done, 1)

            def turn_shift(h):
                pe.wait_ge(shift_done, 2 * (h + 1))
                nc.tensor.transpose(turn[:, 0:P], shift[:, :, :].rearrange("p a t -> p (a t)"),
                                    ident[:, :]).then_inc(turn_done, 1)

            def scores(h, s, n):
                j, kt = A_STEPS[n]
                q0, nq, diagonal = step_shape(n)
                k0 = frames(kt)[0]
                bank = score[n % 3]
                if not (isinstance(h, int) and h == 0 and n < 3):
                    pe.wait_ge(exp_done, before(h, n, 3, NS))
                nc.tensor.matmul(bank[:, 0:nq], K1[s][:, k0:k0 + P], Q1[s][:, q0:q0 + nq], start=True, stop=False)
                mm = nc.tensor.matmul(bank[:, 0:nq], K2[s][:, k0:k0 + P], Q2[s][:, q0:q0 + nq],
                                      start=False, stop=True)
                if diagonal:
                    d = frames(kt)[1]
                    mm = nc.tensor.matmul(bank[:, 0:d], mask_r[:, :], ident_r[:, 0:d], start=False, stop=True,
                                          skip_group_check=True)
                mm.then_inc(score_done, 1)

            def values(h, s, n):
                j, kt = A_STEPS[n]
                q0, nq, _ = step_shape(n)
                off, r = q0 - block_frames(j)[0], used_rows(kt)
                if kt == 0 and not (isinstance(h, int) and h == 0 and j < 2):
                    pe.wait_ge(o_copied, NJ * h + j - 1)
                pe.wait_ge(plo_done, NS * h + n + 1)
                p = prob_r[n % SPLITS]
                for i, (v, part) in enumerate(((0, p.hi), (0, p.lo), (1, p.hi))):
                    mm = nc.tensor.matmul(o_ps[j % 2][:, off:off + nq], V[s][0:r, kt, v, :], part[0:r, 0:nq],
                                          start=kt == 0 and i == 0, stop=True, skip_group_check=True)
                mm.then_inc(pv_done, 1)

            def head(h, s, first, last):
                half = (h - s) // 2 if isinstance(h, int) else None
                pe.wait_ge(rest_landed[s], 192 * (half + 1) if half is not None else 96 * (h - s) + 192)
                pe.wait_ge(c_landed[s], 64 * (half + 1) if half is not None else 32 * (h - s) + 64)
                for n in range(NS + LAG if last else NS):
                    if not last and 0 <= n - M_FIRST < NM:
                        maxima(h + 1, 1 - s, n - M_FIRST)
                    if not last and n == M_FIRST + NM + 1:
                        turn_shift(h + 1)
                    if n < NS:
                        scores(h, s, n)
                    if n >= LAG:
                        values(h, s, n - LAG)
                    elif not first:
                        values(h - 1, 1 - s, NS + n - LAG)

            pe.wait_ge(consts_r, 2)
            for m in range(NM):
                maxima(0, 0, m)
            turn_shift(0)
            heads(pe, head)

        @block.scalar
        def _(act):
            def turned(h):
                act.wait_ge(turn_done, h + 1)
                if not (isinstance(h, int) and h == 0):
                    act.wait_ge(c_stored, 16 * h)
                nc.scalar.activation(shift_T[:, :], turn[:, 0:P], ACT.Copy).then_inc(shift_T_done, 1)

            def store_shift(h):
                act.wait_ge(shift_T_done, h + 1)
                act.dma_start(c_rows, shift_T[:, :]).then_inc(c_stored, 16)

            def load_shift(h, s):
                act.wait_ge(c_stored, 16 * (h + 1))
                if isinstance(h, int) and h < 2:
                    act.wait_ge(rows_set, 4 * (h + 1))
                else:
                    act.wait_ge(score_done, NS * (h - 1))
                for i in range(2):
                    t0 = i * P // 2
                    load_on(act, Q2[s][HD + i:HD + i + 1, 0:META], c_rows[t0:t0 + 1, 0:META], c_landed[s])
                    load_on(act, Q2[s][HD + i:HD + i + 1, META:], c_rows[t0 + 1:t0 + TILES + 1, :]
                            .rearrange("(o t) c -> o (t c)", o=1), c_landed[s])

            def exps(h, n):
                _, kt = A_STEPS[n]
                _, nq, _ = step_shape(n)
                r = used_rows(kt)
                act.wait_ge(score_done, NS * h + n + 1)
                if not (isinstance(h, int) and h == 0 and n < EXPS):
                    act.wait_ge(plo_done, before(h, n, EXPS, NS))
                nc.scalar.activation(prob[n % EXPS][0:r, 0:nq], score[n % 3][0:r, 0:nq], ACT.Exp,
                                     scale=float(HD) ** -0.5).then_inc(exp_done, 1)

            def highs(h, n):
                _, kt = A_STEPS[n]
                _, nq, _ = step_shape(n)
                r = used_rows(kt)
                act.wait_ge(exp_done, NS * h + n + 1)
                if not (isinstance(h, int) and h == 0 and n < SPLITS):
                    act.wait_ge(pv_done, before(h, n, SPLITS, NS))
                nc.scalar.activation(prob_r[n % SPLITS].hi[0:r, 0:nq], prob[n % EXPS][0:r, 0:nq], ACT.Copy) \
                    .then_inc(phi_done, 1)

            def copy_o(h, j):
                n = block_frames(j)[1]
                act.wait_ge(pv_done, NS * h + A_ENDS[j] + 1)
                if not (isinstance(h, int) and h == 0):
                    act.wait_ge(o_stored[j], 16 * h)
                nc.scalar.activation(o_sb[j][:, 0:n], o_ps[j % 2][0:HD + 1, 0:n], ACT.Copy).then_inc(o_copied, 1)

            def store_o(h, j):
                q0, n = block_frames(j)
                act.wait_ge(o_copied, NJ * h + j + 1)
                act.dma_start(row(a_out, h)[:, q0:q0 + n], o_sb[j][:, 0:n]).then_inc(o_stored[j], 16)

            def head(h, s, first, last):
                for n in range(NS + 1 if last else NS):
                    if n < NS:
                        exps(h, n)
                    if n:
                        highs(h, n - 1)
                    elif not first:
                        highs(h - 1, NS - 1)
                    for j in range(NJ - 1):
                        if n == A_ENDS[j] + LAG + 1:
                            copy_o(h, j)
                        if n == A_ENDS[j] + LAG + 2:
                            store_o(h, j)
                    if not first and n == LAG:
                        copy_o(h - 1, NJ - 1)
                    if not first and n == LAG + 1:
                        store_o(h - 1, NJ - 1)
                    if not last and n == M_FIRST + NM + 3:
                        turned(h + 1)
                    if not last and n == M_FIRST + NM + 4:
                        store_shift(h + 1)
                    if not last and n == M_FIRST + NM + 8:
                        load_shift(h + 1, 1 - s)
                if last:
                    copy_o(h, NJ - 1)
                    store_o(h, NJ - 1)

            act.wait_ge(consts, 4)
            for src, dst in ((ident, ident_r), (mask, mask_r)):
                nc.scalar.activation(dst[:, :], src[:, :], ACT.Copy).then_inc(consts_r, 1)
            turned(0)
            store_shift(0)
            load_shift(0, 0)
            heads(act, head)

        @block.vector
        def _(dve):
            def peaks(h, m):
                i, k0, k1, c, _ = M_CHUNKS[m]
                r = frames(i)[1]
                dve.wait_ge(mlog_done, NM * h + m + 1)
                if m == 0 and not (isinstance(h, int) and h == 0):
                    dve.wait_ge(top_done, h)
                nc.vector.tensor_reduce(peak[0:r, i, c:c + 1], mlog[m % 2][0:r, 0:k1 - k0], AX_X,
                                        ALU.max).then_inc(peak_done, 1)

            def shifts(h):
                dve.wait_ge(peak_done, NM * (h + 1))
                nc.vector.tensor_reduce(top[:, :], peak[:, :, :], AX_X, ALU.max).then_inc(top_done, 1)
                dve.wait_ge(top_done, h + 1)
                if not (isinstance(h, int) and h == 0):
                    dve.wait_ge(turn_done, h)
                nc.vector.tensor_scalar(shift[:, 0, 0:TILES + 1].bitcast(F32R), top[:, :], -1.0, None, ALU.mult) \
                    .then_inc(shift_done, 1)
                dve.wait_ge(shift_done, 2 * h + 1)
                nc.vector.scalar_tensor_tensor(shift[:, 1, 0:TILES + 1].bitcast(F32R), top[:, :], -1.0, shift[:, 0, 0:TILES + 1],
                                               ALU.mult, ALU.subtract).then_inc(shift_done, 1)

            def lows(h, n):
                _, kt = A_STEPS[n]
                _, nq, _ = step_shape(n)
                r = used_rows(kt)
                dve.wait_ge(phi_done, NS * h + n + 1)
                nc.vector.tensor_tensor(prob_r[n % SPLITS].lo[0:r, 0:nq], prob[n % EXPS][0:r, 0:nq],
                                        prob_r[n % SPLITS].hi[0:r, 0:nq].bitcast(F32), ALU.subtract) \
                    .then_inc(plo_done, 1)

            def head(h, s, first, last):
                for n in range(NS + LO_LAG if last else NS):
                    if not last and 0 <= n - M_FIRST < NM:
                        peaks(h + 1, n - M_FIRST)
                    if not last and n == M_FIRST + NM:
                        shifts(h + 1)
                    if n >= LO_LAG:
                        lows(h, n - LO_LAG)
                    elif not first:
                        lows(h - 1, NS + n - LO_LAG)

            for t in (KM, QM):
                nc.vector.memset(t[HD:AUG, :].bitcast(F32), 1.0).then_inc(max_rows_set, 1)
            dve.wait_ge(max_rows_set, 2)
            nc.vector.memset(QM[HD:HD + 2, :].bitcast(F32), 0.0).then_inc(max_rows_set, 1)
            nc.vector.memset(peak[:, :, :], NEG).then_inc(cleared, 1)
            nc.vector.memset(shift[:, :, :], 0.0).then_inc(cleared, 1)
            dve.wait_ge(cleared, 2)
            for m in range(NM):
                peaks(0, m)
            shifts(0)
            heads(dve, head)


def out_projection(nc, x, meta, g2, w_out, w_pool, p_scale, a_in, d_in, inv_rows, h2_out, n_out):
    with ExitStack() as ctx:
        sb, ps, sem, pair = tools(nc, ctx, "out")
        ident = sb("ident", [P, P])
        g_row = sb("g_row", [P, D])
        wp_raw = sb("wp_raw", [P, GROUPS * P])
        wp = pair("wp", [P, GROUPS * P])
        scale = sb("scale", [P, GROUPS])
        d_raw = [sb(f"d_raw{s}", [P, GROUPS, P]) for s in range(2)]
        dd = [pair(f"dd{s}", [P, GROUPS, P]) for s in range(2)]
        w_raw = sb("w_raw", [P, KT, D])
        w = pair("w", [P, KT, D])
        h_in = [sb(f"h_in{s}", [P, D]) for s in range(2)]
        KA = AW // P
        ap = [sb(f"ap{s}", [P, KT, P]) for s in range(2)]
        inv = [sb(f"inv{s}", [P, KA, P]) for s in range(2)]
        sums = sb("sums", [P, HEADS * L // P])
        cat = [pair(f"cat{s}", [P, KT, P]) for s in range(2)]
        h2 = [sb(f"h2{s}", [P, D]) for s in range(2)]
        xs = sb("xs", [P, D])
        junk = sb("junk", [P, D], BF16)
        nT = [sb(f"nT{s}", [P, KT, P]) for s in range(2)]
        stat = sb("stat", [P, 2, 4])

        acc = ps("acc", [P, 2, 2, 512])
        turn = ps("turn", [P, 2, 512])
        mapped = [ps(f"mapped{s}", [P, 512]) for s in range(2)]

        consts, cleared = sem("consts"), sem("cleared")
        sums_landed, inv_done, inv_stored = sem("sums_landed"), sem("inv_done"), sem("inv_stored")
        small_landed, wp_landed = sem("small_landed"), sem("wp_landed")
        wp_hi_done, wp_lo_done = sem("wp_hi_done"), sem("wp_lo_done")
        d_landed = [sem(f"d_landed{s}") for s in range(2)]
        d_hi_done, d_lo_done = sem("d_hi_done"), sem("d_lo_done")
        map_done, ap_done = sem("map_done"), sem("ap_done")
        w_landed = [sem(f"w_landed{j}") for j in range(KT // 2)]
        w_hi_done = sem("w_hi_done")
        w_lo_done = [sem(f"w_lo_done{s}") for s in range(2)]
        h_landed = [sem(f"h_landed{s}") for s in range(2)]
        a_landed = [sem(f"a_landed{s}") for s in range(2)]
        cat_hi_done, cat_lo_done = sem("cat_hi_done"), sem("cat_lo_done")
        out_done, h2_done = sem("out_done"), sem("h2_done")
        square_done, mean_done, root_done = sem("square_done"), sem("mean_done"), sem("root_done")
        rstd_done, xs_done = sem("rstd_done"), sem("xs_done")
        turn_done, n_copied = sem("turn_done"), sem("n_copied")
        h2_stored = [sem(f"h2_stored{s}") for s in range(2)]
        n_stored = [sem(f"n_stored{s}") for s in range(2)]
        block = ctx.enter_context(nc.Block())
        def early(t, n=2):
            return isinstance(t, int) and t < n

        @block.sync
        def _(sp):
            def load_d(t, s):
                f0, n = frames(t)
                if not early(t):
                    sp.wait_ge(d_hi_done, 1)
                    sp.wait_ge(d_lo_done, t - 1)
                sp.dma_start(d_raw[s][:, :, 0:n], d_in[:, :, bass.ds(f0, n)].rearrange("g p c -> p g c")) \
                    .then_inc(d_landed[s], 16)

            sp.dma_start(wp_raw[:, :], w_pool).then_inc(wp_landed, 16)
            load_d(0, 0)
            load_d(1, 1)
            rows = P // HEADS
            for h in range(HEADS):
                sp.dma_start(sums[h * rows:(h + 1) * rows, :],
                             a_in[h, HD:HD + 1, :].rearrange("o (r c) -> (o r) c", r=rows)).then_inc(sums_landed, 16)
            sp.dma_start(scale[:, :], p_scale).then_inc(small_landed, 16)
            sp.dma_start(g_row[:, :], g2).then_inc(small_landed, 16)

            for j in range(KT // 2):
                if j == KT // 4:
                    sp.wait_ge(inv_done, 1)
                    sp.dma_start(inv_rows.rearrange("h (r c) -> (h r) c", r=rows), sums[:, :]) \
                        .then_inc(inv_stored, 16)
                sp.dma_start(w_raw[:, 2 * j:2 * j + 2, :], w_out[2 * j:2 * j + 2, :, :].rearrange("k p d -> p k d")) \
                    .then_inc(w_landed[j], 16)
            sp.wait_ge(inv_stored, 16)

            def load(t, s):
                f0, n = frames(t)
                if not early(t):
                    sp.wait_ge(cat_hi_done, 1)
                    sp.wait_ge(h2_done, 2 * t - 2)
                src = meta if isinstance(t, int) and t == 0 else x[bass.ds((t - 1) * P, P), :]
                sp.dma_start(h_in[s][0:n, :], src).then_inc(h_landed[s], 16)
                for e in range(2):
                    part = slice(e * HD, (e + 1) * HD)
                    heads = a_in.rearrange("(k e) r c -> r e k c", e=2)
                    sp.dma_start(ap[s][part, 0:KA, 0:n], heads[0:HD, e, :, bass.ds(f0, n)]).then_inc(a_landed[s], 16)
                    scales = inv_rows.rearrange("(o k e) c -> o e k c", e=2, o=1)[:, e, :, bass.ds(f0, n)]
                    sp.dma_start(inv[s][part, :, 0:n], scales.to_broadcast([HD, KA, n])).then_inc(a_landed[s], 16)

            def store_h2(t, s):
                f0, n = frames(t)
                sp.wait_ge(out_done, 2)
                sp.wait_ge(h2_done, 2 * t + 2)
                sp.dma_start(h2_out[bass.ds(f0, n), :], h2[s][0:n, :]).then_inc(h2_stored[s], 16)

            def store_n(t, s):
                f0, n = frames(t)
                sp.wait_ge(n_copied, 2)
                sp.wait_ge(n_copied, 2 * t + 2)
                sp.dma_start(n_out[:, :, bass.ds(f0, n)], nT[s][:, :, 0:n]).then_inc(n_stored[s], 16)

            load(0, 0)
            load(1, 1)
            load_d(2, 0)
            load_d(3, 1)
            load(2, 0)
            store_h2(0, 0)

            def step(t, s):
                load_d(t + 3, 1 - s)
                load(t + 2, s)
                store_h2(t, s)
                store_n(t - 1, 1 - s)

            step(1, 1)
            step(2, 0)
            with sp.Fori(1, TILES // 2 - 2) as i:
                for s in range(2):
                    step(2 * i + 1 + s, (1 + s) % 2)
            step(TILES - 3, 1)
            load(TILES, 0)
            store_h2(TILES - 2, 0)
            store_n(TILES - 3, 1)
            for t in (TILES - 1, TILES):
                store_h2(t, t % 2)
            for t in range(TILES - 2, TILES + 1):
                store_n(t, t % 2)
            for s in range(2):
                sp.wait_ge(h2_stored[s], 16 * ((TILES + 2 - s) // 2))
                sp.wait_ge(n_stored[s], 16 * ((TILES + 2 - s) // 2))

        @block.gpsimd
        def _(pool):
            nc.gpsimd.memset(ident[:, :], 0.0).then_inc(consts, 1)
            pool.wait_ge(consts, 1)
            nc.gpsimd.affine_select(out=ident[:, :], in_=ident[:, :], compare_op=ALU.not_equal, fill=1.0,
                                    base=0, pattern=[[-1, P]], channel_multiplier=1).then_inc(consts, 1)
            pool.wait_ge(consts, 2)
            for k in range(0, KT, 2):
                pool.wait_ge(w_hi_done, k + 1)
                nc.gpsimd.tensor_tensor(w.lo[:, k, :], w_raw[:, k, :], w.hi[:, k, :].bitcast(F32),
                                        ALU.subtract).then_inc(w_lo_done[0], 1)

        @block.scalar
        def _(act):
            act.wait_ge(wp_landed, 16)
            nc.scalar.activation(wp.hi[:, :], wp_raw[:, :], ACT.Copy).then_inc(wp_hi_done, 1)

            def d_his(t, s):
                _, n = frames(t)
                act.wait_ge(d_landed[s], 8 * t + (16 - 8 * s))
                if not early(t):
                    act.wait_ge(map_done, t - 1)
                nc.scalar.activation(dd[s].hi[:, :, 0:n], d_raw[s][:, :, 0:n], ACT.Copy).then_inc(d_hi_done, 1)

            def cat_his(t, s):
                _, n = frames(t)
                act.wait_ge(ap_done, 2 * t + 2)
                if not early(t):
                    act.wait_ge(out_done, 2 * t - 2)
                nc.scalar.activation(cat[s].hi[:, :, 0:n], ap[s][:, :, 0:n], ACT.Copy).then_inc(cat_hi_done, 1)

            def norms(t, s, cat_ahead=True, d_ahead=True):
                _, n = frames(t)
                act.wait_ge(h2_done, 2 * t + 2)
                nc.scalar.activation(junk[0:n, :], h2[s][0:n, :], ACT.Square,
                                     accum_out=stat[0:n, s, 0:1]).then_inc(square_done, 1)
                act.wait_ge(mean_done, t + 1)
                nc.scalar.activation(stat[0:n, s, 2:3], stat[0:n, s, 1:2], ACT.Sqrt).then_inc(root_done, 1)
                if cat_ahead:
                    cat_his(t + 2, s)
                if d_ahead:
                    d_his(t + 3, 1 - s)
                for h in range(2):
                    act.wait_ge(turn_done, 2 * t + h + 1)
                    if not early(t) and h == 0:
                        act.wait_ge(n_stored[s], 8 * (t - s))
                    nc.scalar.activation(nT[s][:, 4 * h:4 * h + 4, 0:n],
                                         turn[:, h, :].rearrange("p (k c) -> p k c", k=4)[:, :, 0:n],
                                         ACT.Copy).then_inc(n_copied, 1)

            d_his(0, 0)
            d_his(1, 1)
            for k in range(KT):
                act.wait_ge(w_landed[k // 2], 16)
                nc.scalar.activation(w.hi[:, k, :], w_raw[:, k, :], ACT.Copy).then_inc(w_hi_done, 1)
            d_his(2, 0)
            cat_his(0, 0)
            cat_his(1, 1)
            for t in range(3):
                norms(t, t % 2)
            with act.Fori(1, TILES // 2 - 2) as i:
                for s in range(2):
                    norms(2 * i + 1 + s, (1 + s) % 2)
            norms(TILES - 3, 1)
            norms(TILES - 2, 0, True, False)
            norms(TILES - 1, 1, False, False)
            norms(TILES, 0, False, False)

        @block.vector
        def _(dve):
            dve.wait_ge(wp_hi_done, 1)
            nc.vector.tensor_tensor(wp.lo[:, :], wp_raw[:, :], wp.hi[:, :].bitcast(F32), ALU.subtract) \
                .then_inc(wp_lo_done, 1)

            def d_lows(t, s):
                _, n = frames(t)
                dve.wait_ge(d_hi_done, t + 1)
                nc.vector.tensor_tensor(dd[s].lo[:, :, 0:n], d_raw[s][:, :, 0:n], dd[s].hi[:, :, 0:n].bitcast(F32),
                                        ALU.subtract).then_inc(d_lo_done, 1)

            def cat_lows(t, s):
                _, n = frames(t)
                a, p = ap[s][:, 0:KA, 0:n], ap[s][:, KA:KT, 0:n]
                dve.wait_ge(a_landed[s], 32 * t + (64 - 32 * s))
                nc.vector.tensor_tensor(a, a, inv[s][:, :, 0:n], ALU.mult).then_inc(ap_done, 1)
                dve.wait_ge(map_done, t + 1)
                nc.vector.tensor_tensor(p, mapped[s][:, :].rearrange("p (g c) -> p g c", g=GROUPS)[:, :, 0:n],
                                        scale.rearrange("p (g c) -> p g c", c=1).to_broadcast([P, GROUPS, n]),
                                        ALU.mult).then_inc(ap_done, 1)
                dve.wait_ge(cat_hi_done, t + 1)
                nc.vector.tensor_tensor(cat[s].lo[:, :, 0:n], ap[s][:, :, 0:n], cat[s].hi[:, :, 0:n].bitcast(F32),
                                        ALU.subtract).then_inc(cat_lo_done, 1)

            def residual(t, s):
                _, n = frames(t)
                dve.wait_ge(h_landed[s], 8 * t + (16 - 8 * s))
                if not early(t):
                    dve.wait_ge(h2_stored[s], 8 * (t - s))
                for h in range(2):
                    dve.wait_ge(out_done, 2 * t + h + 1)
                    nc.vector.tensor_tensor(h2[s][0:n, h * 512:(h + 1) * 512], acc[0:n, s, h, :],
                                            h_in[s][0:n, h * 512:(h + 1) * 512], ALU.add).then_inc(h2_done, 1)

            def norms(t, s):
                _, n = frames(t)
                dve.wait_ge(square_done, t + 1)
                nc.vector.tensor_scalar(stat[0:n, s, 1:2], stat[0:n, s, 0:1], 1.0 / D, EPS,
                                        ALU.mult, ALU.add).then_inc(mean_done, 1)
                dve.wait_ge(root_done, t + 1)
                nc.vector.reciprocal(stat[0:n, s, 3:4], stat[0:n, s, 2:3]).then_inc(rstd_done, 1)
                dve.wait_ge(rstd_done, t + 1)
                if not early(t, 1):
                    dve.wait_ge(turn_done, 2 * t)
                nc.vector.scalar_tensor_tensor(xs[0:n, :], h2[s][0:n, :], stat[0:n, s, 3:4], g_row[0:n, :],
                                               ALU.mult, ALU.mult).then_inc(xs_done, 1)

            def rest(t, s, cat_ahead=True, d_ahead=True):
                residual(t, s)
                norms(t, s)
                if cat_ahead:
                    cat_lows(t + 2, s)
                if d_ahead:
                    d_lows(t + 3, 1 - s)

            for t in range(2):
                d_lows(t, t)
            dve.wait_ge(sums_landed, 16 * HEADS)
            nc.vector.reciprocal(sums[:, :], sums[:, :]).then_inc(inv_done, 1)
            nc.vector.memset(cat[0].hi[:, :, META:].bitcast(F32), 0.0).then_inc(cleared, 1)
            nc.vector.memset(cat[0].lo[:, :, META:].bitcast(F32), 0.0).then_inc(cleared, 1)
            dve.wait_ge(small_landed, 32)
            for k in range(1, KT, 2):
                dve.wait_ge(w_hi_done, k + 1)
                nc.vector.tensor_tensor(w.lo[:, k, :], w_raw[:, k, :], w.hi[:, k, :].bitcast(F32),
                                        ALU.subtract).then_inc(w_lo_done[1], 1)
            d_lows(2, 0)
            cat_lows(0, 0)
            cat_lows(1, 1)
            for t in range(3):
                rest(t, t % 2)
            with dve.Fori(1, TILES // 2 - 2) as i:
                for s in range(2):
                    rest(2 * i + 1 + s, (1 + s) % 2)
            rest(TILES - 3, 1)
            rest(TILES - 2, 0, True, False)
            rest(TILES - 1, 1, False, False)
            rest(TILES, 0, False, False)

        @block.tensor
        def _(pe):
            pe.wait_ge(wp_lo_done, 1)

            def map_pool(t, s):
                _, n = frames(t)
                pe.wait_ge(d_lo_done, t + 1)
                if not early(t):
                    pe.wait_ge(ap_done, 2 * t - 2)
                for g in range(GROUPS):
                    for j, (u, v) in enumerate(PASSES):
                        mm = nc.tensor.matmul(mapped[s][:, g * P:g * P + n], wp.part(u)[:, g * P:(g + 1) * P],
                                              dd[s].part(v)[:, g, 0:n], start=j == 0, stop=j == 2)
                mm.then_inc(map_done, 1)

            def products(t, s):
                pe.wait_ge(cat_lo_done, t + 1)
                if not early(t):
                    pe.wait_ge(h2_done, 2 * t - 2)
                for h in range(2):
                    for k in range(KT):
                        for j, (u, v) in enumerate(PASSES):
                            mm = nc.tensor.matmul(acc[:, s, h, :], cat[s].part(u)[:, k, :],
                                                  w.part(v)[:, k, h * 512:(h + 1) * 512],
                                                  start=k == 0 and j == 0, stop=k == KT - 1 and j == 2)
                    mm.then_inc(out_done, 1)

            def turns(t, s):
                _, n = frames(t)
                pe.wait_ge(xs_done, t + 1)
                for h in range(2):
                    if not early(t, 1):
                        pe.wait_ge(n_copied, 2 * t + h - 1)
                    for k in range(4):
                        mm = nc.tensor.transpose(turn[:, h, k * P:k * P + n],
                                                 xs[0:n, (4 * h + k) * P:(4 * h + k + 1) * P], ident[0:n, 0:n])
                    mm.then_inc(turn_done, 1)

            for t in range(2):
                map_pool(t, t)
            pe.wait_ge(consts, 2)
            for part in range(2):
                pe.wait_ge(w_lo_done[part], KT // 2)
            pe.wait_ge(cleared, 2)
            products(0, 0)
            map_pool(2, 0)

            def step(t, s, d_ahead=True):
                products(t + 1, 1 - s)
                turns(t, s)
                if d_ahead:
                    map_pool(t + 3, 1 - s)

            for t in range(3):
                step(t, t % 2)
            with pe.Fori(1, TILES // 2 - 2) as i:
                for s in range(2):
                    step(2 * i + 1 + s, (1 + s) % 2)
            step(TILES - 3, 1)
            step(TILES - 2, 0, False)
            step(TILES - 1, 1, False)
            turns(TILES, 0)


def mlp(nc, n_in, h2_in, w_mlp, conv, gf, out):
    CJ = 3
    NC = FT // CJ
    HALF = SEQ // 2
    UB = (HALF + 2) // 3
    TH = HALF // P
    XN_AT = (4, 6, 7)
    POS = {"g0": 0, "v0": 1, "g1": 2, "v1": 3, "d0": 4, "d1": 5, "d2": 6, "g2": 7, "v2": 8}
    NP = len(POS)
    with ExitStack() as ctx:
        sb, ps, sem, pair = tools(nc, ctx, "mlp")
        xn = pair("xn", [P, KT, HALF + 2])
        y = sb("y", [P, TH, D])
        raw = [sb(f"raw{s}", [P, D]) for s in range(3)]
        up_w = [pair(f"up_w{s}", [P, D]) for s in range(3)]
        down_w = [pair(f"down_w{j}", [P, D]) for j in range(CJ)]
        hid = [pair(f"hid{j}", [P, HALF]) for j in range(CJ)]
        up = [sb(f"up{w}", [P, HALF + 2]) for w in range(2)]
        cv = [sb(f"cv{w}", [P, HALF]) for w in range(2)]
        cp = sb("cp", [P, 2 * CJ, 4])
        gf_row = sb("gf_row", [P, D])
        junk = sb("junk", [P, D], BF16)
        stat = sb("stat", [P, TH, 4])

        up_ps = [ps(f"up_ps{b}", [P, 512]) for b in range(3)]
        dn_ps = [ps(f"dn_ps{b}", [P, 512]) for b in range(4)]

        xn_landed = [sem(f"xn_landed{b}") for b in range(3)]
        xn_hi, xn_lo = sem("xn_hi"), sem("xn_lo")
        y_landed = sem("y_landed")
        gf_landed, cp_landed = sem("gf_landed"), sem("cp_landed")
        raw_landed = [sem(f"raw_landed{s}") for s in range(3)]
        split_hi, split_lo = sem("split_hi"), sem("split_lo")
        up_done, up_copied = sem("up_done"), sem("up_copied")
        tap_done = sem("tap_done")
        conv_done = [sem(f"conv_done{w}") for w in range(2)]
        silu_done, prod_done = sem("silu_done"), sem("prod_done")
        hid_hi, hid_lo = sem("hid_hi"), sem("hid_lo")
        dn_done, y_added = sem("dn_done"), sem("y_added")
        square_done, mean_done, root_done = sem("square_done"), sem("mean_done"), sem("root_done")
        rstd_done, y_normed, y_stored = sem("rstd_done"), sem("y_normed"), sem("y_stored")
        block = ctx.enter_context(nc.Block())
        UNITS = 2 * TH

        def chunks(eng, body, tail):
            for half in range(2):
                body(0, NC * half, half)
                with eng.Fori(1, NC) as c:
                    body(c, c + NC * half, half)
                tail(half)

        def target(pos):
            if 4 <= pos <= 6:
                return down_w[pos - 4]
            u = pos if pos < 4 else pos - CJ
            return up_w[u % 3]

        @block.sync
        def _(sp):
            sp.dma_start(gf_row[:, :], gf).then_inc(gf_landed, 16)

            def body(c, C, half):
                for pos in range(NP):
                    if not (half == 0 and isinstance(c, int) and pos < 3):
                        sp.wait_ge(split_lo, NP * C + pos - 2)
                    src = w_mlp[bass.ds(c, 1), pos, :, :].rearrange("o p n -> (o p) n")
                    sp.dma_start(raw[pos % 3][:, :], src).then_inc(raw_landed[pos % 3], 16)
                    if pos == 2:
                        if not (half == 0 and isinstance(c, int)):
                            sp.wait_ge(conv_done[1], CJ * C)
                        sp.dma_start(cp[:, :, :], row(conv, c).rearrange("p (t k) -> p t k", k=4)) \
                            .then_inc(cp_landed, 16)

            chunks(sp, body, lambda half: None)

        @block.gpsimd
        def _(pool):
            def load_xn(half):
                f0 = META - 2 + HALF * half
                if half:
                    pool.wait_ge(up_done, 3 * 6 * NC)
                for b in range(3):
                    pool.dma_start(xn.lo[:, :, b * UB:(b + 1) * UB].bitcast(F32),
                                   n_in[:, :, f0 + b * UB:f0 + (b + 1) * UB]).then_inc(xn_landed[b], 16)

            def load_y(half):
                if half:
                    pool.wait_ge(y_stored, 16 * TH)
                f0 = META + HALF * half
                pool.dma_start(y[:, :, :], h2_in[f0:f0 + HALF, :].rearrange("(t p) d -> p t d", p=P)) \
                    .then_inc(y_landed, 16)

            def lo(C, pos, dst):
                pool.wait_ge(split_hi, NP * C + pos + 1)
                nc.gpsimd.tensor_tensor(dst.lo[:, :], raw[pos % 3][:, :], dst.hi[:, :].bitcast(F32),
                                        ALU.subtract).then_inc(split_lo, 1)

            def body(c, C, half):
                for pos in range(NP):
                    lo(C, pos, target(pos))
                if half and isinstance(c, int):
                    load_y(1)

            load_xn(0)
            load_y(0)
            chunks(pool, body, lambda half: load_xn(1) if half == 0 else None)

        @block.scalar
        def _(act):
            def hi(C, pos, k=0):
                act.wait_ge(raw_landed[pos % 3], 16 * (3 * (C + k) + pos // 3 + 1))
                if 4 <= pos <= 6:
                    if not (isinstance(C, int) and C == 0):
                        act.wait_ge(dn_done, UNITS * C)
                else:
                    u = (pos if pos < 4 else pos - CJ) + 6 * k
                    if not (isinstance(C, int) and C == 0 and u < 3):
                        act.wait_ge(up_done, 3 * (6 * C + u - 2))
                dst = target(pos)
                nc.scalar.activation(dst.hi[:, :], raw[pos % 3][:, :], ACT.Copy).then_inc(split_hi, 1)

            def copy_up(C, j, w):
                if not (isinstance(C, int) and C == 0 and j == 0):
                    act.wait_ge(conv_done[w], CJ * C + j)
                for b in range(3):
                    act.wait_ge(up_done, 3 * (6 * C + 2 * j + w) + b + 1)
                    nc.scalar.activation(up[w][:, b * UB:(b + 1) * UB], up_ps[b][:, 0:UB], ACT.Copy) \
                        .then_inc(up_copied, 1)

            def gate(C, j):
                act.wait_ge(conv_done[0], CJ * C + j + 1)
                nc.scalar.activation(cv[0][:, :], cv[0][:, :], ACT.Silu).then_inc(silu_done, 1)
                if j == 0 and not (isinstance(C, int) and C == 0):
                    act.wait_ge(dn_done, UNITS * C)
                act.wait_ge(prod_done, CJ * C + j + 1)
                nc.scalar.activation(hid[j].hi[:, :], cv[1][:, :], ACT.Copy).then_inc(hid_hi, 1)

            def body_with(last):
                def body(c, C, half):
                    ahead = ((2, 3), (7, 8), (0, 1))
                    for j in range(CJ):
                        for w in range(2):
                            if j < 2:
                                hi(C, ahead[j][w])
                            elif not (last and isinstance(C, int) and C == 2 * NC - 1):
                                hi(C, ahead[j][w], 1)
                            copy_up(C, j, w)
                        gate(C, j)
                        if j == 0:
                            for pos in (4, 5, 6):
                                hi(C, pos)
                return body

            def split_xn(half, b):
                act.wait_ge(xn_landed[b], 16 * (half + 1))
                part = (slice(None), slice(None), slice(b * UB, (b + 1) * UB))
                nc.scalar.activation(xn.hi[part], xn.lo[part].bitcast(F32), ACT.Copy).then_inc(xn_hi, 1)

            def tail(half):
                C = NC * (half + 1)
                for t in range(TH):
                    if half == 0 and t + 1 in XN_AT:
                        split_xn(1, XN_AT.index(t + 1))
                    act.wait_ge(y_added, 4 + UNITS * (C - 1) + 2 * t + 2)
                    nc.scalar.activation(junk[:, :], y[:, t, :], ACT.Square,
                                         accum_out=stat[:, t, 0:1]).then_inc(square_done, 1)
                    act.wait_ge(mean_done, TH * half + t + 1)
                    nc.scalar.activation(stat[:, t, 2:3], stat[:, t, 1:2], ACT.Sqrt).then_inc(root_done, 1)
                    if t:
                        store(half, t - 1)
                store(half, TH - 1)

            def store(half, t):
                act.wait_ge(y_normed, TH * half + t + 1)
                f0 = HALF * half + t * P
                act.dma_start(out[f0:f0 + P, :], y[:, t, :]).then_inc(y_stored, 16)

            hi(0, 0)
            split_xn(0, 0)
            hi(0, 1)
            split_xn(0, 1)
            split_xn(0, 2)
            body = body_with(True)
            body(0, 0, 0)
            with act.Fori(1, NC) as c:
                body(c, c, 0)
            tail(0)
            body(0, NC, 1)
            with act.Fori(1, NC - 1) as c:
                body(c, c + NC, 1)
            body(NC - 1, 2 * NC - 1, 1)
            tail(1)
            act.wait_ge(y_stored, 2 * 16 * TH)

        @block.vector
        def _(dve):
            def convolve(C, j, w):
                i, T = 2 * j + w, CJ * C + j
                if j == 0 and w == 0:
                    dve.wait_ge(cp_landed, 16 * (C + 1))
                dve.wait_ge(up_copied, 3 * (6 * C + i) + 3)
                if w == 1 and not (isinstance(C, int) and C == 0 and j == 0):
                    dve.wait_ge(hid_hi, T)
                k = 2 * (6 * C + i)
                nc.vector.tensor_scalar(cv[w][:, :], up[w][:, 2:HALF + 2], cp[:, i, 2:3], cp[:, i, 3:4],
                                        ALU.mult, ALU.add).then_inc(tap_done, 1)
                for tap in (1, 0):
                    dve.wait_ge(tap_done, k + 2 - tap)
                    nc.vector.scalar_tensor_tensor(cv[w][:, :], up[w][:, tap:HALF + tap], cp[:, i, tap:tap + 1],
                                                   cv[w][:, :], ALU.mult, ALU.add) \
                        .then_inc(tap_done if tap else conv_done[w], 1)

            def product(C, j):
                T = CJ * C + j
                dve.wait_ge(silu_done, T + 1)
                dve.wait_ge(conv_done[1], T + 1)
                nc.vector.tensor_tensor(cv[1][:, :], cv[0][:, :], cv[1][:, :], ALU.mult).then_inc(prod_done, 1)

            def lows(C, j):
                dve.wait_ge(hid_hi, CJ * C + j + 1)
                nc.vector.tensor_tensor(hid[j].lo[:, :], cv[1][:, :], hid[j].hi[:, :].bitcast(F32),
                                        ALU.subtract).then_inc(hid_lo, 1)

            def add(C, u):
                t, e = u // 2, u % 2
                dve.wait_ge(dn_done, UNITS * C + u + 1)
                part = y[:, t, e * 512:(e + 1) * 512]
                nc.vector.tensor_tensor(part, dn_ps[u % 4][:, :], part, ALU.add).then_inc(y_added, 1)

            def body(c, C, half):
                for j in range(CJ):
                    for w in range(2):
                        convolve(C, j, w)
                    product(C, j)
                    if j == 0 and not isinstance(c, int):
                        dve.wait_ge(y_landed, 16 * (half + 1))
                        for u in range(UNITS):
                            add(C - 1, u)
                    lows(C, j)

            def norm(half, t):
                n = TH * half + t + 1
                dve.wait_ge(square_done, n)
                nc.vector.tensor_scalar(stat[:, t, 1:2], stat[:, t, 0:1], 1.0 / D, EPS,
                                        ALU.mult, ALU.add).then_inc(mean_done, 1)
                dve.wait_ge(root_done, n)
                nc.vector.reciprocal(stat[:, t, 3:4], stat[:, t, 2:3]).then_inc(rstd_done, 1)
                dve.wait_ge(rstd_done, n)
                nc.vector.scalar_tensor_tensor(y[:, t, :], y[:, t, :], stat[:, t, 3:4], gf_row[:, :],
                                               ALU.mult, ALU.mult).then_inc(y_normed, 1)

            def split_xn(half, b):
                dve.wait_ge(xn_hi, 3 * half + b + 1)
                part = (slice(None), slice(None), slice(b * UB, (b + 1) * UB))
                nc.vector.tensor_tensor(xn.lo[part], xn.lo[part].bitcast(F32), xn.hi[part].bitcast(F32),
                                        ALU.subtract).then_inc(xn_lo, 1)

            def tail(half):
                C = NC * (half + 1) - 1
                for t in range(TH):
                    if half == 0 and t in XN_AT:
                        split_xn(1, XN_AT.index(t))
                    add(C, 2 * t)
                    add(C, 2 * t + 1)
                    if t:
                        norm(half, t - 1)
                norm(half, TH - 1)

            nc.vector.memset(stat[:, :, :], 0.0).then_inc(y_added, 4)
            for b in range(3):
                split_xn(0, b)
            dve.wait_ge(gf_landed, 16)
            chunks(dve, body, tail)

        @block.tensor
        def _(pe):
            def up_tile(C, i, half):
                j, w = divmod(i, 2)
                pos = POS["gv"[w] + str(j)]
                U = 6 * C + i
                pe.wait_ge(split_lo, NP * C + pos + 1)
                first = isinstance(C, int) and C == 0 and i == 0
                for b in range(3):
                    if half is not None:
                        pe.wait_ge(xn_lo, 3 * half + b + 1)
                    if not first:
                        pe.wait_ge(up_copied, 3 * U + b - 2)
                    for k in range(KT):
                        for n, (u, v) in enumerate(PASSES):
                            mm = nc.tensor.matmul(up_ps[b][:, 0:UB], up_w[i % 3].part(u)[:, k * P:(k + 1) * P],
                                                  xn.part(v)[:, k, b * UB:(b + 1) * UB],
                                                  start=k == 0 and n == 0, stop=k == KT - 1 and n == 2)
                    mm.then_inc(up_done, 1)

            def down_part(C, u, tiles):
                t, e = divmod(u, 2)
                for j in tiles:
                    for n, (a, b) in enumerate(PASSES):
                        mm = nc.tensor.matmul(dn_ps[u % 4][:, :], hid[j].part(a)[:, t * P:(t + 1) * P],
                                              down_w[j].part(b)[:, e * 512:(e + 1) * 512],
                                              start=j == 0 and n == 0, stop=j == CJ - 1 and n == 2)
                return mm

            def down(C, early=False):
                pe.wait_ge(split_lo, NP * C + 7)
                ahead = 4 if early else 0
                pe.wait_ge(hid_lo, CJ * C + (2 if early else CJ))
                for u in range(ahead):
                    pe.wait_ge(y_added, 4 + UNITS * C + u - 3)
                    down_part(C, u, range(2))
                if early:
                    pe.wait_ge(hid_lo, CJ * C + CJ)
                for u in range(UNITS):
                    if u >= ahead:
                        pe.wait_ge(y_added, 4 + UNITS * C + u - 3)
                    down_part(C, u, range(2 if u < ahead else 0, CJ)).then_inc(dn_done, 1)

            def body(c, C, half):
                for i in range(2 * CJ):
                    up_tile(C, i, half if isinstance(c, int) and i == 0 else None)
                    if i == 1 and not isinstance(c, int):
                        down(C - 1)

            chunks(pe, body, lambda half: down(NC * (half + 1) - 1, True))


def host(inputs):
    import numpy as np

    a = {k: np.asarray(v) for k, v in inputs.items()}
    w_in, o_f, o_p = a["w_in"][0], 3 * AW, 3 * AW + HEADS

    def tiled(w):
        return w.reshape(-1, P, w.shape[1]).transpose(1, 0, 2)

    q, k, v = (tiled(w_in[:, i * AW:(i + 1) * AW]) for i in range(3))
    u = tiled(w_in[:, o_p:])
    chans = [np.concatenate([q[:, :, h * HD:(h + 1) * HD], k[:, :, h * HD:(h + 1) * HD]], axis=2)
             for h in range(HEADS)]
    chans += [u[:, :, g * P:(g + 1) * P] for g in range(GROUPS)]
    chans = [c.reshape(P, KT * P) for c in chans]
    w_up, w_down = a["w_up"][0], a["w_down"][0].reshape(FT, P, D)
    gate, value = (w_up[:, i * FF:(i + 1) * FF].reshape(KT, P, FT, P).transpose(2, 1, 0, 3).reshape(FT, P, D)
                   for i in range(2))
    order = [(gate, 0), (value, 0), (gate, 1), (value, 1), (w_down, 0), (w_down, 1), (w_down, 2),
             (gate, 2), (value, 2)]
    w_mlp = np.stack([np.stack([w[3 * c + j] for w, j in order]) for c in range(FT // 3)])
    taps = np.concatenate([a["conv_w"][0], a["conv_b"]], axis=0).reshape(4, 2, FT // 3, 3, P)
    conv = taps.transpose(2, 4, 3, 1, 0).reshape(FT // 3, P, 24)
    return {
        "x": a["x"][0], "meta": a["meta_tokens"],
        "g1": np.broadcast_to(a["norm1_g"][0], (P, D)),
        "w_item": np.stack([np.concatenate(chans[2 * i:2 * i + 2], axis=1) for i in range(6)]),
        "w_v": np.stack([v[:, :, h * AW // 2:(h + 1) * AW // 2].reshape(P, -1) for h in range(2)]),
        "w_f": tiled(w_in[:, o_f:o_f + P]).reshape(P, KT * P),
        "b_f": a["b_f"][0][:, None],
        "g2": np.broadcast_to(a["norm2_g"][0], (P, D)),
        "w_out": a["w_out"][0].reshape(KT, P, D),
        "w_pool": a["w_pool"][0].transpose(1, 0, 2).reshape(P, GROUPS * P),
        "p_scale": a["pool_scale"][0].reshape(GROUPS, P).T,
        "w_mlp": w_mlp, "conv": conv,
        "gf": np.broadcast_to(a["normf_g"], (P, D)),
    }


SCRATCH = {
    "z_hi": (HEADS + GROUPS, P, L), "z_lo": (HEADS + GROUPS, P, L),
    "v_aug": (HEADS, TILES + 1, P, VA), "g_rows": (2, HEADS, L), "c_rows": (P, P),
    "a_rows": (HEADS, HD + 1, L), "d_rows": (GROUPS, P, L),
    "inv_rows": (HEADS, L),
    "h2": (L, D), "n": (P, KT, L),
}


def encoder_block(nc, i, o):
    t = {k: nc.dram_tensor(k, shape, F32).ap() for k, shape in SCRATCH.items()}
    in_projection(nc, i["x"], i["meta"], i["g1"], i["w_item"], i["w_v"], i["w_f"], i["b_f"],
                  t["z_hi"], t["z_lo"], t["v_aug"], t["g_rows"])
    attention(nc, t["z_hi"], t["z_lo"], t["v_aug"], t["g_rows"], t["c_rows"], t["a_rows"], t["d_rows"])
    out_projection(nc, i["x"], i["meta"], i["g2"], i["w_out"], i["w_pool"], i["p_scale"],
                   t["a_rows"], t["d_rows"], t["inv_rows"], t["h2"], t["n"])
    mlp(nc, t["n"], t["h2"], i["w_mlp"], i["conv"], i["gf"], o)


def kernel(**inputs):
    import numpy as np
    import concourse.bacc as bacc
    from concourse.bass_utils import run_bass_kernel_spmd

    nc = bacc.Bacc("TRN2", target_bir_lowering=False, num_devices=1)
    arrays = {k: np.ascontiguousarray(v) for k, v in host(inputs).items()}
    ins = {k: nc.dram_tensor("in_" + k, v.shape, F32, kind="ExternalInput").ap() for k, v in arrays.items()}
    out = nc.dram_tensor("out", (SEQ, D), F32, kind="ExternalOutput").ap()
    encoder_block(nc, ins, out)
    r = run_bass_kernel_spmd(nc, [{"in_" + k: v for k, v in arrays.items()}], core_ids=[0])
    return r.results[0]["out"].reshape(1, SEQ, D)
```
